# Optimizing a Trainium2 kernel written in Bass

```python
import math
import jax, jax.numpy as jnp
from jax import lax
import numpy as np

D_MODEL = 1024
BATCH = 1
SEQ = 512
DEPTH = 1

EPS = 1e-6
HY_WIDTH = 512
SHORT_CONV = 3
FILTER_BANDS = 16
FILTER_EMB = 1 + 2 * FILTER_BANDS
FILTER_HIDDEN = 64
FILTER_DECAY_TARGET = 1e-2
FAST_DECAY_PCT = 0.3
SLOW_DECAY_PCT = 1.5
FILTER_SHIFT = 0.05
MIN_DECAY = math.log(FILTER_DECAY_TARGET) / SLOW_DECAY_PCT
MAX_DECAY = math.log(FILTER_DECAY_TARGET) / FAST_DECAY_PCT
N_HEADS = 8
QK_NOPE = 64
QK_ROPE = 32
V_HEAD = 64
Q_LORA = 384
KV_LORA = 256
ROPE_THETA = 10000.0
Q_BLOCK = 128
MLA_WIDTH = N_HEADS * V_HEAD
N_BRANCH = 2
OFF_Q = 3 * HY_WIDTH
OFF_KV = OFF_Q + Q_LORA
OFF_KR = OFF_KV + KV_LORA
OFF_GATE = OFF_KR + QK_ROPE
IN_COLS = OFF_GATE + N_BRANCH * D_MODEL
N_GROUPS = 4
EXPERTS_PER_GROUP = 8
N_EXPERTS = N_GROUPS * EXPERTS_PER_GROUP
TOP_K = 2
D_EXPERT = 256

kernel_name = "hybrid_hyena_mla_hiermoe_adaln_block"

def _rmsnorm(x, g):
    xf = x.astype(jnp.float32)
    y = xf * lax.rsqrt(jnp.mean(xf * xf, axis=-1, keepdims=True) + EPS)
    return (y * g.astype(jnp.float32)).astype(x.dtype)

def _centred_short_conv(u, w, b):
    up = jnp.pad(u, ((0, 0), (1, 1), (0, 0)))
    return up[:, :-2] * w[0] + up[:, 1:-1] * w[1] + up[:, 2:] * w[2] + b

def _hyena_filter(L, w1, b1, f1, w2, b2, f2, w3):
    f32 = jnp.float32
    t = jnp.linspace(0.0, 1.0, L, dtype=f32)[:, None]
    t_r = jnp.arange(L, dtype=f32)[:, None]
    bands = jnp.linspace(1e-4, FILTER_BANDS - 1, FILTER_BANDS, dtype=f32)[None, :]
    ang = 2.0 * math.pi * bands * t_r / L
    z = jnp.concatenate([t, jnp.cos(ang), -jnp.sin(ang)], axis=-1)
    h = jnp.sin(f1.astype(f32) * (z @ w1.astype(f32) + b1.astype(f32)))
    h = jnp.sin(f2.astype(f32) * (h @ w2.astype(f32) + b2.astype(f32)))
    h = (h @ w3.astype(f32)).reshape(L, 2, HY_WIDTH)
    deltas = jnp.linspace(MIN_DECAY, MAX_DECAY, HY_WIDTH, dtype=f32)
    window = jnp.exp(-t * jnp.abs(deltas)[None, :]) + FILTER_SHIFT
    h = h * window[:, None, :]
    h_fwd, h_bwd = h[:, 0], h[:, 1]
    g = jnp.concatenate([h_fwd, jnp.zeros((1, HY_WIDTH), f32), h_bwd[:0:-1]], axis=0)
    return g / jnp.sum(jnp.abs(g), axis=0, keepdims=True)

def _bidir_long_conv(u, g, bias):
    L = u.shape[1]
    uf32 = u.astype(jnp.float32)
    uf = jnp.fft.rfft(uf32, n=2 * L, axis=1)
    gf = jnp.fft.rfft(g, axis=0)
    y = jnp.fft.irfft(uf * gf[None], n=2 * L, axis=1)[:, :L]
    return (y + bias.astype(jnp.float32) * uf32).astype(u.dtype)

def _rope_tables(L):
    pos = jnp.arange(L, dtype=jnp.float32)
    inv = ROPE_THETA ** (-jnp.arange(0, QK_ROPE, 2, dtype=jnp.float32) / QK_ROPE)
    ang = pos[:, None] * inv[None, :]
    return jnp.cos(ang), jnp.sin(ang)

def _rope(x, cos, sin):
    half = x.shape[-1] // 2
    x1 = x[..., :half].astype(jnp.float32)
    x2 = x[..., half:].astype(jnp.float32)
    return jnp.concatenate([x1 * cos - x2 * sin, x1 * sin + x2 * cos], axis=-1).astype(x.dtype)

def _mla(cq_raw, ckv_raw, kr_raw, g_q, g_kv, w_uq, w_uk, w_uv, cos, sin):
    B, L, _ = cq_raw.shape
    q = (_rmsnorm(cq_raw, g_q) @ w_uq).reshape(B, L, N_HEADS, QK_NOPE + QK_ROPE)
    q_nope = q[..., :QK_NOPE]
    q_rope = _rope(q[..., QK_NOPE:], cos[:, None, :], sin[:, None, :])
    c_kv = _rmsnorm(ckv_raw, g_kv)
    k_nope = jnp.einsum('blc,chd->blhd', c_kv, w_uk)
    v = jnp.einsum('blc,chd->blhd', c_kv, w_uv)
    k_rope = _rope(kr_raw, cos, sin)
    nb = L // Q_BLOCK
    qn = q_nope.reshape(B, nb, Q_BLOCK, N_HEADS, QK_NOPE).swapaxes(0, 1)
    qr = q_rope.reshape(B, nb, Q_BLOCK, N_HEADS, QK_ROPE).swapaxes(0, 1)
    scale = (QK_NOPE + QK_ROPE) ** -0.5

    def block(args):
        qn_b, qr_b = args
        s = (jnp.einsum('bqhd,bkhd->bhqk', qn_b, k_nope)
             + jnp.einsum('bqhr,bkr->bhqk', qr_b, k_rope))
        p = jax.nn.softmax(s.astype(jnp.float32) * scale, axis=-1).astype(v.dtype)
        return jnp.einsum('bhqk,bkhd->bqhd', p, v)

    o = lax.map(block, (qn, qr))
    return o.swapaxes(0, 1).reshape(B, L, MLA_WIDTH)

def _token_mixer(h, w_in, hy_conv_w, hy_conv_b, filt_w1, filt_b1, filt_freq1, filt_w2,
                 filt_b2, filt_freq2, filt_w3, hy_bias, q_norm_g, kv_norm_g, w_uq, w_uk,
                 w_uv, w_hy_out, w_mla_out, w_mix_out, cos, sin):
    B, L, _ = h.shape
    proj = h @ w_in
    hy = _centred_short_conv(proj[..., :OFF_Q], hy_conv_w, hy_conv_b)
    x0, x1, v = hy[..., :HY_WIDTH], hy[..., HY_WIDTH:2 * HY_WIDTH], hy[..., 2 * HY_WIDTH:]
    g = _hyena_filter(L, filt_w1, filt_b1, filt_freq1, filt_w2, filt_b2, filt_freq2, filt_w3)
    y_hy = x0 * _bidir_long_conv(v * x1, g, hy_bias)
    y_mla = _mla(proj[..., OFF_Q:OFF_KV], proj[..., OFF_KV:OFF_KR], proj[..., OFF_KR:OFF_GATE],
                 q_norm_g, kv_norm_g, w_uq, w_uk, w_uv, cos, sin)
    gates = jax.nn.sigmoid(proj[..., OFF_GATE:].reshape(B, L, N_BRANCH, D_MODEL))
    mix = gates[..., 0, :] * (y_hy @ w_hy_out) + gates[..., 1, :] * (y_mla @ w_mla_out)
    return mix @ w_mix_out

def _hier_moe(h, w_group, b_group, w_router, b_router, w_gate, w_up, w_down):
    B, L, D = h.shape
    t = h.reshape(B * L, D)
    n = t.shape[0]
    g_logits = (t @ w_group + b_group).astype(jnp.float32)
    p_group = jax.nn.softmax(g_logits, axis=-1)
    g_idx = jnp.argmax(g_logits, axis=-1)
    p_sel = jnp.max(p_group, axis=-1)
    e_logits = (t @ w_router + b_router).astype(jnp.float32).reshape(n, N_GROUPS, EXPERTS_PER_GROUP)
    e_in_group = e_logits[jnp.arange(n), g_idx]
    top_v, top_i = lax.top_k(e_in_group, TOP_K)
    w = jax.nn.softmax(top_v, axis=-1) * p_sel[:, None]
    e_idx = g_idx[:, None] * EXPERTS_PER_GROUP + top_i
    combine = jnp.einsum('nk,nke->ne', w, jax.nn.one_hot(e_idx, N_EXPERTS, dtype=jnp.float32))
    out = jnp.zeros((n, D), jnp.float32)
    for e in range(N_EXPERTS):
        a = jax.nn.silu(t @ w_gate[e]) * (t @ w_up[e])
        out = out + combine[:, e:e + 1] * (a @ w_down[e])
    return out.astype(h.dtype).reshape(B, L, D)

def setup_inputs(seed: int = 0) -> dict:
    key = jax.random.key(seed)
    keys = jax.random.split(key, 40)
    ctr = [0]

    def nk():
        k = keys[ctr[0]]
        ctr[0] += 1
        return k

    def nrm(shape, fan_in, s=1.0):
        return s * jax.random.normal(nk(), shape, jnp.float32) * fan_in ** -0.5

    def gain(shape):
        return 1.0 + 0.05 * jax.random.normal(nk(), shape, jnp.float32)

    def small(shape, s=0.02):
        return s * jax.random.normal(nk(), shape, jnp.float32)

    Dp, D = DEPTH, D_MODEL
    return {
        "x": jax.random.normal(nk(), (BATCH, SEQ, D), jnp.float32),
        "c": jax.random.normal(nk(), (BATCH, D), jnp.float32),
        "ada_w": nrm((Dp, D, 6 * D), D, 0.5),
        "ada_b": small((Dp, 6 * D)),
        "norm_mix_g": gain((Dp, D)),
        "w_in": nrm((Dp, D, IN_COLS), D),
        "hy_conv_w": nrm((Dp, SHORT_CONV, 3 * HY_WIDTH), SHORT_CONV),
        "hy_conv_b": small((Dp, 3 * HY_WIDTH)),
        "filt_w1": nrm((Dp, FILTER_EMB, FILTER_HIDDEN), FILTER_EMB),
        "filt_b1": small((Dp, FILTER_HIDDEN), 0.1),
        "filt_freq1": gain((Dp, FILTER_HIDDEN)),
        "filt_w2": nrm((Dp, FILTER_HIDDEN, FILTER_HIDDEN), FILTER_HIDDEN),
        "filt_b2": small((Dp, FILTER_HIDDEN), 0.1),
        "filt_freq2": gain((Dp, FILTER_HIDDEN)),
        "filt_w3": nrm((Dp, FILTER_HIDDEN, 2 * HY_WIDTH), FILTER_HIDDEN),
        "hy_bias": small((Dp, HY_WIDTH), 0.1),
        "q_norm_g": gain((Dp, Q_LORA)),
        "kv_norm_g": gain((Dp, KV_LORA)),
        "w_uq": nrm((Dp, Q_LORA, N_HEADS * (QK_NOPE + QK_ROPE)), Q_LORA),
        "w_uk": nrm((Dp, KV_LORA, N_HEADS, QK_NOPE), KV_LORA),
        "w_uv": nrm((Dp, KV_LORA, N_HEADS, V_HEAD), KV_LORA),
        "w_hy_out": nrm((Dp, HY_WIDTH, D), HY_WIDTH),
        "w_mla_out": nrm((Dp, MLA_WIDTH, D), MLA_WIDTH),
        "w_mix_out": nrm((Dp, D, D), D),
        "norm_ffn_g": gain((Dp, D)),
        "w_group": nrm((Dp, D, N_GROUPS), D),
        "b_group": small((Dp, N_GROUPS), 0.01),
        "w_router": nrm((Dp, D, N_EXPERTS), D),
        "b_router": small((Dp, N_EXPERTS), 0.01),
        "w_gate": nrm((Dp, N_EXPERTS, D, D_EXPERT), D),
        "w_up": nrm((Dp, N_EXPERTS, D, D_EXPERT), D),
        "w_down": nrm((Dp, N_EXPERTS, D_EXPERT, D), D_EXPERT),
        "final_norm_g": gain((D,)),
    }

def reference(x, c, ada_w, ada_b, norm_mix_g, w_in, hy_conv_w, hy_conv_b, filt_w1, filt_b1,
              filt_freq1, filt_w2, filt_b2, filt_freq2, filt_w3, hy_bias, q_norm_g, kv_norm_g,
              w_uq, w_uk, w_uv, w_hy_out, w_mla_out, w_mix_out, norm_ffn_g, w_group, b_group,
              w_router, b_router, w_gate, w_up, w_down, final_norm_g):
    L = x.shape[1]
    cos, sin = _rope_tables(L)
    c_act = jax.nn.silu(c)
    for l in range(DEPTH):
        mod = (c_act @ ada_w[l] + ada_b[l])[:, None, :]
        sh1, sc1, gt1, sh2, sc2, gt2 = jnp.split(mod, 6, axis=-1)
        h = _rmsnorm(x, norm_mix_g[l]) * (1.0 + sc1) + sh1
        x = x + gt1 * _token_mixer(h, w_in[l], hy_conv_w[l], hy_conv_b[l], filt_w1[l], filt_b1[l],
                                   filt_freq1[l], filt_w2[l], filt_b2[l], filt_freq2[l], filt_w3[l],
                                   hy_bias[l], q_norm_g[l], kv_norm_g[l], w_uq[l], w_uk[l], w_uv[l],
                                   w_hy_out[l], w_mla_out[l], w_mix_out[l], cos, sin)
        h = _rmsnorm(x, norm_ffn_g[l]) * (1.0 + sc2) + sh2
        x = x + gt2 * _hier_moe(h, w_group[l], b_group[l], w_router[l], b_router[l],
                                w_gate[l], w_up[l], w_down[l])
    return _rmsnorm(x, final_norm_g)


_drawn_inputs = setup_inputs


def setup_inputs(seed=0):
    import zlib

    import numpy as np

    out = dict(_drawn_inputs(seed))
    spreads = {}
    factors = {'ada_b': 3.887,
     'norm_mix_g': 8.0,
     'hy_conv_b': 8.0,
     'filt_w1': 3.668,
     'filt_b1': 8.0,
     'filt_freq1': 8.0,
     'filt_w2': 3.962,
     'filt_b2': 8.0,
     'filt_freq2': 8.0,
     'filt_w3': 4.286,
     'q_norm_g': 8.0,
     'kv_norm_g': 8.0,
     'w_uq': 3.897,
     'w_uk': 4.261,
     'norm_ffn_g': 3.385,
     'b_group': 43.159,
     'b_router': 49.056}
    for name, (base, spread) in spreads.items():
        noise = np.random.default_rng([zlib.crc32(name.encode()), seed]).standard_normal(out[name].shape)
        drawn = base * np.exp(spread * noise) if base else spread * noise
        out[name] = __import__('jax').numpy.asarray(drawn.astype(out[name].dtype))
    for name, factor in factors.items():
        out[name] = (out[name] * factor).astype(out[name].dtype)
    return out
```

```python
import math
from contextlib import ExitStack

import concourse.bass as bass
from concourse import mybir

F32 = mybir.dt.float32
U32 = mybir.dt.uint32
I32 = mybir.dt.int32
ALU = mybir.AluOpType
ACT = mybir.ActivationFunctionType
X = mybir.AxisListType.X

P = 128
L = 512
TT = L // P
D = 1024
DC = D // P
HY = 512
HC = HY // P
NH, NOPE, ROPE, VH = 8, 64, 32, 64
QKD = NOPE + ROPE
QL, KVL = 384, 256
QC, KC = QL // P, KVL // P
OFF_Q = 3 * HY
OFF_KV = OFF_Q + QL
OFF_KR = OFF_KV + KVL
OFF_GATE = OFF_KR + ROPE
EPS = 1e-6
NG, EPG = 4, 8
NE = NG * EPG
DE = 256
BLK = 96
NBLK = -(-L // BLK)
MORE = BLK * (NBLK - 1)
EXPERT_SLOTS = 4
BIG = 3.0e38
SCORE_SCALE = float(QKD) ** -0.5
TWO_PI = 2.0 * math.pi
ROUND = 1.5 * 2.0 ** 23
PI2_HI = 6.28125
PI2_LO = TWO_PI - PI2_HI

C_ID, C_ONE, C_LT, C_I32, C_I32B, C_IB, C_TOK, C_I4, C_I4B = 0, 128, 256, 384, 416, 448, 448 + BLK, 452 + BLK, 456 + BLK
C_END = 460 + BLK

RING = 5
CHUNK = 4096


def block_kernel(nc, a, out, h2_dram, y_dram, y_more):
    ctx = ExitStack()
    with ctx:
        def sb(name, cols, dt=F32):
            return ctx.enter_context(nc.sbuf_tensor(name, [P, cols], dt))

        def sem(name):
            return ctx.enter_context(nc.semaphore(name))

        cst = sb("cst", C_END)
        ring = sb("ring", RING * CHUNK)
        ht_mem = sb("ht_mem", DC * L)
        bcast = sb("bcast", 4 * D)
        AR = 84 * 256
        arena = sb("arena", AR)
        cols = sb("cols", 256)
        small = sb("small", 1024)
        smallu = sb("smallu", 256, U32)
        banks = [ctx.enter_context(nc.psum_tensor(f"bank{i}", [P, 512], F32)) for i in range(8)]

        ident, ones = cst[:, C_ID:C_ID + P], cst[:, C_ONE:C_ONE + P]
        lower = cst[:, C_LT:C_LT + P]

        def view(mem, at_, size_, **dims):
            v = mem[:, at_:at_ + size_]
            names = list(dims)
            return v.rearrange(f"p ({' '.join(names)}) -> p {' '.join(names)}", **{k: dims[k] for k in names[1:]})

        hT = view(ht_mem, 0, DC * L, c=DC, t=L)
        ccol, cact = cols[:, 0:8], cols[:, 8:16]
        modcol = cols[:, 16:32]
        g1col, a1col = cols[:, 32:40], cols[:, 40:48]
        convw = view(cols, 48, 36, w=3, c=12)
        convb = cols[:, 84:96]
        fb1, ff1, fb2, ff2 = (cols[0:64, 96 + i:97 + i] for i in range(4))
        hybias, invl1 = cols[:, 100:104], cols[:, 104:108]
        gq, gkv = cols[:, 108:111], cols[:, 111:113]
        ss, rstd, srt = cols[:, 116:120], cols[:, 120:124], cols[:, 124:128]
        ss2, rstd2, srt2 = cols[:, 128:132], cols[:, 132:136], cols[:, 136:140]
        ss3, rstd3, srt3 = cols[:, 140:144], cols[:, 144:148], cols[:, 148:152]
        rowmax, negmax, rowsum, rinv = (cols[:, 152 + 4 * i:156 + 4 * i] for i in range(4))
        cexp, cden, crec = cols[:, 168:176], cols[:, 176:184], cols[:, 184:192]

        K = 256
        filt = view(arena, 0, 16 * K, t=TT, d=2, c=HY)
        spec = view(arena, 0, 16 * K, f=4, r=2, c=HY)
        G = view(arena, 16 * K, 16 * K, f=4, r=2, c=HY)
        xin = view(arena, 32 * K, 16 * K, t=TT, d=D)
        x0T = view(arena, 32 * K, 8 * K, c=HC, t=L)
        uT = view(arena, 40 * K, 8 * K, c=HC, t=L)
        argT = arena[0:64, 48 * K:50 * K]
        rndT = arena[0:64, 50 * K:52 * K]
        absum = view(arena, 48 * K, 8 * K, t=TT, c=HY)
        x1T = view(arena, 48 * K, 8 * K, c=HC, t=L)
        uTok = view(arena, 48 * K, 8 * K, t=TT, c=HY)
        window = view(arena, 56 * K, 8 * K, t=TT, c=HY)
        cm = view(arena, 56 * K, 8 * K, b=4, n=512)
        adasum = view(arena, 64 * K, 4 * K, b=2, n=512)
        adab = view(arena, 68 * K, 4 * K, b=2, n=512)
        zT = arena[0:33, 72 * K:74 * K]
        fw1 = arena[0:33, 74 * K:74 * K + 64]
        fw2 = arena[0:64, 74 * K + 64:74 * K + 128]
        fw3 = arena[0:64, 76 * K:80 * K]
        xsq = arena[:, 72 * K:76 * K]
        yhy = view(arena, 72 * K, 8 * K, c=HC, t=L)
        s1T = arena[0:64, 80 * K:82 * K]
        s2T = arena[0:64, 82 * K:84 * K]
        cvt = view(arena, 80 * K, 4 * K, b=2, t=512)
        dftf = view(bcast, 0, 16 * K, s=2, c=4, n=512)
        qh = view(arena, 0, 16 * K, h=NH, t=L)
        kh = view(arena, 16 * K, 16 * K, h=NH, t=L)
        cqT = view(arena, 32 * K, 6 * K, c=QC, t=L)
        ckvT = view(arena, 38 * K, 4 * K, c=KC, t=L)
        sqT = view(arena, 42 * K, 6 * K, b=3, t=L)
        rb = arena[:, 48 * K:50 * K]
        rope = view(arena, 50 * K, 4 * K, s=2, t=L)
        wrot = view(arena, 54 * K, 3 * K, c=QC, h=NH, n=ROPE)
        wkrot = view(arena, 57 * K, K, c=DC, n=ROPE)
        rt = view(arena, 58 * K, 4 * K, b=2, t=L)
        krope = arena[:, 62 * K:64 * K]
        ktmp = arena[:, 82 * K:84 * K]
        prob = view(arena, 32 * K, 6 * K, b=3, n=L)
        pT = view(arena, 42 * K, 4 * K, b=2, n=L)
        v_sb = view(arena, 48 * K, 8 * K, t=TT, n=NH * VH)
        ymla = view(arena, 56 * K, 8 * K, c=4, t=L)
        mixT = view(arena, 0, 16 * K, c=DC, t=L)
        x1 = view(arena, 16 * K, 16 * K, t=TT, d=D)
        sg = view(arena, 32 * K, 8 * K, b=4, n=512)
        gated = view(arena, 42 * K, 4 * K, b=2, n=512)
        h2T = view(arena, 0, 16 * K, c=DC, t=L)
        h2 = view(ht_mem, 0, 16 * K, t=TT, d=D)
        wr = view(arena, 32 * K, DC * (NG + NE), c=DC, n=NG + NE)
        brow = arena[0:1, 34 * K:34 * K + NG + NE]
        g2b = arena[:, 36 * K:40 * K]
        fgb = arena[:, 80 * K:84 * K]
        hg = view(arena, 0, 8 * K, b=2, d=D)
        hgT = view(arena, 8 * K, 6 * K, b=2, c=DC, s=BLK)
        sgl = view(arena, 32 * K, 4 * BLK, b=2, n=2 * BLK)
        aT = view(arena, 32 * K + 4 * BLK, 4 * BLK, b=2, n=2 * BLK)
        yb = view(arena, 40 * K, 8 * K, b=2, d=D)
        emem = [(ring, 0), (ring, 24 * K), (ring, 48 * K), (arena, 48 * K)]
        wg_s = [view(m, o, 8 * K, c=DC, n=DE) for m, o in emem]
        wu_s = [view(m, o + 8 * K, 8 * K, c=DC, n=DE) for m, o in emem]
        wd_s = [view(m, o + 16 * K, 8 * K, c=2, n=D) for m, o in emem]
        yg = view(ht_mem, 0, 16 * K, b=4, d=D)
        outb = view(ring, 24 * K, 8 * K, b=2, d=D)
        osq = ring[:, 32 * K:36 * K]
        R0 = 72 * K
        lg = view(arena, R0, 144, t=TT, n=NG + NE)
        em = view(arena, R0 + 144, 128, t=TT, n=NE)
        eq = view(arena, R0 + 272, 128, t=TT, n=NE)
        oh1 = view(arena, R0 + 400, 128, t=TT, n=NE)
        oh2 = view(arena, R0 + 528, 128, t=TT, n=NE)
        ohs = view(arena, R0 + 656, 128, t=TT, n=NE)
        rk = view(arena, R0 + 784, 128, t=TT, n=NE)
        ohv = view(arena, R0 + 912, 256, k=2, t=TT, n=NE)
        Rm = view(arena, R0 + 1168, 8 * BLK, k=2, t=TT, s=BLK)
        (gmax, gsum, psel, i0, m1, m2, i1, i2, dv, ed, w1c, w2c, yc1, yc2, r1, r2) = (small[:, 4 * i:4 * i + 4] for i in range(16))
        r12 = view(small, 56, 8, k=2, t=TT)
        gs, gm, pen, geq = (view(small, 64 + 16 * i, 16, t=TT, n=NG) for i in range(4))
        cnt, over = small[:, 128:160], small[:, 160:161]
        idxu = smallu[0:BLK, 0:32]
        yrow = view(smallu, 32, 8, k=2, t=TT)
        morerow = view(smallu, 48, 8, k=2, t=TT)
        wfirst = view(small, 184, 8, k=2, t=TT)
        wmore = view(small, 192, 8, k=2, t=TT)
        rowf, rankf = small[:, 200:204], small[:, 204:208]
        idxc = smallu[0:BLK, 40:42]
        overu = smallu[:, 44:45]

        pe_done = sem("pe_unit_done")
        read_sem = {"act": sem("act_unit_read"), "dve": sem("dve_unit_read")}
        dve_step, act_step = sem("dve_step"), sem("act_step")
        ring_in = [sem(f"ring_in{i}") for i in range(RING)]
        bias_clear, bias_in, ada_done = sem("ada_bias_clear"), [sem(f"ada_bias_in{i}") for i in range(2)], sem("ada_sum_done")
        loaded = {n: sem("in_" + n) for n in
                  "cst c zT fw fb window dftf x g1col conv hyb gqk rope ffng router x1 fing".split()}
        cact_done, sin_arg, sin_done, filt_ready, absum_ready = (sem(n) for n in (
            "c_act", "sin_arg", "sin_done", "filter_ready", "filter_abs_ready"))
        x_sumsq, x_scaled, a1_ready, sqrt_arg, sqrt_done = (sem(n) for n in (
            "x_sumsq", "x_scaled", "a1_ready", "sqrt_arg", "sqrt_done"))
        conv_centre, u_ready, spec_ready, yhy_ready = (sem(n) for n in (
            "conv_centre", "u_ready", "spectrum_ready", "y_hyena"))
        sq_ready, latent_ready, rotw_ready, kr_done, kr_copied, q_rope = (sem(n) for n in (
            "latent_square", "latent_normed", "rotated_weights", "k_rope", "k_rope_copied", "q_rope"))
        max_done, prob_done = sem("row_max"), sem("probs_normed")
        mix_done, x1_done, x1_sumsq, h2_done, h2_out = (sem(n) for n in (
            "mix_done", "x1_done", "x1_sumsq", "h2_done", "h2_written"))
        onehots, gexp, gexp_done, wexp, wexp_done, slots_ready, idx_ready, over_ready = (sem(n) for n in (
            "onehots", "g_shifted", "g_exp", "w_shifted", "w_exp", "slot_onehots", "slot_tokens", "overflow_known"))
        gu_in = [sem(f"gate_up_in{i}") for i in range(EXPERT_SLOTS)]
        dn_in = [sem(f"down_in{i}") for i in range(EXPERT_SLOTS)]
        rows_in = [sem(f"rows_in{i}") for i in range(2)]
        y_out = [sem(f"y_written{i}") for i in range(2)]
        turned, turned_act, turned_dve, gu_done, silu_done, a_done, y_done, y_act, y_dve = (sem(n) for n in (
            "rows_turned", "turned_read_act", "turned_read_dve", "gate_up_done", "silu_done", "hidden_done",
            "expert_y_done", "y_read_act", "y_read_dve"))
        back_in = [sem(f"back_in{i}") for i in range(4)]
        x2_done, x2_sumsq, sqrt3_arg, sqrt3_done, out_ready = (sem(n) for n in (
            "x2_done", "x2_sumsq", "sqrt3_arg", "sqrt3_done", "out_ready"))
        out_done = [sem(f"out_written{i}") for i in range(2)]
        o_slots, o_tok, o_idx, o_rows, o_turned, o_read, o_gu, o_silu, o_hidden, o_y, o_yread, o_out, o_w = (
            sem("over_" + n) for n in ("slots", "tokens", "idx", "rows", "turned", "turned_read", "gate_up", "silu",
                                       "hidden", "y", "y_read", "y_out", "weights"))
        rows_known, o_back, o_added = sem("y_rows_known"), sem("over_back"), sem("over_added")
        o_scaled = sem("over_scaled")
        o_rank, o_idxu = sem("over_rank"), sem("over_slot_tokens")

        units = []

        def plan(reader, *keys):
            units.extend((k, reader) for k in keys)

        NA, LAG = NH * TT, 3
        plan("dve", ("F1",), ("F2",), *(("F3", t, d) for t in range(TT) for d in range(2)), ("L1",))
        plan("act", *(("G", f, r) for f in range(4) for r in range(2)), *(("AC", j) for j in range(4)),
             *(("XT", c) for c in range(DC)))
        plan("dve", *(("H", m) for m in range(3 * HC)))
        plan("act", *(("UT", t) for t in range(TT)))
        plan("dve", *(("UF", f, r) for f in range(4) for r in range(2)))
        plan("act", ("AB", 4), ("AB", 5))
        plan("dve", *(("YI", c) for c in range(HC)))
        plan("act", *(("CQ", m) for m in range(QC)), *(("CK", m) for m in range(KC)))
        plan("dve", ("KR",), ("KT",), ("QS",), ("KS",))
        plan("act", ("AB", 6), ("AB", 7), *(("QN", i) for i in range(4)))
        plan("dve", *((k, g) for g in range(2) for k in ("QR", "QT")))
        plan("act", *(("KN", i) for i in range(4)), *(("V", t) for t in range(TT)))
        AB_AT = {4: 8, 10: 9, 16: 10, 22: 11}
        for n in range(NA + LAG):
            if n < NA:
                plan("act", ("S", n))
            if n in AB_AT:
                plan("act", ("AB", AB_AT[n]))
            if n >= LAG:
                plan("dve", ("T", n - LAG))
                plan("act", ("O", n - LAG))
        for d in range(DC):
            plan("act", ("GA", d), ("GB", d))
            plan("dve", ("MA", d), ("MB", d))
        plan("dve", *(("W", hf, t) for hf in range(2) for t in range(TT)))
        plan("act", *(("HT", c) for c in range(DC)))
        plan("dve", ("LG",), ("RK",), ("IX",))
        number = {k: n for n, (k, _) in enumerate(units)}
        reader, nth, seen = dict(units), {}, {"act": 0, "dve": 0}
        for k, r in units:
            seen[r] += 1
            nth[k] = seen[r]

        def bank(*k):
            return banks[number[k] % 8]

        def claim(*k):
            n = number[k]
            if n >= 8:
                old = units[n - 8][0]
                nc.tensor.wait_ge(read_sem[reader[old]], nth[old])

        def ready(eng, *k):
            eng.wait_ge(pe_done, number[k] + 1)

        def taken(eng, *k):
            eng.wait_ge(read_sem[reader[k]], nth[k])

        w_in3 = a["w_in"][0].rearrange("(c p) n -> p c n", p=P)
        ada3 = a["ada_w"][0].rearrange("(c p) n -> p c n", p=P)
        mix3 = a["w_mix_out"][0].rearrange("(c p) n -> p c n", p=P)
        chunks = [("ada", 0), ("ada", 1), ("ada", 2), ("ada", 3), ("hy", 0), ("hy", 1), ("hy", 2), ("ada", 4), ("ada", 5),
                  ("dft",), ("cq",), ("ckv",), ("ada", 6), ("ada", 7), ("uquk",), ("uv",), ("ada", 8), ("ada", 9), ("ada", 10),
                  ("ada", 11), ("g", 0, 0), ("g", 1, 0), ("whyo",), ("wmlao",), ("g", 0, 1), ("g", 1, 1), ("mix", 0), ("mix", 1)]
        place = {k: n for n, k in enumerate(chunks)}
        last_use = {("hy", 0): ("H", 3), ("hy", 1): ("H", 7), ("hy", 2): ("H", 11), ("dft",): ("YI", 3),
                    ("cq",): ("CQ", QC - 1), ("ckv",): ("KT",), ("uquk",): ("KN", 3), ("uv",): ("V", 3),
                    ("g", 0, 0): ("GA", 3), ("g", 1, 0): ("GB", 3), ("whyo",): ("MA", 7), ("wmlao",): ("MB", 7),
                    ("g", 0, 1): ("GA", 7), ("g", 1, 1): ("GB", 7), ("mix", 0): ("W", 0, 3), ("mix", 1): ("W", 1, 3)}

        def at(*k):
            s = place[k] % RING
            return ring[:, s * CHUNK:(s + 1) * CHUNK]

        def arrived(eng, *k):
            n = place[k]
            eng.wait_ge(ring_in[n % RING], 16 * sum(7 if chunks[m] == ("uquk",) else 1 for m in range(n % RING, n + 1, RING)))

        w8 = {k: at(*k).rearrange("p (c n) -> p c n", c=DC) for k in chunks if k[0] in ("ada", "hy", "g", "mix")}
        wcq = at("cq")[:, 0:DC * QL].rearrange("p (c n) -> p c n", c=DC)
        wckv = at("ckv")[:, 0:DC * (KVL + ROPE)].rearrange("p (c n) -> p c n", c=DC)
        dfti = at("dft").rearrange("p (s c n) -> p s c n", s=2, c=4)
        QN_COLS = QC * NH * NOPE
        wuqn = at("uquk")[:, 0:QN_COLS].rearrange("p (c h n) -> p c h n", c=QC, h=NH)
        wuqr = at("uquk")[:, QN_COLS:QC * NH * QKD].rearrange("p (c h n) -> p c h n", c=QC, h=NH)
        wuk = at("uquk")[:, QC * NH * QKD:QC * NH * QKD + KC * NH * NOPE].rearrange("p (c n) -> p c n", c=KC)
        wuv = at("uv")[:, 0:KC * NH * VH].rearrange("p (c n) -> p c n", c=KC)
        whyo = at("whyo").rearrange("p (c n) -> p c n", c=HC)
        wmlao = at("wmlao").rearrange("p (c n) -> p c n", c=HC)
        wg_d = a["w_gate"][0].rearrange("e (p c) n -> e p (c n)", c=DC)
        wu_d = a["w_up"][0].rearrange("e (p c) n -> e p (c n)", c=DC)
        wd_d = a["w_down"][0].rearrange("e (c p) n -> e p c n", p=P)
        y_flat = y_dram.rearrange("e s d -> (e s) d")
        more_flat = y_more.rearrange("e s d -> (e s) d")

        def entry(v, e):
            if isinstance(e, int):
                return v[e]
            v = v[bass.ds(e, 1)]
            return v.rearrange("o p n -> (o p) n") if len(v.shape) == 3 else v.rearrange("o p c n -> (o p) c n")

        def over_flag(eng):
            eng.wait_ge(over_ready, 1)
            return eng.value_load(overu[0:1, 0:1], min_val=0, max_val=1)

        block = ctx.enter_context(nc.Block())

        @block.sync
        def _(sp):
            def load_expert(e, s):
                sp.dma_start(wg_s[s].rearrange("p c n -> p (c n)"), entry(wg_d, e)).then_inc(gu_in[s], 16)
                sp.dma_start(wu_s[s].rearrange("p c n -> p (c n)"), entry(wu_d, e)).then_inc(gu_in[s], 16)
                sp.dma_start(wd_s[s], entry(wd_d, e)).then_inc(dn_in[s], 16)

            source = {("dft",): (at("dft"), a["dfti"]), ("cq",): (wcq, w_in3[:, :, OFF_Q:OFF_KV]),
                      ("ckv",): (wckv, w_in3[:, :, OFF_KV:OFF_GATE]),
                      ("uv",): (wuv, a["w_uv"][0].rearrange("(c p) h n -> p c (h n)", p=P)),
                      ("whyo",): (whyo, a["w_hy_out"][0].rearrange("(c p) n -> p c n", p=P)),
                      ("wmlao",): (wmlao, a["w_mla_out"][0].rearrange("(c p) n -> p c n", p=P)),
                      ("uquk",): (wuk, a["w_uk"][0].rearrange("(c p) h n -> p c (h n)", p=P))}
            for k in chunks:
                if k[0] == "ada":
                    source[k] = (w8[k], ada3[:, :, k[1] * 512:(k[1] + 1) * 512])
                elif k[0] == "hy":
                    source[k] = (w8[k], w_in3[:, :, k[1] * 512:(k[1] + 1) * 512])
                elif k[0] == "g":
                    o = OFF_GATE + k[1] * D + k[2] * 512
                    source[k] = (w8[k], w_in3[:, :, o:o + 512])
                elif k[0] == "mix":
                    source[k] = (w8[k], mix3[:, :, k[1] * 512:(k[1] + 1) * 512])
            for n, k in enumerate(chunks):
                if n >= RING:
                    old = chunks[n - RING]
                    if old[0] == "ada":
                        sp.wait_ge(ada_done, old[1] + 1)
                    else:
                        ready(sp, *last_use[old])
                sp.dma_start(*source[k]).then_inc(ring_in[n % RING], 16)
                if k == ("uquk",):
                    wuq_d = a["w_uq"][0].rearrange("(c p) (h n) -> c p h n", p=P, h=NH)
                    for c in range(QC):
                        sp.dma_start(wuqn[:, c], wuq_d[c, :, :, 0:NOPE]).then_inc(ring_in[n % RING], 16)
                        sp.dma_start(wuqr[:, c], wuq_d[c, :, :, NOPE:QKD]).then_inc(ring_in[n % RING], 16)
                if k[0] == "ada":
                    j = k[1]
                    if j >= 2:
                        sp.wait_ge(ada_done, j - 1)
                    else:
                        sp.wait_ge(bias_clear, 1)
                    sp.dma_start(adab[0:1, j % 2, :], a["ada_b"][0:1, j * 512:(j + 1) * 512]).then_inc(bias_in[j % 2], 16)
                if k == ("g", 0, 1):
                    taken(sp, "O", NA - 1)
                    sp.dma_start(x1, a["x"][0].rearrange("(t p) d -> p t d", p=P)).then_inc(loaded["x1"], 16)
            ready(sp, "MB", DC - 1)
            load_expert(3, 3)
            ready(sp, "W", 1, TT - 1)
            for e in range(3):
                load_expert(e, e)
            for t in range(TT):
                sp.wait_ge(h2_done, t + 1)
                sp.dma_start(h2_dram[t * P:(t + 1) * P, :], h2[:, t, :]).then_inc(h2_out, 16)

            def write_rows(e, s):
                sp.wait_ge(y_act, e + 1)
                sp.wait_ge(y_dve, e + 1)
                sp.dma_start(entry(y_dram, e), yb[0:BLK, s % 2, :]).then_inc(y_out[s % 2], 16)

            with sp.Fori(0, NE // EXPERT_SLOTS - 1) as i:
                for s in range(EXPERT_SLOTS):
                    e = i * EXPERT_SLOTS + s
                    write_rows(e, s)
                    load_expert(e + EXPERT_SLOTS, s)
            for s in range(EXPERT_SLOTS):
                write_rows(NE - EXPERT_SLOTS + s, s)
            sp.dma_start(fgb, a["final_norm_g"].rearrange("(o n) -> o n", o=1).broadcast_to([P, D])).then_inc(loaded["fing"], 16)

            with sp.If(over_flag(sp) > 0):
                with sp.Fori(0, NBLK - 1) as b:
                    with sp.Fori(0, NE) as e:
                        n = b * NE + e
                        sp.wait_ge(o_yread, n + 1)
                        sp.dma_start(wg_s[0].rearrange("p c n -> p (c n)"), entry(wg_d, e)).then_inc(o_w, 16)
                        sp.dma_start(wu_s[0].rearrange("p c n -> p (c n)"), entry(wu_d, e)).then_inc(o_w, 16)
                        sp.dma_start(wd_s[0], entry(wd_d, e)).then_inc(o_w, 16)
                        sp.wait_ge(o_yread, n + 2)
                        sp.dma_start(more_flat[bass.ds(e * MORE + b * BLK, BLK), :], yb[0:BLK, 0, :]).then_inc(o_out, 16)
            for t in range(TT):
                sp.wait_ge(out_ready, t + 1)
                sp.dma_start(out[0, t * P:(t + 1) * P, :], outb[:, t % 2, :]).then_inc(out_done[t % 2], 16)
            for i in range(2):
                sp.wait_ge(out_done[i], 16 * (TT // 2))

        @block.gpsimd
        def _(pool):
            def col(dst, v, s):
                pool.dma_start(dst, v.rearrange("(c p) -> p c", p=P), allow_slow_non_contiguous=True).then_inc(loaded[s], 16)
            pool.dma_start(zT, a["zT"]).then_inc(loaded["zT"], 16)
            pool.dma_start(fw1, a["filt_w1"][0]).then_inc(loaded["fw"], 16)
            for dst, nm in ((fb1, "filt_b1"), (ff1, "filt_freq1"), (fb2, "filt_b2"), (ff2, "filt_freq2")):
                pool.dma_start(dst, a[nm][0].rearrange("(p o) -> p o", o=1), allow_slow_non_contiguous=True).then_inc(loaded["fb"], 16)
            col(ccol, a["c"][0], "c")
            pool.dma_start(fw2, a["filt_w2"][0]).then_inc(loaded["fw"], 16)
            pool.dma_start(fw3, a["filt_w3"][0]).then_inc(loaded["fw"], 16)
            pool.dma_start(cst[:, :], a["cst"]).then_inc(loaded["cst"], 16)
            pool.dma_start(window, a["window"].rearrange("(t p) c -> p t c", p=P)).then_inc(loaded["window"], 16)
            pool.dma_start(bcast[:, :], a["dftf"]).then_inc(loaded["dftf"], 16)
            pool.dma_start(xin, a["x"][0].rearrange("(t p) d -> p t d", p=P)).then_inc(loaded["x"], 16)
            col(g1col, a["norm_mix_g"][0], "g1col")
            for w in range(3):
                col(convw[:, w, :], a["hy_conv_w"][0, w], "conv")
            col(convb, a["hy_conv_b"][0], "conv")
            col(hybias, a["hy_bias"][0], "hyb")
            col(gq, a["q_norm_g"][0], "gqk")
            col(gkv, a["kv_norm_g"][0], "gqk")
            taken(pool, "YI", 3)
            ready(pool, "YI", 3)
            pool.dma_start(rope, a["rope"]).then_inc(loaded["rope"], 16)
            pool.wait_ge(kr_done, 1)
            for h in range(NH):
                nc.gpsimd.tensor_copy(kh[NOPE:QKD, h, :], krope[NOPE:QKD, :]).then_inc(kr_copied, 1)
            pool.wait_ge(mix_done, DC)
            pool.dma_start(g2b, a["norm_ffn_g"].broadcast_to([P, D])).then_inc(loaded["ffng"], 16)
            pool.dma_start(wr[:, :, 0:NG], a["w_group"][0].rearrange("(c p) n -> p c n", p=P)).then_inc(loaded["router"], 16)
            pool.dma_start(wr[:, :, NG:NG + NE], a["w_router"][0].rearrange("(c p) n -> p c n", p=P)).then_inc(loaded["router"], 16)
            pool.dma_start(brow[:, 0:NG], a["b_group"][0:1, :]).then_inc(loaded["router"], 16)
            pool.dma_start(brow[:, NG:NG + NE], a["b_router"][0:1, :]).then_inc(loaded["router"], 16)
            pool.wait_ge(idx_ready, 1)
            pool.wait_ge(h2_out, 16 * TT)

            for e in range(NE):
                if e >= 2:
                    pool.wait_ge(turned, e - 1)
                pool.indirect_dma_start(out=hg[0:BLK, e % 2, :], out_offset=None, in_=h2_dram[:, :],
                                        in_offset=bass.IndirectOffsetOnAxis(ap=idxu[:, e:e + 1], axis=0)).then_inc(rows_in[e % 2], 16)
            with pool.If(over_flag(pool) > 0):
                with pool.Fori(0, NBLK - 1) as b:
                    with pool.Fori(0, NE) as e:
                        n = b * NE + e
                        pool.wait_ge(o_idx, n + 1)
                        nc.gpsimd.tensor_tensor(small[:, 176:177], ones[:, 0:1], ones[:, 0:1], ALU.mult)
                        pool.indirect_dma_start(out=hg[0:BLK, 0, :], out_offset=None, in_=h2_dram[:, :],
                                                in_offset=bass.IndirectOffsetOnAxis(ap=idxc[:, 0:1], axis=0)).then_inc(o_rows, 16)
                pool.wait_ge(o_out, 16 * (NBLK - 1) * NE)
                for t in range(TT):
                    for k in range(2):
                        n = 2 * t + k
                        if n:
                            pool.wait_ge(o_added, n)
                        pool.indirect_dma_start(out=yg[:, 0, :], out_offset=None, in_=more_flat,
                                                in_offset=bass.IndirectOffsetOnAxis(ap=morerow[:, k, t:t + 1], axis=0)).then_inc(o_back, 16)
                pool.wait_ge(o_added, 2 * TT)
            for s in range(2):
                pool.wait_ge(y_out[s], 16 * (NE // 2))
            pool.wait_ge(rows_known, 1)
            for t in range(TT):
                for k in range(2):
                    n = 2 * t + k
                    if n >= 4:
                        pool.wait_ge(x2_done, t - 1)
                    pool.indirect_dma_start(out=yg[:, n % 4, :], out_offset=None, in_=y_flat,
                                            in_offset=bass.IndirectOffsetOnAxis(ap=yrow[:, k, t:t + 1], axis=0)).then_inc(back_in[n % 4], 16)

        @block.scalar
        def _(act):
            A = nc.scalar.activation
            step = [0]

            def link(ins):
                step[0] += 1
                ins.then_inc(act_step, 1)
                act.wait_ge(act_step, step[0])

            act.wait_ge(loaded["c"], 16)
            A(cact, ccol, ACT.Silu).then_inc(cact_done, 1)
            for n, dst in enumerate((s1T, s2T)):
                act.wait_ge(sin_arg, n + 1)
                A(dst, argT, ACT.Sin).then_inc(sin_done, 1)
            for f in range(4):
                for r in range(2):
                    ready(act, "G", f, r)
                    A(G[:, f, r, :], bank("G", f, r)[:, :], ACT.Copy).then_inc(read_sem["act"], 1)
            act.wait_ge(loaded["x"], 16)
            for t in range(TT):
                if t:
                    act.wait_ge(x_sumsq, t)
                A(xsq, xin[:, t, :], ACT.Square, accum_out=ss[:, t:t + 1]).then_inc(x_sumsq, 1)
            act.wait_ge(sqrt_arg, 1)
            A(srt, rstd, ACT.Sqrt).then_inc(sqrt_done, 1)
            for j in range(4):
                ready(act, "AC", j)
                A(modcol[:, 4 * j:4 * j + 4], bank("AC", j)[:, 0:4], ACT.Copy).then_inc(read_sem["act"], 1)
            act.wait_ge(a1_ready, 1)
            for c in range(DC):
                ready(act, "XT", c)
                A(hT[:, c, :], bank("XT", c)[:, :], ACT.Identity, bias=modcol[:, c:c + 1],
                  scale=a1col[:, c:c + 1]).then_inc(read_sem["act"], 1)

            def ada_row(j):
                ready(act, "AB", j)
                A(bcast[:, (j - 4) * 512:(j - 3) * 512], bank("AB", j)[:, :], ACT.Copy).then_inc(read_sem["act"], 1)

            act.wait_ge(loaded["conv"], 64)
            for m in range(3 * HC):
                ready(act, "H", m)
                if m >= 10:
                    act.wait_ge(u_ready, m - 9)
                dst = x0T[:, m, :] if m < HC else x1T[:, m - HC, :] if m < 2 * HC else cvt[:, m % 2, :]
                A(dst, bank("H", m)[:, :], ACT.Identity, bias=convb[:, m:m + 1],
                  scale=convw[:, 1, m:m + 1]).then_inc(conv_centre, 1)
            for t in range(TT):
                ready(act, "UT", t)
                A(uTok[:, t, :], bank("UT", t)[:, :], ACT.Copy).then_inc(read_sem["act"], 1)
            ada_row(4), ada_row(5)
            act.wait_ge(yhy_ready, HC)
            for m in range(QC + KC):
                k = ("CQ", m) if m < QC else ("CK", m - QC)
                raw = cqT[:, m, :] if m < QC else ckvT[:, m - QC, :]
                sq = sqT[:, m, :] if m < QC else rt[:, m - QC, :]
                ready(act, *k)
                A(sq, bank(*k)[:, :], ACT.Square).then_inc(sq_ready, 1)
                A(raw, bank(*k)[:, :], ACT.Copy).then_inc(read_sem["act"], 1)
            for n in range(2):
                act.wait_ge(sqrt_arg, 2 + n)
                A(rb, rb, ACT.Sqrt).then_inc(sqrt_done, 1)
            ada_row(6), ada_row(7)

            def two_heads(k, i, dst):
                ready(act, k, i)
                link(A(dst[0:NOPE, 2 * i, :], bank(k, i)[0:64, :], ACT.Copy))
                A(dst[0:NOPE, 2 * i + 1, :], bank(k, i)[64:128, :], ACT.Copy).then_inc(read_sem["act"], 1)

            for i in range(4):
                two_heads("QN", i, qh)
            for i in range(4):
                two_heads("KN", i, kh)
            act.wait_ge(q_rope, NH)
            for t in range(TT):
                ready(act, "V", t)
                A(v_sb[:, t, :], bank("V", t)[:, :], ACT.Copy).then_inc(read_sem["act"], 1)
            act.wait_ge(kr_copied, NH)

            def exps(n):
                act.wait_ge(max_done, n + 1)
                if n >= 3:
                    ready(act, "T", n - 3)
                A(prob[:, n % 3, :], bank("S", n)[:, :], ACT.Exp, bias=negmax[:, n % 4:n % 4 + 1], scale=SCORE_SCALE,
                  accum_out=rowsum[:, n % 4:n % 4 + 1]).then_inc(read_sem["act"], 1)

            def head_rows(n):
                h, t = n // TT, n % TT
                o = VH * (h % 2)
                ready(act, "O", n)
                A(ymla[o:o + VH, h // 2, t * P:(t + 1) * P], bank("O", n)[o:o + VH, 0:P], ACT.Copy).then_inc(read_sem["act"], 1)

            for n in range(NA + LAG):
                if n < NA:
                    exps(n)
                if n in AB_AT:
                    ada_row(AB_AT[n])
                if n >= LAG:
                    head_rows(n - LAG)
            for d in range(DC):
                for g, k in enumerate(("GA", "GB")):
                    ready(act, k, d)
                    if d >= 2:
                        act.wait_ge(mix_done, d - 1)
                    A(sg[:, (2 * d + g) % 4, :], bank(k, d)[:, :], ACT.Sigmoid).then_inc(read_sem["act"], 1)
            for t in range(TT):
                act.wait_ge(x1_done, t + 1)
                if t:
                    act.wait_ge(x1_sumsq, t)
                A(h2[:, 3, :], x1[:, t, :], ACT.Square, accum_out=ss2[:, t:t + 1]).then_inc(x1_sumsq, 1)
            act.wait_ge(sqrt_arg, 4)
            A(srt2, rstd2, ACT.Sqrt).then_inc(sqrt_done, 1)
            for c in range(DC):
                ready(act, "HT", c)
                A(h2T[:, c, :], bank("HT", c)[:, :], ACT.Copy).then_inc(read_sem["act"], 1)
            act.wait_ge(gexp, 1)
            A(gs, gs, ACT.Exp).then_inc(gexp_done, 1)
            act.wait_ge(wexp, 1)
            A(ed, dv, ACT.Exp).then_inc(wexp_done, 1)

            def turned_rows(e, s):
                act.wait_ge(turned, e + 1)
                if not (isinstance(e, int) and e < 2):
                    act.wait_ge(gu_done, e - 1)
                A(hgT[:, s % 2, 0:4, :], banks[0][:, 0:4 * BLK].rearrange("p (c s) -> p c s", c=4), ACT.Copy).then_inc(turned_act, 1)

            def silu(e, s):
                act.wait_ge(gu_done, e + 1)
                if not (isinstance(e, int) and e < 2):
                    act.wait_ge(a_done, e - 1)
                A(sgl[:, s % 2, :], banks[2 + s % 2][:, 0:2 * BLK], ACT.Silu).then_inc(silu_done, 1)

            def y_half(e, s, i):
                act.wait_ge(y_done, e + 1)
                if not (isinstance(e, int) and e < 2):
                    act.wait_ge(y_out[s % 2], i * 32 + 16 * (s // 2))
                A(yb[0:BLK, s % 2, 0:512], banks[4 + 2 * (s % 2)][0:BLK, :], ACT.Copy).then_inc(y_act, 1)

            def four(i, first=False, last=False):
                for s in range(EXPERT_SLOTS):
                    e = i * EXPERT_SLOTS + s
                    silu(e, s)
                    if not (first and s == 0):
                        y_half(e - 1, (s - 1) % 4, i - 1 if s == 0 else i)
                    if not (last and s == EXPERT_SLOTS - 1):
                        turned_rows(e + 1, s + 1)
            turned_rows(0, 0)
            four(0, first=True)
            with act.Fori(1, NE // EXPERT_SLOTS - 1) as i:
                four(i)
            four(NE // EXPERT_SLOTS - 1, last=True)
            y_half(NE - 1, 3, NE // EXPERT_SLOTS - 1)
            with act.If(over_flag(act) > 0):
                with act.Fori(0, NBLK - 1) as b:
                    with act.Fori(0, NE) as e:
                        act.wait_ge(o_gu, b * NE + e + 1)
                        A(sgl[:, 0, :], banks[2][:, 0:2 * BLK], ACT.Silu).then_inc(o_silu, 1)
            for t in range(TT):
                act.wait_ge(x2_done, t + 1)
                if t:
                    act.wait_ge(x2_sumsq, t)
                A(osq, x1[:, t, :], ACT.Square, accum_out=ss3[:, t:t + 1]).then_inc(x2_sumsq, 1)
                act.wait_ge(sqrt3_arg, t + 1)
                A(srt3[:, t:t + 1], rstd3[:, t:t + 1], ACT.Sqrt).then_inc(sqrt3_done, 1)

        @block.tensor
        def _(pe):
            def product(o, pairs):
                for i, (l, r) in enumerate(pairs):
                    mm = nc.tensor.matmul(o, l, r, start=(i == 0), stop=(i == len(pairs) - 1))
                return mm

            def tile_product(k, rows, pairs):
                claim(*k)
                product(bank(*k)[rows, :], pairs).then_inc(pe_done, 1)

            def full(k, pairs):
                tile_product(k, slice(0, P), pairs)

            def turn(k, parts):
                claim(*k)
                for i, p in enumerate(parts):
                    mm = nc.tensor.transpose(bank(*k)[:, i * P:(i + 1) * P], p, ident)
                mm.then_inc(pe_done, 1)

            pe.wait_ge(loaded["zT"], 16)
            pe.wait_ge(loaded["fw"], 48)
            tile_product(("F1",), slice(0, 64), [(fw1, zT)])
            pe.wait_ge(sin_done, 1)
            tile_product(("F2",), slice(0, 64), [(fw2, s1T)])
            pe.wait_ge(sin_done, 2)
            for t in range(TT):
                for d in range(2):
                    full(("F3", t, d), [(s2T[:, t * P:(t + 1) * P], fw3[:, d * HY:(d + 1) * HY])])
            pe.wait_ge(loaded["cst"], 16)
            pe.wait_ge(absum_ready, TT)
            claim("L1")
            for c in range(HC):
                mm = product(bank("L1")[:, c:c + 1], [(absum[:, t, c * P:(c + 1) * P], ones[:, 0:1]) for t in range(TT)])
            mm.then_inc(pe_done, 1)
            pe.wait_ge(loaded["dftf"], 16)
            for f in range(4):
                for r in range(2):
                    full(("G", f, r), [(dftf[:, r, t, f * P:(f + 1) * P], filt[:, t, r, :]) for t in range(TT)])
            for j in range(4):
                pe.wait_ge(ada_done, j + 1)
                claim("AC", j)
                for c in range(4):
                    mm = product(bank("AC", j)[:, c:c + 1], [(adasum[:, j % 2, c * P:(c + 1) * P], ones[:, 0:1])])
                mm.then_inc(pe_done, 1)
            pe.wait_ge(x_scaled, 1)
            for c in range(DC):
                turn(("XT", c), [xin[:, t, c * P:(c + 1) * P] for t in range(TT)])
            taken(pe, "XT", DC - 1)
            for m in range(3 * HC):
                arrived(pe, "hy", m // 4)
                full(("H", m), [(w8[("hy", m // 4)][:, c, (m % 4) * P:(m % 4 + 1) * P], hT[:, c, :]) for c in range(DC)])
            pe.wait_ge(u_ready, HC)
            for t in range(TT):
                turn(("UT", t), [uT[:, c, t * P:(t + 1) * P] for c in range(HC)])
            taken(pe, "UT", TT - 1)
            for f in range(4):
                for r in range(2):
                    full(("UF", f, r), [(dftf[:, r, t, f * P:(f + 1) * P], uTok[:, t, :]) for t in range(TT)])

            def ada_row(j):
                pe.wait_ge(ada_done, j + 1)
                full(("AB", j), [(ones, adasum[:, j % 2, :])])
            ada_row(4), ada_row(5)
            arrived(pe, "dft")
            pe.wait_ge(spec_ready, 4)
            for c in range(HC):
                full(("YI", c), [(spec[:, f, r, c * P:(c + 1) * P], dfti[:, r, f, :]) for f in range(4) for r in range(2)])
            arrived(pe, "cq")
            for m in range(QC):
                full(("CQ", m), [(wcq[:, c, m * P:(m + 1) * P], hT[:, c, :]) for c in range(DC)])
            arrived(pe, "ckv")
            for m in range(KC):
                full(("CK", m), [(wckv[:, c, m * P:(m + 1) * P], hT[:, c, :]) for c in range(DC)])
            tile_product(("KR",), slice(NOPE, QKD), [(wckv[:, c, KVL:KVL + ROPE], hT[:, c, :]) for c in range(DC)])
            pe.wait_ge(rotw_ready, 1)
            tile_product(("KT",), slice(NOPE, QKD), [(wkrot[:, c, :], hT[:, c, :]) for c in range(DC)])
            pe.wait_ge(sq_ready, QC)
            full(("QS",), [(ones, sqT[:, m, :]) for m in range(QC)])
            pe.wait_ge(sq_ready, QC + KC)
            full(("KS",), [(ones, rt[:, m, :]) for m in range(KC)])
            ada_row(6), ada_row(7)
            arrived(pe, "uquk")
            pe.wait_ge(latent_ready, QC)
            for i in range(4):
                full(("QN", i), [(wuqn[:, c, 2 * i:2 * i + 2, :], cqT[:, c, :]) for c in range(QC)])
            pe.wait_ge(rotw_ready, 2)
            for g in range(2):
                full(("QR", g), [(wuqr[:, c, 4 * g:4 * g + 4, :], cqT[:, c, :]) for c in range(QC)])
                full(("QT", g), [(wrot[:, c, 4 * g:4 * g + 4, :], cqT[:, c, :]) for c in range(QC)])
            pe.wait_ge(latent_ready, QC + KC)
            for i in range(4):
                full(("KN", i), [(wuk[:, c, i * P:(i + 1) * P], ckvT[:, c, :]) for c in range(KC)])
            arrived(pe, "uv")
            for t in range(TT):
                full(("V", t), [(ckvT[:, c, t * P:(t + 1) * P], wuv[:, c, :]) for c in range(KC)])
            taken(pe, "KN", 3)
            pe.wait_ge(q_rope, NH)
            pe.wait_ge(kr_copied, NH)
            taken(pe, "V", TT - 1)
            for n in range(NA + LAG):
                if n < NA:
                    h, t = n // TT, n % TT
                    full(("S", n), [(qh[0:QKD, h, t * P:(t + 1) * P], kh[0:QKD, h, :])])
                if n in AB_AT:
                    ada_row(AB_AT[n])
                if n >= LAG:
                    m = n - LAG
                    h, o = m // TT, VH * (m // TT % 2)
                    pe.wait_ge(prob_done, m + 1)
                    turn(("T", m), [prob[:, m % 3, k * P:(k + 1) * P] for k in range(TT)])
                    taken(pe, "T", m)
                    claim("O", m)
                    product(bank("O", m)[o:o + VH, 0:P], [(v_sb[:, k, h * VH:(h + 1) * VH], pT[:, m % 2, k * P:(k + 1) * P])
                                                          for k in range(TT)]).then_inc(pe_done, 1)
            for d in range(DC):
                for g, k in enumerate(("GA", "GB")):
                    arrived(pe, "g", g, d // 4)
                    full((k, d), [(w8[("g", g, d // 4)][:, c, (d % 4) * P:(d % 4 + 1) * P], hT[:, c, :]) for c in range(DC)])
                if d == 0:
                    arrived(pe, "whyo")
                    arrived(pe, "wmlao")
                    taken(pe, "O", NA - 1)
                full(("MA", d), [(whyo[:, c, d * P:(d + 1) * P], yhy[:, c, :]) for c in range(HC)])
                full(("MB", d), [(wmlao[:, c, d * P:(d + 1) * P], ymla[:, c, :]) for c in range(HC)])
            pe.wait_ge(mix_done, DC)
            for hf in range(2):
                arrived(pe, "mix", hf)
                for t in range(TT):
                    full(("W", hf, t), [(mixT[:, c, t * P:(t + 1) * P], w8[("mix", hf)][:, c, :]) for c in range(DC)])
            pe.wait_ge(h2_done, TT)
            for c in range(DC):
                turn(("HT", c), [h2[:, t, c * P:(c + 1) * P] for t in range(TT)])
            taken(pe, "HT", DC - 1)
            pe.wait_ge(loaded["router"], 64)
            claim("LG")
            for t in range(TT):
                mm = product(bank("LG")[:, t * 36:(t + 1) * 36], [(h2T[:, c, t * P:(t + 1) * P], wr[:, c, :]) for c in range(DC)]
                             + [(ones[0:1, :], brow)])
            mm.then_inc(pe_done, 1)
            pe.wait_ge(onehots, 1)
            claim("RK")
            for t in range(TT):
                product(bank("RK")[:, t * NE:(t + 1) * NE], [(lower, ohs[:, t, :])] + [(ones, ohs[:, j, :]) for j in range(t)])
            product(bank("RK")[:, TT * NE:(TT + 1) * NE], [(ones, ohs[:, j, :]) for j in range(TT)]).then_inc(pe_done, 1)
            pe.wait_ge(slots_ready, 1)
            claim("IX")
            product(bank("IX")[0:BLK, 0:NE], [(Rm[:, k, t, :], ohv[:, k, t, :]) for k in range(2) for t in range(TT)]
                    ).then_inc(pe_done, 1)

            def turn_rows(s, sem_):
                v = hg[0:BLK, s % 2, :].rearrange("s (p c) -> s c p", c=DC)
                for c in range(DC):
                    mm = nc.tensor.transpose(banks[c // 4][:, (c % 4) * BLK:(c % 4 + 1) * BLK], v[:, c, :], ident[0:BLK, 0:BLK])
                mm.then_inc(sem_, 1)

            def gate_up(w, s, b, sem_):
                for g in range(4):
                    m = (wg_s, wu_s)[g // 2][w]
                    mm = product(banks[2 + b][:, g * BLK:(g + 1) * BLK],
                                 [(m[:, c, (g % 2) * P:(g % 2 + 1) * P], hgT[:, s % 2, c, :]) for c in range(DC)])
                mm.then_inc(sem_, 1)

            def down(w, s, b, sem_):
                for hf in range(2):
                    mm = product(banks[4 + 2 * b + hf][0:BLK, :],
                                 [(aT[:, s % 2, f * BLK:(f + 1) * BLK], wd_s[w][:, f, hf * 512:(hf + 1) * 512]) for f in range(2)])
                mm.then_inc(sem_, 1)

            def turn_expert(e, s, i):
                pe.wait_ge(rows_in[s % 2], i * 32 + 16 * (s // 2) + 16)
                if not (isinstance(e, int) and e == 0):
                    pe.wait_ge(turned_act, e)
                    pe.wait_ge(turned_dve, e)
                turn_rows(s, turned)

            def gate_up_expert(e, s, i):
                pe.wait_ge(turned_act, e + 1)
                pe.wait_ge(turned_dve, e + 1)
                pe.wait_ge(gu_in[s], i * 32 + 32)
                if not (isinstance(e, int) and e < 2):
                    pe.wait_ge(a_done, e - 1)
                gate_up(s, s, s % 2, gu_done)

            def down_expert(e, s, i):
                pe.wait_ge(a_done, e + 1)
                pe.wait_ge(dn_in[s], i * 16 + 16)
                if not (isinstance(e, int) and e < 2):
                    pe.wait_ge(y_act, e - 1)
                    pe.wait_ge(y_dve, e - 1)
                down(s, s, s % 2, y_done)

            def four(i, first=False, last=False):
                for s in range(EXPERT_SLOTS):
                    e = i * EXPERT_SLOTS + s
                    gate_up_expert(e, s, i)
                    if not (first and s == 0):
                        down_expert(e - 1, (s - 1) % 4, i - 1 if s == 0 else i)
                    if not (last and s == EXPERT_SLOTS - 1):
                        turn_expert(e + 1, (s + 1) % 4, i + 1 if s == 3 else i)
            taken(pe, "IX")
            turn_expert(0, 0, 0)
            four(0, first=True)
            with pe.Fori(1, NE // EXPERT_SLOTS - 1) as i:
                four(i)
            four(NE // EXPERT_SLOTS - 1, last=True)
            down_expert(NE - 1, 3, NE // EXPERT_SLOTS - 1)
            with pe.If(over_flag(pe) > 0):
                with pe.Fori(0, NBLK - 1) as b:
                    pe.wait_ge(o_slots, b + 1)
                    product(banks[7][0:BLK, 0:NE], [(Rm[:, k, t, :], ohv[:, k, t, :]) for k in range(2) for t in range(TT)]
                            ).then_inc(o_tok, 1)
                    with pe.Fori(0, NE) as e:
                        n = b * NE + e
                        pe.wait_ge(o_rows, n * 16 + 16)
                        turn_rows(0, o_turned)
                        pe.wait_ge(o_read, n + 1)
                        pe.wait_ge(o_w, n * 48 + 48)
                        gate_up(0, 0, 0, o_gu)
                        pe.wait_ge(o_hidden, n + 1)
                        down(0, 0, 0, o_y)

        @block.vector
        def _(dve):
            V = nc.vector
            step = [0]

            def link(ins):
                step[0] += 1
                ins.then_inc(dve_step, 1)
                dve.wait_ge(dve_step, step[0])

            def read(ins):
                ins.then_inc(read_sem["dve"], 1)

            link(V.memset(adab[:, :, :], 0.0))
            V.memset(over, 0.0).then_inc(bias_clear, 1)
            dve.wait_ge(loaded["fb"], 64)
            for n, (b, f) in enumerate(((fb1, ff1), (fb2, ff2))):
                k = (f"F{n + 1}",)
                ready(dve, *k)
                if n:
                    dve.wait_ge(sin_done, n)
                ins = V.tensor_scalar(argT, bank(*k)[0:64, :], b, f, ALU.add, ALU.mult)
                read(ins)
                taken(dve, *k)
                link(V.tensor_scalar(rndT, argT, 1.0 / TWO_PI, ROUND, ALU.mult, ALU.add))
                link(V.tensor_scalar(rndT, rndT, ROUND, None, ALU.subtract))
                link(V.scalar_tensor_tensor(out=argT, in0=rndT, scalar=-PI2_HI, in1=argT, op0=ALU.mult, op1=ALU.add))
                link(V.scalar_tensor_tensor(out=argT, in0=rndT, scalar=-PI2_LO, in1=argT, op0=ALU.mult, op1=ALU.add))
                V.tensor_scalar(argT, argT, -3.1415925, 3.1415925, ALU.max, ALU.min).then_inc(sin_arg, 1)

            def ada(j):
                if j == 0:
                    dve.wait_ge(cact_done, 1)
                arrived(dve, "ada", j)
                dve.wait_ge(bias_in[j % 2], 16 * (j // 2 + 1))
                if j >= 2:
                    ready(dve, "AC" if j < 6 else "AB", j - 2)
                for c in range(DC):
                    ins = V.scalar_tensor_tensor(out=adasum[:, j % 2, :], in0=w8[("ada", j)][:, c, :], scalar=cact[:, c:c + 1],
                                                 in1=adab[:, j % 2, :] if c == 0 else adasum[:, j % 2, :], op0=ALU.mult, op1=ALU.add)
                    if c < DC - 1:
                        link(ins)
                ins.then_inc(ada_done, 1)

            dve.wait_ge(loaded["window"], 16)
            dve.wait_ge(sin_done, 2)
            for t in range(TT):
                for d in range(2):
                    ready(dve, "F3", t, d)
                    read(V.tensor_tensor(filt[:, t, d, :], bank("F3", t, d)[:, :], window[:, t, :], ALU.mult))
                taken(dve, "F3", t, 1)
                if t == 0:
                    link(V.memset(filt[0:1, 0, 1, :], 0.0))
                V.tensor_tensor(absum[:, t, :], filt[:, t, 0, :], filt[:, t, 1, :], ALU.add)
                link(V.tensor_tensor(filt[:, t, 1, :], filt[:, t, 0, :], filt[:, t, 1, :], ALU.subtract))
                link(V.tensor_copy(filt[:, t, 0, :], absum[:, t, :]))
                fs, fd = filt[:, t, 0, :], filt[:, t, 1, :]
                link(V.scalar_tensor_tensor(out=absum[:, t, :], in0=fs, scalar=-1.0, in1=fs, op0=ALU.mult, op1=ALU.max))
                link(V.scalar_tensor_tensor(out=absum[:, t, :], in0=fd, scalar=-1.0, in1=absum[:, t, :], op0=ALU.mult, op1=ALU.max))
                V.tensor_tensor(absum[:, t, :], absum[:, t, :], fd, ALU.max).then_inc(absum_ready, 1)
            ada(0)
            ada(1)
            ready(dve, "L1")
            read(V.reciprocal(invl1, bank("L1")[:, 0:HC]))
            dve.wait_ge(x_sumsq, TT)
            V.tensor_scalar(rstd, ss, 1.0 / D, EPS, ALU.mult, ALU.add).then_inc(sqrt_arg, 1)
            dve.wait_ge(sqrt_done, 1)
            link(V.reciprocal(rstd, srt))
            for t in range(TT):
                ins = V.tensor_scalar(xin[:, t, :], xin[:, t, :], rstd[:, t:t + 1], None, ALU.mult)
            ins.then_inc(x_scaled, 1)
            ada(2)
            ada(3)
            taken(dve, "AC", 3)
            dve.wait_ge(loaded["g1col"], 16)
            V.scalar_tensor_tensor(out=a1col, in0=modcol[:, 8:16], scalar=1.0, in1=g1col, op0=ALU.add, op1=ALU.mult
                                   ).then_inc(a1_ready, 1)
            for m in range(3 * HC):
                dve.wait_ge(conv_centre, m + 1)
                dst = x0T[:, m, :] if m < HC else x1T[:, m - HC, :] if m < 2 * HC else cvt[:, m % 2, :]
                b = bank("H", m)
                link(V.scalar_tensor_tensor(out=dst[:, 1:L], in0=b[:, 0:L - 1], scalar=convw[:, 0, m:m + 1],
                                            in1=dst[:, 1:L], op0=ALU.mult, op1=ALU.add))
                read(V.scalar_tensor_tensor(out=dst[:, 0:L - 1], in0=b[:, 1:L], scalar=convw[:, 2, m:m + 1],
                                            in1=dst[:, 0:L - 1], op0=ALU.mult, op1=ALU.add))
                if m >= 2 * HC:
                    taken(dve, "H", m)
                    V.tensor_tensor(uT[:, m - 2 * HC, :], dst, x1T[:, m - 2 * HC, :], ALU.mult).then_inc(u_ready, 1)
            ada(4)
            ada(5)
            taken(dve, "G", 3, 1)
            for f in range(4):
                ready(dve, "UF", f, 1)
                if f:
                    dve.wait_ge(spec_ready, f)
                ur, ui, gr, gi = bank("UF", f, 0)[:, :], bank("UF", f, 1)[:, :], G[:, f, 0, :], G[:, f, 1, :]
                V.tensor_tensor(cm[:, 0, :], ur, gr, ALU.mult)
                V.tensor_tensor(cm[:, 1, :], ui, gi, ALU.mult)
                read(V.tensor_tensor(cm[:, 2, :], ur, gi, ALU.mult))
                read(V.tensor_tensor(cm[:, 3, :], ui, gr, ALU.mult))
                taken(dve, "UF", f, 1)
                V.tensor_tensor(spec[:, f, 0, :], cm[:, 0, :], cm[:, 1, :], ALU.subtract)
                V.tensor_tensor(spec[:, f, 1, :], cm[:, 2, :], cm[:, 3, :], ALU.add).then_inc(spec_ready, 1)
            dve.wait_ge(loaded["hyb"], 16)
            for c in range(HC):
                ready(dve, "YI", c)
                read(V.tensor_scalar(cm[:, c, :], bank("YI", c)[:, :], invl1[:, c:c + 1], None, ALU.mult))
                taken(dve, "YI", c)
                link(V.scalar_tensor_tensor(out=cm[:, c, :], in0=uT[:, c, :], scalar=hybias[:, c:c + 1], in1=cm[:, c, :],
                                            op0=ALU.mult, op1=ALU.add))
                V.tensor_tensor(yhy[:, c, :], cm[:, c, :], x0T[:, c, :], ALU.mult).then_inc(yhy_ready, 1)
            H2 = ROPE // 2
            dve.wait_ge(yhy_ready, HC)
            arrived(dve, "ckv")
            V.tensor_scalar(wkrot[:, :, 0:H2], wckv[:, :, KVL + H2:KVL + ROPE], -1.0, None, ALU.mult)
            V.tensor_copy(wkrot[:, :, H2:ROPE], wckv[:, :, KVL:KVL + H2]).then_inc(rotw_ready, 1)
            dve.wait_ge(loaded["rope"], 16)
            ready(dve, "KR")
            read(V.tensor_tensor(krope[NOPE:QKD, :], bank("KR")[NOPE:QKD, :], rope[NOPE:QKD, 0, :], ALU.mult))
            ready(dve, "KT")
            read(V.tensor_tensor(ktmp[NOPE:QKD, :], bank("KT")[NOPE:QKD, :],
                                 rope[NOPE:QKD, 1, :], ALU.mult))
            taken(dve, "KT")
            V.tensor_tensor(krope[NOPE:QKD, :], krope[NOPE:QKD, :], ktmp[NOPE:QKD, :], ALU.add).then_inc(kr_done, 1)
            dve.wait_ge(loaded["gqk"], 32)
            for n, (k, width, tiles, lat, g) in enumerate((("QS", QL, QC, cqT, gq), ("KS", KVL, KC, ckvT, gkv))):
                ready(dve, k)
                ins = V.tensor_scalar(rb, bank(k)[:, :], 1.0 / width, EPS, ALU.mult, ALU.add)
                read(ins)
                taken(dve, k)
                dve.engine_nop().then_inc(sqrt_arg, 1)
                dve.wait_ge(sqrt_done, 2 + n)
                link(V.reciprocal(rb, rb))
                taken(dve, "CK", KC - 1)
                for m in range(tiles):
                    V.scalar_tensor_tensor(out=lat[:, m, :], in0=lat[:, m, :], scalar=g[:, m:m + 1], in1=rb,
                                           op0=ALU.mult, op1=ALU.mult).then_inc(latent_ready, 1)
                if n == 0:
                    dve.wait_ge(latent_ready, QC)
            arrived(dve, "uquk")
            for c in range(QC):
                V.tensor_scalar(wrot[:, c, :, 0:H2], wuqr[:, c, :, H2:ROPE], -1.0, None, ALU.mult)
                ins = V.tensor_copy(wrot[:, c, :, H2:ROPE], wuqr[:, c, :, 0:H2])
            ins.then_inc(rotw_ready, 1)
            ada(6)
            ada(7)
            for g in range(2):
                ready(dve, "QR", g)
                if g:
                    dve.wait_ge(q_rope, 4)
                read(V.tensor_tensor(rt[:, 0, :], bank("QR", g)[:, :], rope[:, 0, :], ALU.mult))
                ready(dve, "QT", g)
                read(V.tensor_tensor(rt[:, 1, :], bank("QT", g)[:, :], rope[:, 1, :], ALU.mult))
                taken(dve, "QT", g)
                for j in range(4):
                    r = slice(ROPE * j, ROPE * (j + 1))
                    V.tensor_tensor(qh[NOPE:QKD, 4 * g + j, :], rt[r, 0, :], rt[r, 1, :], ALU.add).then_inc(q_rope, 1)

            def row_max(n):
                ready(dve, "S", n)
                if n >= 4:
                    taken(dve, "S", n - 4)
                link(V.reduce_max(rowmax[:, n % 4:n % 4 + 1], bank("S", n)[:, :], X))
                V.tensor_scalar(negmax[:, n % 4:n % 4 + 1], rowmax[:, n % 4:n % 4 + 1], -SCORE_SCALE, None, ALU.mult
                                ).then_inc(max_done, 1)

            def normalise(n):
                taken(dve, "S", n)
                link(V.reciprocal(rinv[:, n % 4:n % 4 + 1], rowsum[:, n % 4:n % 4 + 1]))
                V.tensor_scalar(prob[:, n % 3, :], prob[:, n % 3, :], rinv[:, n % 4:n % 4 + 1], None, ALU.mult
                                ).then_inc(prob_done, 1)

            def turned_probs(n):
                ready(dve, "T", n)
                if n >= 2:
                    ready(dve, "O", n - 2)
                read(V.tensor_copy(pT[:, n % 2, :], bank("T", n)[:, :]))

            for n in range(NA + LAG):
                if n < NA:
                    row_max(n)
                if n in AB_AT:
                    ada(AB_AT[n])
                if 1 <= n <= NA:
                    normalise(n - 1)
                if n >= LAG:
                    turned_probs(n - LAG)
            for d in range(DC):
                ga, gb = sg[:, 2 * d % 4, :], sg[:, (2 * d + 1) % 4, :]
                taken(dve, "GB", d)
                ready(dve, "MA", d)
                read(V.tensor_tensor(ga, bank("MA", d)[:, :], ga, ALU.mult))
                ready(dve, "MB", d)
                read(V.tensor_tensor(gb, bank("MB", d)[:, :], gb, ALU.mult))
                taken(dve, "MB", d)
                V.tensor_tensor(mixT[:, d, :], ga, gb, ALU.add).then_inc(mix_done, 1)
            taken(dve, "AB", 11)
            dve.wait_ge(loaded["x1"], 16)
            for hf in range(2):
                for t in range(TT):
                    n = hf * TT + t
                    ready(dve, "W", hf, t)
                    read(V.tensor_tensor(gated[:, n % 2, :], bank("W", hf, t)[:, :], bcast[:, hf * 512:(hf + 1) * 512], ALU.mult))
                    taken(dve, "W", hf, t)
                    r = x1[:, t, hf * 512:(hf + 1) * 512]
                    ins = V.tensor_tensor(r, r, gated[:, n % 2, :], ALU.add)
                    if hf:
                        ins.then_inc(x1_done, 1)
            dve.wait_ge(loaded["ffng"], 16)
            link(V.scalar_tensor_tensor(out=bcast[:, 2 * D:3 * D], in0=bcast[:, 2 * D:3 * D], scalar=1.0, in1=g2b,
                                        op0=ALU.add, op1=ALU.mult))
            dve.wait_ge(x1_sumsq, TT)
            V.tensor_scalar(rstd2, ss2, 1.0 / D, EPS, ALU.mult, ALU.add).then_inc(sqrt_arg, 1)
            dve.wait_ge(sqrt_done, 4)
            link(V.reciprocal(rstd2, srt2))
            for t in range(TT):
                link(V.scalar_tensor_tensor(out=h2[:, t, :], in0=x1[:, t, :], scalar=rstd2[:, t:t + 1], in1=bcast[:, 2 * D:3 * D],
                                            op0=ALU.mult, op1=ALU.mult))
                V.tensor_tensor(h2[:, t, :], h2[:, t, :], bcast[:, D:2 * D], ALU.add).then_inc(h2_done, 1)

            def wide(v, n):
                return v.unsqueeze(2).broadcast_to([P, TT, n])

            def const(at_, n):
                return cst[:, at_:at_ + n].unsqueeze(1).broadcast_to([P, TT, n])

            def first_max(vals, top, scratch, index, onehot, n, iota, iota_far):
                link(V.tensor_reduce(top, vals, X, ALU.max))
                link(V.tensor_tensor(scratch, vals, wide(top, n), ALU.is_ge))
                link(V.scalar_tensor_tensor(out=scratch, in0=scratch, scalar=-100.0, in1=const(iota_far, n),
                                            op0=ALU.mult, op1=ALU.add))
                link(V.tensor_reduce(index, scratch, X, ALU.min))
                link(V.tensor_tensor(onehot, const(iota, n), wide(index, n), ALU.is_equal))

            ready(dve, "LG")
            read(V.tensor_copy(lg, bank("LG")[:, 0:144].rearrange("p (t n) -> p t n", t=TT)))
            taken(dve, "LG")
            first_max(lg[:, :, 0:NG], gmax, geq, i0, gm, NG, C_I4, C_I4B)
            V.tensor_tensor(gs, lg[:, :, 0:NG], wide(gmax, NG), ALU.subtract).then_inc(gexp, 1)
            link(V.tensor_scalar(pen, gm, BIG, -BIG, ALU.mult, ALU.add))
            for t in range(TT):
                e3 = em[:, t, :].rearrange("p (g n) -> p g n", g=NG)
                link(V.tensor_tensor(e3, lg[:, t, NG:NG + NE].rearrange("p (g n) -> p g n", g=NG),
                                     gm[:, t, :].unsqueeze(2).broadcast_to([P, NG, EPG]), ALU.mult))
                link(V.tensor_tensor(e3, e3, pen[:, t, :].unsqueeze(2).broadcast_to([P, NG, EPG]), ALU.add))
            first_max(em, m1, eq, i1, oh1, NE, C_I32, C_I32B)
            link(V.scalar_tensor_tensor(out=em, in0=oh1, scalar=-BIG, in1=em, op0=ALU.mult, op1=ALU.add))
            first_max(em, m2, eq, i2, oh2, NE, C_I32, C_I32B)
            V.tensor_tensor(ohs, oh1, oh2, ALU.add).then_inc(onehots, 1)
            V.tensor_tensor(dv, m2, m1, ALU.subtract).then_inc(wexp, 1)
            dve.wait_ge(gexp_done, 1)
            link(V.tensor_reduce(gsum, gs, X, ALU.add))
            link(V.reciprocal(psel, gsum))
            dve.wait_ge(wexp_done, 1)
            link(V.tensor_scalar(w1c, ed, 1.0, None, ALU.add))
            link(V.reciprocal(w2c, w1c))
            link(V.tensor_tensor(w1c, w2c, psel, ALU.mult))
            link(V.tensor_tensor(w2c, w1c, ed, ALU.mult))
            link(V.tensor_tensor(ohv[:, 0], oh1, wide(cst[:, C_TOK:C_TOK + TT], NE), ALU.mult))
            link(V.tensor_tensor(ohv[:, 1], oh2, wide(cst[:, C_TOK:C_TOK + TT], NE), ALU.mult))
            ready(dve, "RK")
            link(V.tensor_copy(cnt, bank("RK")[:, TT * NE:(TT + 1) * NE]))
            read(V.tensor_copy(rk, bank("RK")[:, 0:TT * NE].rearrange("p (t n) -> p t n", t=TT)))
            taken(dve, "RK")
            for oh, r in ((oh1, r1), (oh2, r2)):
                link(V.tensor_tensor(eq, oh, rk, ALU.mult))
                link(V.tensor_reduce(r, eq, X, ALU.add))

            def slot_onehots(sem_):
                for k in range(2):
                    for t in range(TT):
                        ins = V.tensor_scalar(Rm[:, k, t, :], cst[:, C_IB:C_IB + BLK], r12[:, k, t:t + 1], None, ALU.is_equal)
                ins.then_inc(sem_, 1)
            slot_onehots(slots_ready)
            link(V.tensor_reduce(over, cnt, X, ALU.max))
            link(V.tensor_scalar(over, over, float(BLK), None, ALU.is_gt))
            V.tensor_copy(overu, over).then_inc(over_ready, 1)
            ready(dve, "IX")
            read(V.tensor_copy(idxu, bank("IX")[0:BLK, 0:NE]))
            taken(dve, "IX")
            dve.engine_nop().then_inc(idx_ready, 1)
            for k, (i_, r, w) in enumerate(((i1, r1, w1c), (i2, r2, w2c))):
                link(V.tensor_scalar(rankf, r, float(BLK), None, ALU.is_lt))
                link(V.tensor_tensor(wfirst[:, k, :], w, rankf, ALU.mult))
                link(V.tensor_tensor(wmore[:, k, :], w, wfirst[:, k, :], ALU.subtract))
                link(V.tensor_scalar(rankf, r, float(BLK - 1), None, ALU.min))
                link(V.scalar_tensor_tensor(out=rowf, in0=i_, scalar=float(BLK), in1=rankf, op0=ALU.mult, op1=ALU.add))
                link(V.tensor_copy(yrow[:, k, :], rowf))
                link(V.tensor_scalar(rankf, r, float(BLK), 0.0, ALU.subtract, ALU.max))
                link(V.scalar_tensor_tensor(out=rowf, in0=i_, scalar=float(MORE), in1=rankf, op0=ALU.mult, op1=ALU.add))
                link(V.tensor_copy(morerow[:, k, :], rowf))
            dve.engine_nop().then_inc(rows_known, 1)

            def turned_rows(e, s):
                dve.wait_ge(turned, e + 1)
                if not (isinstance(e, int) and e < 2):
                    dve.wait_ge(gu_done, e - 1)
                V.tensor_copy(hgT[:, s % 2, 4:8, :], banks[1][:, 0:4 * BLK].rearrange("p (c s) -> p c s", c=4)).then_inc(turned_dve, 1)

            def hidden(e, s):
                dve.wait_ge(silu_done, e + 1)
                if not (isinstance(e, int) and e < 2):
                    dve.wait_ge(y_done, e - 1)
                V.tensor_tensor(aT[:, s % 2, :], banks[2 + s % 2][:, 2 * BLK:4 * BLK], sgl[:, s % 2, :], ALU.mult).then_inc(a_done, 1)

            def y_half(e, s, i):
                dve.wait_ge(y_done, e + 1)
                if not (isinstance(e, int) and e < 2):
                    dve.wait_ge(y_out[s % 2], i * 32 + 16 * (s // 2))
                V.tensor_copy(yb[0:BLK, s % 2, 512:D], banks[5 + 2 * (s % 2)][0:BLK, :]).then_inc(y_dve, 1)

            def four(i, first=False, last=False):
                for s in range(EXPERT_SLOTS):
                    e = i * EXPERT_SLOTS + s
                    hidden(e, s)
                    if not (first and s == 0):
                        y_half(e - 1, (s - 1) % 4, i - 1 if s == 0 else i)
                    if not (last and s == EXPERT_SLOTS - 1):
                        turned_rows(e + 1, s + 1)
            turned_rows(0, 0)
            four(0, first=True)
            with dve.Fori(1, NE // EXPERT_SLOTS - 1) as i:
                four(i)
            four(NE // EXPERT_SLOTS - 1, last=True)
            y_half(NE - 1, 3, NE // EXPERT_SLOTS - 1)
            with dve.If(over_flag(dve) > 0):
                for s in range(2):
                    dve.wait_ge(y_out[s], 16 * (NE // 2))
                V.memset(rankf, 0.0).then_inc(o_yread, 1)
                with dve.Fori(0, NBLK - 1) as b:
                    V.tensor_scalar(r12, r12, float(BLK), None, ALU.subtract).then_inc(o_rank, 1)
                    dve.wait_ge(o_rank, b + 1)
                    slot_onehots(o_slots)
                    dve.wait_ge(o_tok, b + 1)
                    V.tensor_copy(idxu, banks[7][0:BLK, 0:NE]).then_inc(o_idxu, 1)
                    dve.wait_ge(y_out[0], 16 * (NE // 2))
                    dve.wait_ge(o_idxu, b + 1)
                    with dve.Fori(0, NE) as e:
                        n = b * NE + e
                        V.tensor_copy(idxc[:, 0:1], idxu[:, bass.ds(e, 1)]).then_inc(o_idx, 1)
                        dve.wait_ge(o_turned, n + 1)
                        V.tensor_copy(hgT[:, 0, 0:4, :], banks[0][:, 0:4 * BLK].rearrange("p (c s) -> p c s", c=4))
                        V.tensor_copy(hgT[:, 0, 4:8, :], banks[1][:, 0:4 * BLK].rearrange("p (c s) -> p c s", c=4)).then_inc(o_read, 1)
                        dve.wait_ge(o_silu, n + 1)
                        V.tensor_tensor(aT[:, 0, :], banks[2][:, 2 * BLK:4 * BLK], sgl[:, 0, :], ALU.mult).then_inc(o_hidden, 1)
                        dve.wait_ge(o_y, n + 1)
                        V.tensor_copy(yb[0:BLK, 0, 0:512], banks[4][0:BLK, :])
                        V.tensor_copy(yb[0:BLK, 0, 512:D], banks[5][0:BLK, :]).then_inc(o_yread, 1)
                        dve.wait_ge(o_out, n * 16 + 16)
                for t in range(TT):
                    for k in range(2):
                        n = 2 * t + k
                        dve.wait_ge(o_back, 16 * n + 16)
                        V.scalar_tensor_tensor(out=yg[:, 0, :], in0=yg[:, 0, :], scalar=wmore[:, k, t:t + 1], in1=bcast[:, 3 * D:4 * D],
                                               op0=ALU.mult, op1=ALU.mult).then_inc(o_scaled, 1)
                        dve.wait_ge(o_scaled, n + 1)
                        V.tensor_tensor(x1[:, t, :], x1[:, t, :], yg[:, 0, :], ALU.add).then_inc(o_added, 1)
                dve.wait_ge(o_added, 2 * TT)
            dve.wait_ge(loaded["fing"], 16)
            for t in range(TT):
                a_, b_ = yg[:, 2 * t % 4, :], yg[:, (2 * t + 1) % 4, :]
                dve.wait_ge(back_in[2 * t % 4], 16 * (t // 2 + 1))
                link(V.tensor_scalar(a_, a_, wfirst[:, 0, t:t + 1], None, ALU.mult))
                dve.wait_ge(back_in[(2 * t + 1) % 4], 16 * (t // 2 + 1))
                link(V.scalar_tensor_tensor(out=a_, in0=b_, scalar=wfirst[:, 1, t:t + 1], in1=a_, op0=ALU.mult, op1=ALU.add))
                link(V.tensor_tensor(a_, a_, bcast[:, 3 * D:4 * D], ALU.mult))
                V.tensor_tensor(x1[:, t, :], x1[:, t, :], a_, ALU.add).then_inc(x2_done, 1)
                dve.wait_ge(x2_sumsq, t + 1)
                V.tensor_scalar(rstd3[:, t:t + 1], ss3[:, t:t + 1], 1.0 / D, EPS, ALU.mult, ALU.add).then_inc(sqrt3_arg, 1)
                dve.wait_ge(sqrt3_done, t + 1)
                link(V.reciprocal(rstd3[:, t:t + 1], srt3[:, t:t + 1]))
                if t >= 2:
                    dve.wait_ge(out_done[t % 2], 16 * (t // 2))
                V.scalar_tensor_tensor(out=outb[:, t % 2, :], in0=x1[:, t, :], scalar=rstd3[:, t:t + 1], in1=fgb,
                                       op0=ALU.mult, op1=ALU.mult).then_inc(out_ready, 1)


_INPUTS = ("x c ada_w ada_b norm_mix_g w_in hy_conv_w hy_conv_b filt_w1 filt_b1 filt_freq1 filt_w2 filt_b2 filt_freq2 "
           "filt_w3 hy_bias q_norm_g kv_norm_g w_uq w_uk w_uv w_hy_out w_mla_out w_mix_out norm_ffn_g w_group b_group "
           "w_router b_router w_gate w_up w_down final_norm_g").split()


def shape_constants():
    import numpy as np
    f32 = np.float32
    cst = np.zeros((P, C_END), f32)
    cst[:, C_ID:C_ID + P] = np.eye(P)
    cst[:, C_ONE:C_ONE + P] = 1.0
    cst[:, C_LT:C_LT + P] = np.arange(P)[:, None] < np.arange(P)[None, :]
    cst[:, C_I32:C_I32 + NE] = np.arange(NE)
    cst[:, C_I32B:C_I32B + NE] = np.arange(NE) + 100
    cst[:, C_IB:C_IB + BLK] = np.arange(BLK)
    cst[:, C_TOK:C_TOK + TT] = np.arange(P)[:, None] + P * np.arange(TT)[None, :]
    cst[:, C_I4:C_I4 + NG] = np.arange(NG)
    cst[:, C_I4B:C_I4B + NG] = np.arange(NG) + 100
    t = np.linspace(0.0, 1.0, L, dtype=f32)[:, None]
    pos = np.arange(L, dtype=f32)[:, None]
    bands = np.linspace(1e-4, 15, 16, dtype=f32)[None, :]
    ang = (f32(2.0 * math.pi) * bands * pos) / f32(L)
    z = np.concatenate([t, np.cos(ang), -np.sin(ang)], axis=1).astype(f32)
    lo, hi = math.log(1e-2) / 1.5, math.log(1e-2) / 0.3
    deltas = np.linspace(lo, hi, HY, dtype=f32)
    window = (np.exp(-t * np.abs(deltas)[None, :]) + f32(0.05)).astype(f32)
    theta = 2.0 * np.pi * (np.arange(L)[None, :] + 0.5) * np.arange(L)[:, None] / (2 * L)
    fwd = np.stack([np.cos(theta), -np.sin(theta)])
    inv = np.stack([np.cos(theta).T, -np.sin(theta).T]) / L

    def rows_to_partitions(m):
        return np.ascontiguousarray(m.reshape(2, 4, P, L).transpose(2, 0, 1, 3).reshape(P, 8 * L).astype(f32))
    rinv = f32(10000.0) ** (-np.arange(0, ROPE, 2, dtype=f32) / f32(ROPE))
    ra = np.arange(L, dtype=f32)[:, None] * rinv[None, :].astype(f32)
    rope = np.stack([np.tile(np.cos(ra).T, (8, 1)), np.tile(np.sin(ra).T, (8, 1))], axis=1).astype(f32)
    return {"cst": cst, "zT": np.ascontiguousarray(z.T), "window": window, "dftf": rows_to_partitions(fwd),
            "dfti": rows_to_partitions(inv), "rope": np.ascontiguousarray(rope)}


def kernel(**inputs):
    import numpy as np
    import concourse.bacc as bacc
    from concourse.bass_utils import run_bass_kernel_spmd

    nc = bacc.Bacc("TRN2", target_bir_lowering=False, num_devices=1)
    arrays, args = {}, {}
    given = {n: np.ascontiguousarray(inputs[n]) for n in _INPUTS}
    given.update(shape_constants())
    for n, v in given.items():
        arrays["in_" + n] = v
        args[n] = nc.dram_tensor("in_" + n, v.shape, mybir.dt.from_np(v.dtype), kind="ExternalInput").ap()
    out = nc.dram_tensor("out_0", (1, L, D), F32, kind="ExternalOutput").ap()
    h2_dram = nc.dram_tensor("h2_rows", (L, D), F32, kind="Internal").ap()
    y_dram = nc.dram_tensor("expert_rows", (NE, BLK, D), F32, kind="Internal").ap()
    y_more = nc.dram_tensor("expert_rows_more", (NE, MORE, D), F32, kind="Internal").ap()
    block_kernel(nc, args, out, h2_dram, y_dram, y_more)
    r = run_bass_kernel_spmd(nc, [arrays], core_ids=[0])
    return r.results[0]["out_0"]
```

```python
import math
from contextlib import ExitStack

import concourse.bass as bass
from concourse import mybir

F32 = mybir.dt.float32
U32 = mybir.dt.uint32
I32 = mybir.dt.int32
ALU = mybir.AluOpType
ACT = mybir.ActivationFunctionType
X = mybir.AxisListType.X

P = 128
L = 512
TT = L // P
D = 1024
DC = D // P
HY = 512
HC = HY // P
NH, NOPE, ROPE, VH = 8, 64, 32, 64
QKD = NOPE + ROPE
QL, KVL = 384, 256
QC, KC = QL // P, KVL // P
OFF_Q = 3 * HY
OFF_KV = OFF_Q + QL
OFF_KR = OFF_KV + KVL
OFF_GATE = OFF_KR + ROPE
EPS = 1e-6
NG, EPG = 4, 8
NE = NG * EPG
DE = 256
BLK = 80
NBLK = -(-L // BLK)
MORE = BLK * (NBLK - 1)
EXPERT_SLOTS = 4
BIG = 3.0e38
SCORE_SCALE = float(QKD) ** -0.5
TWO_PI = 2.0 * math.pi
ROUND = 1.5 * 2.0 ** 23
PI2_HI = 6.28125
PI2_LO = TWO_PI - PI2_HI

C_ID, C_ONE, C_LT, C_I32, C_I32B, C_IB, C_TOK, C_I4, C_I4B = 0, 128, 256, 384, 416, 448, 448 + BLK, 452 + BLK, 456 + BLK
C_END = 460 + BLK

RING = 5
CHUNK = 4096


def block_kernel(nc, a, out, h2_dram, y_dram, y_more):
    ctx = ExitStack()
    with ctx:
        def sb(name, cols, dt=F32):
            return ctx.enter_context(nc.sbuf_tensor(name, [P, cols], dt))

        def sem(name):
            return ctx.enter_context(nc.semaphore(name))

        cst = sb("cst", C_END)
        ring = sb("ring", RING * CHUNK)
        ht_mem = sb("ht_mem", DC * L)
        bcast = sb("bcast", 4 * D)
        AR = 84 * 256
        arena = sb("arena", AR)
        cols = sb("cols", 256)
        small = sb("small", 1024)
        smallu = sb("smallu", 256, U32)
        banks = [ctx.enter_context(nc.psum_tensor(f"bank{i}", [P, 512], F32)) for i in range(8)]

        ident, ones = cst[:, C_ID:C_ID + P], cst[:, C_ONE:C_ONE + P]
        lower = cst[:, C_LT:C_LT + P]

        def view(mem, at_, size_, **dims):
            v = mem[:, at_:at_ + size_]
            names = list(dims)
            return v.rearrange(f"p ({' '.join(names)}) -> p {' '.join(names)}", **{k: dims[k] for k in names[1:]})

        hT = view(ht_mem, 0, DC * L, c=DC, t=L)
        ccol, cact = cols[:, 0:8], cols[:, 8:16]
        modcol = cols[:, 16:32]
        g1col, a1col = cols[:, 32:40], cols[:, 40:48]
        convw = view(cols, 48, 36, w=3, c=12)
        convb = cols[:, 84:96]
        fb1, ff1, fb2, ff2 = (cols[0:64, 96 + i:97 + i] for i in range(4))
        hybias, invl1 = cols[:, 100:104], cols[:, 104:108]
        gq, gkv = cols[:, 108:111], cols[:, 111:113]
        ss, rstd, srt = cols[:, 116:120], cols[:, 120:124], cols[:, 124:128]
        ss2, rstd2, srt2 = cols[:, 128:132], cols[:, 132:136], cols[:, 136:140]
        ss3, rstd3, srt3 = cols[:, 140:144], cols[:, 144:148], cols[:, 148:152]
        rowmax, negmax, rowsum, rinv = (cols[:, 152 + 4 * i:156 + 4 * i] for i in range(4))
        cexp, cden, crec = cols[:, 168:176], cols[:, 176:184], cols[:, 184:192]

        K = 256
        filt = view(arena, 0, 16 * K, t=TT, d=2, c=HY)
        spec = view(arena, 0, 16 * K, f=4, r=2, c=HY)
        G = view(arena, 16 * K, 16 * K, f=4, r=2, c=HY)
        xin = view(arena, 32 * K, 16 * K, t=TT, d=D)
        x0T = view(arena, 32 * K, 8 * K, c=HC, t=L)
        uT = view(arena, 40 * K, 8 * K, c=HC, t=L)
        argT = arena[0:64, 48 * K:50 * K]
        rndT = arena[0:64, 50 * K:52 * K]
        fraw = view(arena, 16 * K, 16 * K, t=TT, d=2, c=HY)
        x1T = view(arena, 48 * K, 8 * K, c=HC, t=L)
        uTok = view(arena, 48 * K, 8 * K, t=TT, c=HY)
        window = view(arena, 56 * K, 8 * K, t=TT, c=HY)
        cm = view(arena, 56 * K, 8 * K, b=4, n=512)
        adasum = view(arena, 64 * K, 4 * K, b=2, n=512)
        adab = view(arena, 68 * K, 4 * K, b=2, n=512)
        zT = arena[0:33, 72 * K:74 * K]
        fw1 = arena[0:33, 74 * K:74 * K + 64]
        fw2 = arena[0:64, 74 * K + 64:74 * K + 128]
        fw3 = arena[0:64, 76 * K:80 * K]
        xsq = arena[:, 48 * K:52 * K]
        yhy = view(arena, 72 * K, 8 * K, c=HC, t=L)
        s1T = arena[0:64, 80 * K:82 * K]
        s2T = arena[0:64, 82 * K:84 * K]
        cvt = view(arena, 80 * K, 4 * K, b=2, t=512)
        dftf = view(bcast, 0, 16 * K, s=2, c=4, n=512)
        qh = view(arena, 0, 16 * K, h=NH, t=L)
        kh = view(arena, 16 * K, 16 * K, h=NH, t=L)
        cqT = view(arena, 32 * K, 6 * K, c=QC, t=L)
        ckvT = view(arena, 38 * K, 4 * K, c=KC, t=L)
        sqT = view(arena, 42 * K, 6 * K, b=3, t=L)
        rb = arena[:, 48 * K:50 * K]
        rope = view(arena, 50 * K, 4 * K, s=2, t=L)
        wrot = view(arena, 54 * K, 3 * K, c=QC, h=NH, n=ROPE)
        wkrot = view(arena, 57 * K, K, c=DC, n=ROPE)
        rt = view(arena, 58 * K, 4 * K, b=2, t=L)
        krope = arena[:, 62 * K:64 * K]
        ktmp = arena[:, 82 * K:84 * K]
        prob = view(arena, 32 * K, 8 * K, b=4, n=L)
        pT = view(arena, 42 * K, 4 * K, b=2, n=L)
        v_sb = view(arena, 48 * K, 8 * K, t=TT, n=NH * VH)
        ymla = view(arena, 56 * K, 8 * K, c=4, t=L)
        mixT = view(arena, 0, 16 * K, c=DC, t=L)
        x1 = view(arena, 16 * K, 16 * K, t=TT, d=D)
        sg = view(arena, 32 * K, 8 * K, b=4, n=512)
        x1sq = view(arena, 42 * K, 4 * K, b=2, n=512)
        gated = view(arena, 80 * K, 4 * K, b=2, n=512)
        h2T = view(arena, 0, 16 * K, c=DC, t=L)
        h2 = view(ht_mem, 0, 16 * K, t=TT, d=D)
        wr = view(arena, 32 * K, DC * (NG + NE), c=DC, n=NG + NE)
        brow = arena[0:1, 34 * K:34 * K + NG + NE]
        g2b = arena[:, 36 * K:40 * K]
        fgb = arena[:, 80 * K:84 * K]
        hg = view(arena, 0, 8 * K, b=2, d=D)
        hgT = view(arena, 8 * K, 2 * DC * BLK, b=2, c=DC, s=BLK)
        sgl = view(arena, 32 * K, 4 * BLK, b=2, n=2 * BLK)
        aT = view(arena, 32 * K + 4 * BLK, 4 * BLK, b=2, n=2 * BLK)
        yb = view(arena, 40 * K, 8 * K, b=2, d=D)
        emem = [(ring, 0), (arena, 48 * K), (ring, 24 * K), (ring, 48 * K)]
        wg_s = [view(m, o, 8 * K, c=DC, n=DE) for m, o in emem]
        wu_s = [view(m, o + 8 * K, 8 * K, c=DC, n=DE) for m, o in emem]
        wd_s = [view(m, o + 16 * K, 8 * K, c=2, n=D) for m, o in emem]
        yg = view(ht_mem, 0, 16 * K, b=4, d=D)
        outb = view(ring, 24 * K, 8 * K, b=2, d=D)
        osq = ring[:, 32 * K:36 * K]
        R0 = 72 * K
        lg = view(arena, R0, 144, t=TT, n=NG + NE)
        em = view(arena, R0 + 144, 128, t=TT, n=NE)
        eq = view(arena, R0 + 272, 128, t=TT, n=NE)
        oh1 = view(arena, R0 + 400, 128, t=TT, n=NE)
        oh2 = view(arena, R0 + 528, 128, t=TT, n=NE)
        ohs = view(arena, R0 + 656, 128, t=TT, n=NE)
        rk = view(arena, R0 + 784, 128, t=TT, n=NE)
        ohv = view(arena, R0 + 912, 256, k=2, t=TT, n=NE)
        Rm = view(arena, R0 + 1168, 8 * BLK, k=2, t=TT, s=BLK)
        (gmax, gsum, psel, i0, m1, m2, i1, i2, dv, ed, w1c, w2c, yc1, yc2, r1, r2) = (small[:, 4 * i:4 * i + 4] for i in range(16))
        r12 = view(small, 56, 8, k=2, t=TT)
        gs, gm, pen, geq = (view(small, 64 + 16 * i, 16, t=TT, n=NG) for i in range(4))
        cnt, over = small[:, 128:160], small[:, 160:161]
        idxu = smallu[0:BLK, 0:32]
        yrow = view(smallu, 32, 8, k=2, t=TT)
        morerow = view(smallu, 48, 8, k=2, t=TT)
        wfirst = view(small, 184, 8, k=2, t=TT)
        wmore = view(small, 192, 8, k=2, t=TT)
        rowf, rankf = small[:, 200:204], small[:, 204:208]
        idxc = smallu[0:BLK, 40:42]
        overu = smallu[:, 44:45]

        pe_done = sem("pe_unit_done")
        read_sem = {"act": sem("act_unit_read"), "dve": sem("dve_unit_read")}
        dve_step, act_step = sem("dve_step"), sem("act_step")
        ring_in = [sem(f"ring_in{i}") for i in range(RING)]
        bias_clear, bias_in, ada_done = sem("ada_bias_clear"), [sem(f"ada_bias_in{i}") for i in range(2)], sem("ada_sum_done")
        loaded = {n: sem("in_" + n) for n in
                  "cst c zT fw fb window dftf x g1col conv hyb gqk rope ffng router x1 fing".split()}
        cact_done, sin_arg, sin_done, filt_ready, absum_ready = (sem(n) for n in (
            "c_act", "sin_arg", "sin_done", "filter_ready", "filter_abs_ready"))
        x_rms = sem("x_rms")
        x_sumsq, x_scaled, a1_ready, sqrt_arg, sqrt_done = (sem(n) for n in (
            "x_sumsq", "x_scaled", "a1_ready", "sqrt_arg", "sqrt_done"))
        conv_centre, u_ready, spec_ready, yhy_ready = (sem(n) for n in (
            "conv_centre", "u_ready", "spectrum_ready", "y_hyena"))
        sq_ready, latent_ready, rotw_ready, kr_done, kr_copied, q_rope = (sem(n) for n in (
            "latent_square", "latent_normed", "rotated_weights", "k_rope", "k_rope_copied", "q_rope"))
        max_done, prob_done = sem("row_max"), sem("probs_normed")
        mix_done, x1_done, x1_sumsq, h2_done, h2_out = (sem(n) for n in (
            "mix_done", "x1_done", "x1_sumsq", "h2_done", "h2_written"))
        onehots, gexp, gexp_done, wexp, wexp_done, slots_ready, idx_ready, over_ready = (sem(n) for n in (
            "onehots", "g_shifted", "g_exp", "w_shifted", "w_exp", "slot_onehots", "slot_tokens", "overflow_known"))
        gu_in = [sem(f"gate_up_in{i}") for i in range(EXPERT_SLOTS)]
        dn_in = [sem(f"down_in{i}") for i in range(EXPERT_SLOTS)]
        rows_in = [sem(f"rows_in{i}") for i in range(2)]
        y_out = [sem(f"y_written{i}") for i in range(2)]
        turned, turned_act, gu_done, silu_done, a_done, y_done, y_dve = (sem(n) for n in (
            "rows_turned", "turned_read", "gate_up_done", "silu_done", "hidden_done",
            "expert_y_done", "y_read"))
        back_in = [sem(f"back_in{i}") for i in range(4)]
        x2_done, x2_sumsq, sqrt3_arg, sqrt3_done, out_ready = (sem(n) for n in (
            "x2_done", "x2_sumsq", "sqrt3_arg", "sqrt3_done", "out_ready"))
        out_done = [sem(f"out_written{i}") for i in range(2)]
        o_slots, o_tok, o_idx, o_rows, o_turned, o_read, o_gu, o_silu, o_hidden, o_y, o_yread, o_out, o_w = (
            sem("over_" + n) for n in ("slots", "tokens", "idx", "rows", "turned", "turned_read", "gate_up", "silu",
                                       "hidden", "y", "y_read", "y_out", "weights"))
        rows_known, o_back, o_added = sem("y_rows_known"), sem("over_back"), sem("over_added")
        o_carried = sem("over_carried")
        o_rank, o_idxu = sem("over_rank"), sem("over_slot_tokens")

        units = []

        def plan(reader, *keys):
            units.extend((k, reader) for k in keys)

        NA, LAG = NH * TT, 3
        plan("dve", ("F1",), ("F2",), *(("F3", t, d) for t in range(TT) for d in range(2)), ("L1",))
        plan("act", *(("G", f, r) for f in range(4) for r in range(2)), *(("AC", j) for j in range(4)),
             *(("XT", c) for c in range(DC)))
        plan("dve", *(("H", m) for m in range(3 * HC)))
        plan("act", *(("UT", t) for t in range(TT)))
        plan("dve", *(("UF", f, r) for f in range(4) for r in range(2)))
        plan("act", ("AB", 4), ("AB", 5))
        plan("dve", *(("YI", c) for c in range(HC)))
        plan("act", *(("CQ", m) for m in range(QC)), ("CK", 0))
        plan("dve", ("QS",))
        plan("act", ("CK", 1))
        plan("dve", ("KR",), ("KS",), ("KT",))
        plan("act", *(("QN", i) for i in range(4)))
        plan("dve", *((k, g) for g in range(2) for k in ("QR", "QT")))
        plan("act", *(("KN", i) for i in range(4)), *(("V", t) for t in range(TT)))
        AB_AT = {9: 6, 17: 7, 25: 8, 33: 9}
        AB_GATES = {3: 10, 6: 11}
        for n in range(NA + LAG + 1):
            if n < NA:
                plan("act", ("S", n))
            if n in AB_AT:
                plan("act", ("AB", AB_AT[n]))
            if n > LAG:
                plan("act", ("O", n - LAG - 1))
            if LAG <= n < NA + LAG:
                plan("act", ("T", n - LAG))
        for d in range(DC):
            plan("act", ("GA", d), ("GB", d))
            if d in AB_GATES:
                plan("act", ("AB", AB_GATES[d]))
            plan("dve", ("MA", d), ("MB", d))
        for t in range(TT):
            plan("dve", ("W", t, 0), ("W", t, 1))
            if t:
                plan("act", ("HT", t - 1, 0), ("HT", t - 1, 1))
        plan("act", ("HT", TT - 1, 0), ("HT", TT - 1, 1))
        plan("dve", ("LG",), ("RK",), ("IX",))
        number = {k: n for n, (k, _) in enumerate(units)}
        reader, nth, seen = dict(units), {}, {"act": 0, "dve": 0}
        for k, r in units:
            seen[r] += 1
            nth[k] = seen[r]

        def bank(*k):
            return banks[number[k] % 8]

        def claim(*k):
            n = number[k]
            if n >= 8:
                old = units[n - 8][0]
                nc.tensor.wait_ge(read_sem[reader[old]], nth[old])

        def ready(eng, *k):
            eng.wait_ge(pe_done, number[k] + 1)

        def taken(eng, *k):
            eng.wait_ge(read_sem[reader[k]], nth[k])

        w_in3 = a["w_in"][0].rearrange("(c p) n -> p c n", p=P)
        ada3 = a["ada_w"][0].rearrange("(c p) n -> p c n", p=P)
        mix3 = a["w_mix_out"][0].rearrange("(c p) n -> p c n", p=P)
        slot_of = {("ada", 0): 0, ("ada", 1): 1, ("ada", 2): 2, ("ada", 3): 3, ("hy", 0): 4, ("hy", 1): 0, ("hy", 2): 1,
                   ("ada", 4): 2, ("ada", 5): 3, ("dft",): 4, ("cq",): 0, ("ckv",): 1, ("uquk",): 2, ("uv",): 3,
                   ("ada", 6): 4, ("ada", 7): 0, ("ada", 8): 1, ("ada", 9): 2, ("g", 0, 0): 3, ("g", 1, 0): 4,
                   ("whyo",): 0, ("wmlao",): 1, ("ada", 10): 2, ("ada", 11): 2, ("g", 0, 1): 3, ("g", 1, 1): 4,
                   ("mix", 0): 2, ("mix", 1): 3}
        chunks = list(slot_of)
        place = {k: n for n, k in enumerate(chunks)}
        last_use = {("hy", 0): ("H", 3), ("hy", 1): ("H", 7), ("hy", 2): ("H", 11), ("dft",): ("YI", 3),
                    ("cq",): ("CQ", QC - 1), ("ckv",): ("KT",), ("uquk",): ("KN", 3), ("uv",): ("V", 3),
                    ("g", 0, 0): ("GA", 3), ("g", 1, 0): ("GB", 3), ("g", 0, 1): ("GA", 7)}

        def before(k):
            return [m for m in chunks[:place[k]] if slot_of[m] == slot_of[k]]

        def at(*k):
            return ring[:, slot_of[k] * CHUNK:(slot_of[k] + 1) * CHUNK]

        def arrived(eng, *k):
            eng.wait_ge(ring_in[slot_of[k]], 16 * sum(7 if m == ("uquk",) else 1 for m in before(k) + [k]))

        w8 = {k: at(*k).rearrange("p (c n) -> p c n", c=DC) for k in chunks if k[0] in ("ada", "hy", "g", "mix")}
        wcq = at("cq")[:, 0:DC * QL].rearrange("p (c n) -> p c n", c=DC)
        wckv = at("ckv")[:, 0:DC * (KVL + ROPE)].rearrange("p (c n) -> p c n", c=DC)
        dfti = at("dft").rearrange("p (s c n) -> p s c n", s=2, c=4)
        QN_COLS = QC * NH * NOPE
        wuqn = at("uquk")[:, 0:QN_COLS].rearrange("p (c h n) -> p c h n", c=QC, h=NH)
        wuqr = at("uquk")[:, QN_COLS:QC * NH * QKD].rearrange("p (c h n) -> p c h n", c=QC, h=NH)
        wuk = at("uquk")[:, QC * NH * QKD:QC * NH * QKD + KC * NH * NOPE].rearrange("p (c n) -> p c n", c=KC)
        wuv = at("uv")[:, 0:KC * NH * VH].rearrange("p (c n) -> p c n", c=KC)
        whyo = at("whyo").rearrange("p (c n) -> p c n", c=HC)
        wmlao = at("wmlao").rearrange("p (c n) -> p c n", c=HC)
        wg_d = a["w_gate"][0].rearrange("e (p c) n -> e p (c n)", c=DC)
        wu_d = a["w_up"][0].rearrange("e (p c) n -> e p (c n)", c=DC)
        wd_d = a["w_down"][0].rearrange("e (c p) n -> e p c n", p=P)
        y_flat = y_dram.rearrange("e s d -> (e s) d")
        more_flat = y_more.rearrange("e s d -> (e s) d")

        def entry(v, e):
            if isinstance(e, int):
                return v[e]
            v = v[bass.ds(e, 1)]
            return v.rearrange("o p n -> (o p) n") if len(v.shape) == 3 else v.rearrange("o p c n -> (o p) c n")

        def over_flag(eng):
            eng.wait_ge(over_ready, 1)
            return eng.value_load(overu[0:1, 0:1], min_val=0, max_val=1)

        block = ctx.enter_context(nc.Block())

        @block.sync
        def _(sp):
            def load_expert(e, s):
                sp.dma_start(wg_s[s].rearrange("p c n -> p (c n)"), entry(wg_d, e)).then_inc(gu_in[s], 16)
                sp.dma_start(wu_s[s].rearrange("p c n -> p (c n)"), entry(wu_d, e)).then_inc(gu_in[s], 16)
                sp.dma_start(wd_s[s], entry(wd_d, e)).then_inc(dn_in[s], 16)

            source = {("dft",): (at("dft"), a["dfti"]), ("cq",): (wcq, w_in3[:, :, OFF_Q:OFF_KV]),
                      ("ckv",): (wckv, w_in3[:, :, OFF_KV:OFF_GATE]),
                      ("uv",): (wuv, a["w_uv"][0].rearrange("(c p) h n -> p c (h n)", p=P)),
                      ("whyo",): (whyo, a["w_hy_out"][0].rearrange("(c p) n -> p c n", p=P)),
                      ("wmlao",): (wmlao, a["w_mla_out"][0].rearrange("(c p) n -> p c n", p=P)),
                      ("uquk",): (wuk, a["w_uk"][0].rearrange("(c p) h n -> p c (h n)", p=P))}
            for k in chunks:
                if k[0] == "ada":
                    source[k] = (w8[k], ada3[:, :, k[1] * 512:(k[1] + 1) * 512])
                elif k[0] == "hy":
                    source[k] = (w8[k], w_in3[:, :, k[1] * 512:(k[1] + 1) * 512])
                elif k[0] == "g":
                    o = OFF_GATE + k[1] * D + k[2] * 512
                    source[k] = (w8[k], w_in3[:, :, o:o + 512])
                elif k[0] == "mix":
                    source[k] = (w8[k], mix3[:, :, k[1] * 512:(k[1] + 1) * 512])
            sp.dma_start(zT, a["zT"]).then_inc(loaded["zT"], 16)
            sp.dma_start(fw1, a["filt_w1"][0]).then_inc(loaded["fw"], 16)
            sp.dma_start(fw2, a["filt_w2"][0]).then_inc(loaded["fw"], 16)
            sp.dma_start(fw3, a["filt_w3"][0]).then_inc(loaded["fw"], 16)
            for k in chunks:
                for old in before(k)[-1:]:
                    if old[0] == "ada":
                        sp.wait_ge(ada_done, old[1] + 1)
                    else:
                        ready(sp, *last_use[old])
                into = ring_in[slot_of[k]]
                sp.dma_start(*source[k]).then_inc(into, 16)
                if k == ("uquk",):
                    wuq_d = a["w_uq"][0].rearrange("(c p) (h n) -> c p h n", p=P, h=NH)
                    for c in range(QC):
                        sp.dma_start(wuqn[:, c], wuq_d[c, :, :, 0:NOPE]).then_inc(into, 16)
                        sp.dma_start(wuqr[:, c], wuq_d[c, :, :, NOPE:QKD]).then_inc(into, 16)
                if k[0] == "ada":
                    j = k[1]
                    if j >= 2:
                        sp.wait_ge(ada_done, j - 1)
                    else:
                        sp.wait_ge(bias_clear, 1)
                    sp.dma_start(adab[0:1, j % 2, :], a["ada_b"][0:1, j * 512:(j + 1) * 512]).then_inc(bias_in[j % 2], 16)
                if k == ("g", 1, 1):
                    taken(sp, "O", NA - 1)
                    sp.dma_start(x1, a["x"][0].rearrange("(t p) d -> p t d", p=P)).then_inc(loaded["x1"], 16)
            ready(sp, "MB", DC - 1)
            load_expert(0, 0)
            load_expert(1, 1)
            ready(sp, "W", TT - 1, 1)
            load_expert(2, 2)
            load_expert(3, 3)

            def write_rows(e, s):
                sp.wait_ge(y_dve, e + 1)
                sp.dma_start(entry(y_dram, e), yb[0:BLK, s % 2, :]).then_inc(y_out[s % 2], 16)

            with sp.Fori(0, NE // EXPERT_SLOTS - 1) as i:
                for s in range(EXPERT_SLOTS):
                    e = i * EXPERT_SLOTS + s
                    write_rows(e, s)
                    load_expert(e + EXPERT_SLOTS, s)
            for s in range(EXPERT_SLOTS):
                write_rows(NE - EXPERT_SLOTS + s, s)
            sp.dma_start(fgb, a["final_norm_g"].rearrange("(o n) -> o n", o=1).broadcast_to([P, D])).then_inc(loaded["fing"], 16)

            with sp.If(over_flag(sp) > 0):
                with sp.Fori(0, NBLK - 1) as b:
                    with sp.Fori(0, NE) as e:
                        n = b * NE + e
                        sp.wait_ge(o_yread, n + 1)
                        sp.dma_start(wg_s[0].rearrange("p c n -> p (c n)"), entry(wg_d, e)).then_inc(o_w, 16)
                        sp.dma_start(wu_s[0].rearrange("p c n -> p (c n)"), entry(wu_d, e)).then_inc(o_w, 16)
                        sp.dma_start(wd_s[0], entry(wd_d, e)).then_inc(o_w, 16)
                        sp.wait_ge(o_yread, n + 2)
                        sp.dma_start(more_flat[bass.ds(e * MORE + b * BLK, BLK), :], yb[0:BLK, 0, :]).then_inc(o_out, 16)
            for t in range(TT):
                sp.wait_ge(out_ready, t + 1)
                sp.dma_start(out[0, t * P:(t + 1) * P, :], outb[:, t % 2, :]).then_inc(out_done[t % 2], 16)
            for i in range(2):
                sp.wait_ge(out_done[i], 16 * (TT // 2))

        @block.gpsimd
        def _(pool):
            def col(dst, v, s):
                pool.dma_start(dst, v.rearrange("(c p) -> p c", p=P), allow_slow_non_contiguous=True).then_inc(loaded[s], 16)
            col(ccol, a["c"][0], "c")
            col(g1col, a["norm_mix_g"][0], "g1col")
            for w in range(3):
                col(convw[:, w, :], a["hy_conv_w"][0, w], "conv")
            col(convb, a["hy_conv_b"][0], "conv")
            col(hybias, a["hy_bias"][0], "hyb")
            col(gq, a["q_norm_g"][0], "gqk")
            col(gkv, a["kv_norm_g"][0], "gqk")
            taken(pool, "YI", 3)
            ready(pool, "YI", 3)
            pool.dma_start(rope, a["rope"]).then_inc(loaded["rope"], 16)
            pool.wait_ge(kr_done, 1)
            for h in range(NH):
                nc.gpsimd.tensor_copy(kh[NOPE:QKD, h, :], krope[NOPE:QKD, :]).then_inc(kr_copied, 1)
            pool.wait_ge(mix_done, DC)
            pool.dma_start(g2b, a["norm_ffn_g"].broadcast_to([P, D])).then_inc(loaded["ffng"], 16)
            pool.dma_start(wr[:, :, 0:NG], a["w_group"][0].rearrange("(c p) n -> p c n", p=P)).then_inc(loaded["router"], 16)
            pool.dma_start(wr[:, :, NG:NG + NE], a["w_router"][0].rearrange("(c p) n -> p c n", p=P)).then_inc(loaded["router"], 16)
            pool.dma_start(brow[:, 0:NG], a["b_group"][0:1, :]).then_inc(loaded["router"], 16)
            pool.dma_start(brow[:, NG:NG + NE], a["b_router"][0:1, :]).then_inc(loaded["router"], 16)
            pool.wait_ge(idx_ready, 1)
            pool.wait_ge(h2_out, 16 * TT)

            for e in range(NE):
                if e >= 2:
                    pool.wait_ge(turned, e - 1)
                pool.indirect_dma_start(out=hg[0:BLK, e % 2, :], out_offset=None, in_=h2_dram[:, :],
                                        in_offset=bass.IndirectOffsetOnAxis(ap=idxu[:, e:e + 1], axis=0)).then_inc(rows_in[e % 2], 16)
            with pool.If(over_flag(pool) > 0):
                with pool.Fori(0, NBLK - 1) as b:
                    with pool.Fori(0, NE) as e:
                        n = b * NE + e
                        pool.wait_ge(o_idx, n + 1)
                        nc.gpsimd.tensor_tensor(small[:, 176:177], ones[:, 0:1], ones[:, 0:1], ALU.mult).then_inc(o_carried, 1)
                        pool.indirect_dma_start(out=hg[0:BLK, 0, :], out_offset=None, in_=h2_dram[:, :],
                                                in_offset=bass.IndirectOffsetOnAxis(ap=idxc[:, 0:1], axis=0)).then_inc(o_rows, 16)
                        pool.wait_ge(o_carried, n + 1)
                pool.wait_ge(o_out, 16 * (NBLK - 1) * NE)
                for t in range(TT):
                    for k in range(2):
                        n = 2 * t + k
                        if n:
                            pool.wait_ge(o_added, n)
                        pool.indirect_dma_start(out=yg[:, 0, :], out_offset=None, in_=more_flat,
                                                in_offset=bass.IndirectOffsetOnAxis(ap=morerow[:, k, t:t + 1], axis=0)).then_inc(o_back, 16)
                pool.wait_ge(o_added, 2 * TT)
            for s in range(2):
                pool.wait_ge(y_out[s], 16 * (NE // 2))
            pool.wait_ge(rows_known, 1)
            for t in range(TT):
                for k in range(2):
                    n = 2 * t + k
                    if n >= 4:
                        pool.wait_ge(x2_done, t - 1)
                    pool.indirect_dma_start(out=yg[:, n % 4, :], out_offset=None, in_=y_flat,
                                            in_offset=bass.IndirectOffsetOnAxis(ap=yrow[:, k, t:t + 1], axis=0)).then_inc(back_in[n % 4], 16)

        @block.scalar
        def _(act):
            A = nc.scalar.activation
            step = [0]

            def link(ins):
                step[0] += 1
                ins.then_inc(act_step, 1)
                act.wait_ge(act_step, step[0])

            for dst, nm in ((fb1, "filt_b1"), (ff1, "filt_freq1"), (fb2, "filt_b2"), (ff2, "filt_freq2")):
                act.dma_start(dst, a[nm][0].rearrange("(p o) -> p o", o=1), allow_slow_non_contiguous=True).then_inc(loaded["fb"], 16)
            act.dma_start(window, a["window"].rearrange("(t p) c -> p t c", p=P)).then_inc(loaded["window"], 16)
            act.dma_start(xin, a["x"][0].rearrange("(t p) d -> p t d", p=P)).then_inc(loaded["x"], 16)
            act.dma_start(bcast[:, :], a["dftf"]).then_inc(loaded["dftf"], 16)
            act.dma_start(cst[:, :], a["cst"]).then_inc(loaded["cst"], 16)
            act.wait_ge(loaded["c"], 16)
            A(cact, ccol, ACT.Silu).then_inc(cact_done, 1)
            for n, dst in enumerate((s1T, s2T)):
                act.wait_ge(sin_arg, n + 1)
                A(dst, argT, ACT.Sin).then_inc(sin_done, 1)
            act.wait_ge(loaded["x"], 16)
            act.wait_ge(sin_done, 2)
            for t in range(TT):
                if t:
                    act.wait_ge(x_sumsq, t)
                A(xsq, xin[:, t, :], ACT.Square, accum_out=ss[:, t:t + 1]).then_inc(x_sumsq, 1)
            for t in range(TT):
                act.wait_ge(filt_ready, t + 1)
                A(fraw[:, t, :, :], fraw[:, t, :, :], ACT.Abs).then_inc(absum_ready, 1)
            act.wait_ge(sqrt_arg, 1)
            A(srt, rstd, ACT.Sqrt).then_inc(sqrt_done, 1)
            act.wait_ge(x_rms, 1)
            for t in range(TT):
                A(xin[:, t, :], xin[:, t, :], ACT.Copy, scale=rstd[:, t:t + 1]).then_inc(x_scaled, 1)
            for f in range(4):
                for r in range(2):
                    ready(act, "G", f, r)
                    A(G[:, f, r, :], bank("G", f, r)[:, :], ACT.Copy).then_inc(read_sem["act"], 1)
            for j in range(4):
                ready(act, "AC", j)
                A(modcol[:, 4 * j:4 * j + 4], bank("AC", j)[:, 0:4], ACT.Copy).then_inc(read_sem["act"], 1)
            act.wait_ge(a1_ready, 1)
            for c in range(DC):
                ready(act, "XT", c)
                A(hT[:, c, :], bank("XT", c)[:, :], ACT.Identity, bias=modcol[:, c:c + 1],
                  scale=a1col[:, c:c + 1]).then_inc(read_sem["act"], 1)

            def ada_row(j):
                ready(act, "AB", j)
                A(bcast[:, (j - 4) * 512:(j - 3) * 512], bank("AB", j)[:, :], ACT.Copy).then_inc(read_sem["act"], 1)

            act.wait_ge(loaded["conv"], 64)
            for m in range(3 * HC):
                ready(act, "H", m)
                if m >= 10:
                    act.wait_ge(u_ready, m - 9)
                dst = x0T[:, m, :] if m < HC else x1T[:, m - HC, :] if m < 2 * HC else cvt[:, m % 2, :]
                A(dst, bank("H", m)[:, :], ACT.Identity, bias=convb[:, m:m + 1],
                  scale=convw[:, 1, m:m + 1]).then_inc(conv_centre, 1)
            for t in range(TT):
                ready(act, "UT", t)
                A(uTok[:, t, :], bank("UT", t)[:, :], ACT.Copy).then_inc(read_sem["act"], 1)
            ada_row(4), ada_row(5)
            act.wait_ge(yhy_ready, HC)
            for m in range(QC + KC):
                k = ("CQ", m) if m < QC else ("CK", m - QC)
                raw = cqT[:, m, :] if m < QC else ckvT[:, m - QC, :]
                sq = sqT[:, m, :] if m < QC else rt[:, m - QC, :]
                ready(act, *k)
                A(sq, bank(*k)[:, :], ACT.Square).then_inc(sq_ready, 1)
                A(raw, bank(*k)[:, :], ACT.Copy).then_inc(read_sem["act"], 1)
                if k == ("CK", 0):
                    act.wait_ge(sqrt_arg, 2)
                    A(rb, rb, ACT.Sqrt).then_inc(sqrt_done, 1)
            act.wait_ge(sqrt_arg, 3)
            A(rb, rb, ACT.Sqrt).then_inc(sqrt_done, 1)

            def two_heads(k, i, dst):
                ready(act, k, i)
                link(A(dst[0:NOPE, 2 * i, :], bank(k, i)[0:64, :], ACT.Copy))
                A(dst[0:NOPE, 2 * i + 1, :], bank(k, i)[64:128, :], ACT.Copy).then_inc(read_sem["act"], 1)

            for i in range(4):
                two_heads("QN", i, qh)
            for i in range(4):
                two_heads("KN", i, kh)
            act.wait_ge(q_rope, NH)
            for t in range(TT):
                ready(act, "V", t)
                A(v_sb[:, t, :], bank("V", t)[:, :], ACT.Copy).then_inc(read_sem["act"], 1)
            act.wait_ge(kr_copied, NH)

            def exps(n):
                act.wait_ge(max_done, n + 1)
                if n >= 4:
                    ready(act, "T", n - 4)
                A(prob[:, n % 4, :], bank("S", n)[:, :], ACT.Exp, bias=negmax[:, n % 4:n % 4 + 1], scale=SCORE_SCALE,
                  accum_out=rowsum[:, n % 4:n % 4 + 1]).then_inc(read_sem["act"], 1)

            def head_rows(n):
                h, t = n // TT, n % TT
                o = VH * (h % 2)
                ready(act, "O", n)
                A(ymla[o:o + VH, h // 2, t * P:(t + 1) * P], bank("O", n)[o:o + VH, 0:P], ACT.Copy).then_inc(read_sem["act"], 1)

            def turned_probs(n):
                ready(act, "T", n)
                A(pT[:, n % 2, :], bank("T", n)[:, :], ACT.Copy).then_inc(read_sem["act"], 1)

            for n in range(NA + LAG + 1):
                if n < NA:
                    exps(n)
                if n in AB_AT:
                    ada_row(AB_AT[n])
                if n > LAG:
                    head_rows(n - LAG - 1)
                if LAG <= n < NA + LAG:
                    turned_probs(n - LAG)
            for d in range(DC):
                for g, k in enumerate(("GA", "GB")):
                    ready(act, k, d)
                    if d >= 2:
                        act.wait_ge(mix_done, d - 1)
                    A(sg[:, (2 * d + g) % 4, :], bank(k, d)[:, :], ACT.Sigmoid).then_inc(read_sem["act"], 1)
                if d in AB_GATES:
                    ada_row(AB_GATES[d])
            def turned_h2(t):
                for i in range(2):
                    ready(act, "HT", t, i)
                    A(h2T[:, 4 * i:4 * i + 4, t * P:(t + 1) * P], bank("HT", t, i)[:, :].rearrange("p (c s) -> p c s", c=4), ACT.Copy
                      ).then_inc(read_sem["act"], 1)

            for t in range(TT):
                act.wait_ge(x1_done, t + 1)
                if t:
                    act.wait_ge(x1_sumsq, t)
                A(x1sq[:, :, :], x1[:, t, :].rearrange("p (b n) -> p b n", b=2), ACT.Square, accum_out=ss2[:, t:t + 1]).then_inc(x1_sumsq, 1)
                act.wait_ge(sqrt_arg, 4 + t)
                A(srt2[:, t:t + 1], rstd2[:, t:t + 1], ACT.Sqrt).then_inc(sqrt_done, 1)
                act.wait_ge(h2_done, t + 1)
                act.dma_start(h2_dram[t * P:(t + 1) * P, :], h2[:, t, :]).then_inc(h2_out, 16)
                if t:
                    turned_h2(t - 1)
            turned_h2(TT - 1)
            act.wait_ge(gexp, 1)
            A(gs, gs, ACT.Exp).then_inc(gexp_done, 1)
            act.wait_ge(wexp, 1)
            A(ed, dv, ACT.Exp).then_inc(wexp_done, 1)

            def turned_rows(e, s):
                act.wait_ge(turned, e + 1)
                if not (isinstance(e, int) and e < 2):
                    act.wait_ge(gu_done, e - 1)
                for i in range(2):
                    ins = A(hgT[:, s % 2, 4 * i:4 * i + 4, :], banks[i][:, 0:4 * BLK].rearrange("p (c s) -> p c s", c=4), ACT.Copy)
                ins.then_inc(turned_act, 1)

            def silu(e, s):
                act.wait_ge(gu_done, e + 1)
                if not (isinstance(e, int) and e < 2):
                    act.wait_ge(a_done, e - 1)
                A(sgl[:, s % 2, :], banks[2 + s % 2][:, 0:2 * BLK], ACT.Silu).then_inc(silu_done, 1)

            def four(i, last=False):
                for s in range(EXPERT_SLOTS):
                    e = i * EXPERT_SLOTS + s
                    silu(e, s)
                    if not (last and s == EXPERT_SLOTS - 1):
                        turned_rows(e + 1, s + 1)
            turned_rows(0, 0)
            four(0)
            with act.Fori(1, NE // EXPERT_SLOTS - 1) as i:
                four(i)
            four(NE // EXPERT_SLOTS - 1, last=True)
            with act.If(over_flag(act) > 0):
                with act.Fori(0, NBLK - 1) as b:
                    with act.Fori(0, NE) as e:
                        act.wait_ge(o_gu, b * NE + e + 1)
                        A(sgl[:, 0, :], banks[2][:, 0:2 * BLK], ACT.Silu).then_inc(o_silu, 1)
            for t in range(TT):
                act.wait_ge(x2_done, t + 1)
                if t:
                    act.wait_ge(x2_sumsq, t)
                A(osq, x1[:, t, :], ACT.Square, accum_out=ss3[:, t:t + 1]).then_inc(x2_sumsq, 1)
                act.wait_ge(sqrt3_arg, t + 1)
                A(srt3[:, t:t + 1], rstd3[:, t:t + 1], ACT.Sqrt).then_inc(sqrt3_done, 1)

        @block.tensor
        def _(pe):
            def product(o, pairs):
                for i, (l, r) in enumerate(pairs):
                    mm = nc.tensor.matmul(o, l, r, start=(i == 0), stop=(i == len(pairs) - 1))
                return mm

            def tile_product(k, rows, pairs):
                claim(*k)
                product(bank(*k)[rows, :], pairs).then_inc(pe_done, 1)

            def full(k, pairs):
                tile_product(k, slice(0, P), pairs)

            def turn(k, parts):
                claim(*k)
                for i, p in enumerate(parts):
                    mm = nc.tensor.transpose(bank(*k)[:, i * P:(i + 1) * P], p, ident)
                mm.then_inc(pe_done, 1)

            pe.wait_ge(loaded["zT"], 16)
            pe.wait_ge(loaded["fw"], 48)
            tile_product(("F1",), slice(0, 64), [(fw1, zT)])
            pe.wait_ge(sin_done, 1)
            tile_product(("F2",), slice(0, 64), [(fw2, s1T)])
            pe.wait_ge(sin_done, 2)
            for t in range(TT):
                for d in range(2):
                    full(("F3", t, d), [(s2T[:, t * P:(t + 1) * P], fw3[:, d * HY:(d + 1) * HY])])
            pe.wait_ge(loaded["cst"], 16)
            pe.wait_ge(absum_ready, TT)
            claim("L1")
            for c in range(HC):
                mm = product(bank("L1")[:, c:c + 1], [(fraw[:, t, d, c * P:(c + 1) * P], ones[:, 0:1])
                                                      for t in range(TT) for d in range(2)])
            mm.then_inc(pe_done, 1)
            pe.wait_ge(loaded["dftf"], 16)
            for f in range(4):
                for r in range(2):
                    full(("G", f, r), [(dftf[:, r, t, f * P:(f + 1) * P], filt[:, t, r, :]) for t in range(TT)])
            for j in range(4):
                pe.wait_ge(ada_done, j + 1)
                claim("AC", j)
                for c in range(4):
                    mm = product(bank("AC", j)[:, c:c + 1], [(adasum[:, j % 2, c * P:(c + 1) * P], ones[:, 0:1])])
                mm.then_inc(pe_done, 1)
            pe.wait_ge(x_scaled, TT)
            for c in range(DC):
                turn(("XT", c), [xin[:, t, c * P:(c + 1) * P] for t in range(TT)])
            taken(pe, "XT", DC - 1)
            for m in range(3 * HC):
                arrived(pe, "hy", m // 4)
                full(("H", m), [(w8[("hy", m // 4)][:, c, (m % 4) * P:(m % 4 + 1) * P], hT[:, c, :]) for c in range(DC)])
            pe.wait_ge(u_ready, HC)
            for t in range(TT):
                turn(("UT", t), [uT[:, c, t * P:(t + 1) * P] for c in range(HC)])
            taken(pe, "UT", TT - 1)
            for f in range(4):
                for r in range(2):
                    full(("UF", f, r), [(dftf[:, r, t, f * P:(f + 1) * P], uTok[:, t, :]) for t in range(TT)])

            def ada_row(j):
                pe.wait_ge(ada_done, j + 1)
                full(("AB", j), [(ones, adasum[:, j % 2, :])])
            ada_row(4), ada_row(5)
            arrived(pe, "dft")
            pe.wait_ge(spec_ready, 4)
            for c in range(HC):
                full(("YI", c), [(spec[:, f, r, c * P:(c + 1) * P], dfti[:, r, f, :]) for f in range(4) for r in range(2)])
            arrived(pe, "cq")
            for m in range(QC):
                full(("CQ", m), [(wcq[:, c, m * P:(m + 1) * P], hT[:, c, :]) for c in range(DC)])
            arrived(pe, "ckv")

            def ckv(m):
                full(("CK", m), [(wckv[:, c, m * P:(m + 1) * P], hT[:, c, :]) for c in range(DC)])
            ckv(0)
            pe.wait_ge(sq_ready, QC)
            full(("QS",), [(ones, sqT[:, m, :]) for m in range(QC)])
            ckv(1)
            tile_product(("KR",), slice(NOPE, QKD), [(wckv[:, c, KVL:KVL + ROPE], hT[:, c, :]) for c in range(DC)])
            pe.wait_ge(sq_ready, QC + KC)
            full(("KS",), [(ones, rt[:, m, :]) for m in range(KC)])
            pe.wait_ge(rotw_ready, 1)
            tile_product(("KT",), slice(NOPE, QKD), [(wkrot[:, c, :], hT[:, c, :]) for c in range(DC)])
            arrived(pe, "uquk")
            pe.wait_ge(latent_ready, QC)
            for i in range(4):
                full(("QN", i), [(wuqn[:, c, 2 * i:2 * i + 2, :], cqT[:, c, :]) for c in range(QC)])
            pe.wait_ge(rotw_ready, 2)
            for g in range(2):
                full(("QR", g), [(wuqr[:, c, 4 * g:4 * g + 4, :], cqT[:, c, :]) for c in range(QC)])
                full(("QT", g), [(wrot[:, c, 4 * g:4 * g + 4, :], cqT[:, c, :]) for c in range(QC)])
            pe.wait_ge(latent_ready, QC + KC)
            for i in range(4):
                full(("KN", i), [(wuk[:, c, i * P:(i + 1) * P], ckvT[:, c, :]) for c in range(KC)])
            arrived(pe, "uv")
            for t in range(TT):
                full(("V", t), [(ckvT[:, c, t * P:(t + 1) * P], wuv[:, c, :]) for c in range(KC)])
            taken(pe, "KN", 3)
            pe.wait_ge(q_rope, NH)
            pe.wait_ge(kr_copied, NH)
            taken(pe, "V", TT - 1)
            for n in range(NA + LAG + 1):
                if n < NA:
                    h, t = n // TT, n % TT
                    full(("S", n), [(qh[0:QKD, h, t * P:(t + 1) * P], kh[0:QKD, h, :])])
                if n in AB_AT:
                    ada_row(AB_AT[n])
                if n > LAG:
                    m = n - LAG - 1
                    h, o = m // TT, VH * (m // TT % 2)
                    taken(pe, "T", m)
                    claim("O", m)
                    product(bank("O", m)[o:o + VH, 0:P], [(v_sb[:, k, h * VH:(h + 1) * VH], pT[:, m % 2, k * P:(k + 1) * P])
                                                          for k in range(TT)]).then_inc(pe_done, 1)
                if LAG <= n < NA + LAG:
                    m = n - LAG
                    pe.wait_ge(prob_done, m + 1)
                    turn(("T", m), [prob[:, m % 4, k * P:(k + 1) * P] for k in range(TT)])
            for d in range(DC):
                for g, k in enumerate(("GA", "GB")):
                    arrived(pe, "g", g, d // 4)
                    full((k, d), [(w8[("g", g, d // 4)][:, c, (d % 4) * P:(d % 4 + 1) * P], hT[:, c, :]) for c in range(DC)])
                if d in AB_GATES:
                    ada_row(AB_GATES[d])
                if d == 0:
                    arrived(pe, "whyo")
                    arrived(pe, "wmlao")
                    taken(pe, "O", NA - 1)
                full(("MA", d), [(whyo[:, c, d * P:(d + 1) * P], yhy[:, c, :]) for c in range(HC)])
                full(("MB", d), [(wmlao[:, c, d * P:(d + 1) * P], ymla[:, c, :]) for c in range(HC)])
            pe.wait_ge(mix_done, DC)
            def turn_h2(t):
                pe.wait_ge(h2_done, t + 1)
                for i in range(2):
                    turn(("HT", t, i), [h2[:, t, c * P:(c + 1) * P] for c in range(4 * i, 4 * i + 4)])
            for t in range(TT):
                for hf in range(2):
                    arrived(pe, "mix", hf)
                    full(("W", t, hf), [(mixT[:, c, t * P:(t + 1) * P], w8[("mix", hf)][:, c, :]) for c in range(DC)])
                if t:
                    turn_h2(t - 1)
            turn_h2(TT - 1)
            taken(pe, "HT", TT - 1, 1)
            pe.wait_ge(loaded["router"], 64)
            claim("LG")
            for t in range(TT):
                mm = product(bank("LG")[:, t * 36:(t + 1) * 36], [(h2T[:, c, t * P:(t + 1) * P], wr[:, c, :]) for c in range(DC)]
                             + [(ones[0:1, :], brow)])
            mm.then_inc(pe_done, 1)
            pe.wait_ge(onehots, 1)
            claim("RK")
            for t in range(TT):
                product(bank("RK")[:, t * NE:(t + 1) * NE], [(lower, ohs[:, t, :])] + [(ones, ohs[:, j, :]) for j in range(t)])
            product(bank("RK")[:, TT * NE:(TT + 1) * NE], [(ones, ohs[:, j, :]) for j in range(TT)]).then_inc(pe_done, 1)
            pe.wait_ge(slots_ready, 1)
            claim("IX")
            product(bank("IX")[0:BLK, 0:NE], [(Rm[:, k, t, :], ohv[:, k, t, :]) for k in range(2) for t in range(TT)]
                    ).then_inc(pe_done, 1)

            def turn_rows(s, sem_):
                v = hg[0:BLK, s % 2, :].rearrange("s (p c) -> s c p", c=DC)
                for c in range(DC):
                    mm = nc.tensor.transpose(banks[c // 4][:, (c % 4) * BLK:(c % 4 + 1) * BLK], v[:, c, :], ident[0:BLK, 0:BLK])
                mm.then_inc(sem_, 1)

            def gate_up(w, s, b, sem_):
                for g in range(4):
                    m = (wg_s, wu_s)[g // 2][w]
                    mm = product(banks[2 + b][:, g * BLK:(g + 1) * BLK],
                                 [(m[:, c, (g % 2) * P:(g % 2 + 1) * P], hgT[:, s % 2, c, :]) for c in range(DC)])
                mm.then_inc(sem_, 1)

            def down(w, s, b, sem_):
                for hf in range(2):
                    mm = product(banks[4 + 2 * b + hf][0:BLK, :],
                                 [(aT[:, s % 2, f * BLK:(f + 1) * BLK], wd_s[w][:, f, hf * 512:(hf + 1) * 512]) for f in range(2)])
                mm.then_inc(sem_, 1)

            def turn_expert(e, s, i):
                pe.wait_ge(rows_in[s % 2], i * 32 + 16 * (s // 2) + 16)
                if not (isinstance(e, int) and e == 0):
                    pe.wait_ge(turned_act, e)
                turn_rows(s, turned)

            def gate_up_expert(e, s, i):
                pe.wait_ge(turned_act, e + 1)
                pe.wait_ge(gu_in[s], i * 32 + 32)
                if not (isinstance(e, int) and e < 2):
                    pe.wait_ge(a_done, e - 1)
                gate_up(s, s, s % 2, gu_done)

            def down_expert(e, s, i):
                pe.wait_ge(a_done, e + 1)
                pe.wait_ge(dn_in[s], i * 16 + 16)
                if not (isinstance(e, int) and e < 2):
                    pe.wait_ge(y_dve, e - 1)
                down(s, s, s % 2, y_done)

            def four(i, first=False, last=False):
                for s in range(EXPERT_SLOTS):
                    e = i * EXPERT_SLOTS + s
                    gate_up_expert(e, s, i)
                    if not (last and s == EXPERT_SLOTS - 1):
                        turn_expert(e + 1, (s + 1) % 4, i + 1 if s == 3 else i)
                    if not (first and s == 0):
                        down_expert(e - 1, (s - 1) % 4, i - 1 if s == 0 else i)
            taken(pe, "IX")
            turn_expert(0, 0, 0)
            four(0, first=True)
            with pe.Fori(1, NE // EXPERT_SLOTS - 1) as i:
                four(i)
            four(NE // EXPERT_SLOTS - 1, last=True)
            down_expert(NE - 1, 3, NE // EXPERT_SLOTS - 1)
            with pe.If(over_flag(pe) > 0):
                with pe.Fori(0, NBLK - 1) as b:
                    pe.wait_ge(o_slots, b + 1)
                    product(banks[7][0:BLK, 0:NE], [(Rm[:, k, t, :], ohv[:, k, t, :]) for k in range(2) for t in range(TT)]
                            ).then_inc(o_tok, 1)
                    with pe.Fori(0, NE) as e:
                        n = b * NE + e
                        pe.wait_ge(o_rows, n * 16 + 16)
                        turn_rows(0, o_turned)
                        pe.wait_ge(o_read, n + 1)
                        pe.wait_ge(o_w, n * 48 + 48)
                        gate_up(0, 0, 0, o_gu)
                        pe.wait_ge(o_hidden, n + 1)
                        down(0, 0, 0, o_y)

        @block.vector
        def _(dve):
            V = nc.vector
            step = [0]

            def link(ins):
                step[0] += 1
                ins.then_inc(dve_step, 1)
                dve.wait_ge(dve_step, step[0])

            def read(ins):
                ins.then_inc(read_sem["dve"], 1)

            def ada(j, rows=range(DC)):
                if j == 0:
                    dve.wait_ge(cact_done, 1)
                if rows[0] == 0:
                    arrived(dve, "ada", j)
                    dve.wait_ge(bias_in[j % 2], 16 * (j // 2 + 1))
                    if j >= 2:
                        ready(dve, "AC" if j < 6 else "AB", j - 2)
                for c in rows:
                    ins = V.scalar_tensor_tensor(out=adasum[:, j % 2, :], in0=w8[("ada", j)][:, c, :], scalar=cact[:, c:c + 1],
                                                 in1=adab[:, j % 2, :] if c == 0 else adasum[:, j % 2, :], op0=ALU.mult, op1=ALU.add)
                    if c < DC - 1:
                        link(ins)
                    else:
                        ins.then_inc(ada_done, 1)

            link(V.memset(adab[:, :, :], 0.0))
            V.memset(over, 0.0).then_inc(bias_clear, 1)
            dve.wait_ge(loaded["fb"], 64)
            for n, (b, f) in enumerate(((fb1, ff1), (fb2, ff2))):
                k = (f"F{n + 1}",)
                ready(dve, *k)
                if n:
                    dve.wait_ge(sin_done, n)
                ins = V.tensor_scalar(argT, bank(*k)[0:64, :], b, f, ALU.add, ALU.mult)
                read(ins)
                taken(dve, *k)
                link(V.tensor_scalar(rndT, argT, 1.0 / TWO_PI, ROUND, ALU.mult, ALU.add))
                link(V.tensor_scalar(rndT, rndT, ROUND, None, ALU.subtract))
                link(V.scalar_tensor_tensor(out=argT, in0=rndT, scalar=-PI2_HI, in1=argT, op0=ALU.mult, op1=ALU.add))
                link(V.scalar_tensor_tensor(out=argT, in0=rndT, scalar=-PI2_LO, in1=argT, op0=ALU.mult, op1=ALU.add))
                V.tensor_scalar(argT, argT, -3.1415925, 3.1415925, ALU.max, ALU.min).then_inc(sin_arg, 1)
                ada(n)

            dve.wait_ge(loaded["window"], 16)
            dve.wait_ge(sin_done, 2)
            for t in range(TT):
                for d in range(2):
                    ready(dve, "F3", t, d)
                    read(V.tensor_tensor(fraw[:, t, d, :], bank("F3", t, d)[:, :], window[:, t, :], ALU.mult))
                taken(dve, "F3", t, 1)
                if t == 0:
                    link(V.memset(fraw[0:1, 0, 1, :], 0.0))
                V.tensor_tensor(filt[:, t, 0, :], fraw[:, t, 0, :], fraw[:, t, 1, :], ALU.add)
                V.tensor_tensor(filt[:, t, 1, :], fraw[:, t, 0, :], fraw[:, t, 1, :], ALU.subtract).then_inc(filt_ready, 1)
            dve.wait_ge(x_sumsq, TT)
            V.tensor_scalar(rstd, ss, 1.0 / D, EPS, ALU.mult, ALU.add).then_inc(sqrt_arg, 1)
            dve.wait_ge(sqrt_done, 1)
            V.reciprocal(rstd, srt).then_inc(x_rms, 1)
            ready(dve, "L1")
            read(V.reciprocal(invl1, bank("L1")[:, 0:HC]))
            ada(2)
            ada(3)
            taken(dve, "AC", 3)
            dve.wait_ge(loaded["g1col"], 16)
            V.scalar_tensor_tensor(out=a1col, in0=modcol[:, 8:16], scalar=1.0, in1=g1col, op0=ALU.add, op1=ALU.mult
                                   ).then_inc(a1_ready, 1)
            for m in range(3 * HC):
                dve.wait_ge(conv_centre, m + 1)
                dst = x0T[:, m, :] if m < HC else x1T[:, m - HC, :] if m < 2 * HC else cvt[:, m % 2, :]
                b = bank("H", m)
                link(V.scalar_tensor_tensor(out=dst[:, 1:L], in0=b[:, 0:L - 1], scalar=convw[:, 0, m:m + 1],
                                            in1=dst[:, 1:L], op0=ALU.mult, op1=ALU.add))
                read(V.scalar_tensor_tensor(out=dst[:, 0:L - 1], in0=b[:, 1:L], scalar=convw[:, 2, m:m + 1],
                                            in1=dst[:, 0:L - 1], op0=ALU.mult, op1=ALU.add))
                if m >= 2 * HC:
                    taken(dve, "H", m)
                    V.tensor_tensor(uT[:, m - 2 * HC, :], dst, x1T[:, m - 2 * HC, :], ALU.mult).then_inc(u_ready, 1)
            ada(4)
            ada(5)
            taken(dve, "G", 3, 1)
            for f in range(4):
                ready(dve, "UF", f, 1)
                if f:
                    dve.wait_ge(spec_ready, f)
                ur, ui, gr, gi = bank("UF", f, 0)[:, :], bank("UF", f, 1)[:, :], G[:, f, 0, :], G[:, f, 1, :]
                V.tensor_tensor(cm[:, 0, :], ur, gr, ALU.mult)
                V.tensor_tensor(cm[:, 1, :], ui, gi, ALU.mult)
                read(V.tensor_tensor(cm[:, 2, :], ur, gi, ALU.mult))
                read(V.tensor_tensor(cm[:, 3, :], ui, gr, ALU.mult))
                taken(dve, "UF", f, 1)
                V.tensor_tensor(spec[:, f, 0, :], cm[:, 0, :], cm[:, 1, :], ALU.subtract)
                V.tensor_tensor(spec[:, f, 1, :], cm[:, 2, :], cm[:, 3, :], ALU.add).then_inc(spec_ready, 1)
            dve.wait_ge(loaded["hyb"], 16)
            for c in range(HC):
                ready(dve, "YI", c)
                read(V.tensor_scalar(cm[:, c, :], bank("YI", c)[:, :], invl1[:, c:c + 1], None, ALU.mult))
                taken(dve, "YI", c)
                link(V.scalar_tensor_tensor(out=cm[:, c, :], in0=uT[:, c, :], scalar=hybias[:, c:c + 1], in1=cm[:, c, :],
                                            op0=ALU.mult, op1=ALU.add))
                V.tensor_tensor(yhy[:, c, :], cm[:, c, :], x0T[:, c, :], ALU.mult).then_inc(yhy_ready, 1)
            H2 = ROPE // 2
            dve.wait_ge(yhy_ready, HC)
            arrived(dve, "ckv")
            V.tensor_scalar(wkrot[:, :, 0:H2], wckv[:, :, KVL + H2:KVL + ROPE], -1.0, None, ALU.mult)
            V.tensor_copy(wkrot[:, :, H2:ROPE], wckv[:, :, KVL:KVL + H2]).then_inc(rotw_ready, 1)
            dve.wait_ge(loaded["gqk"], 32)

            def latent(n, k, width, tiles, lat, g):
                ready(dve, k)
                read(V.tensor_scalar(rb, bank(k)[:, :], 1.0 / width, EPS, ALU.mult, ALU.add))
                taken(dve, k)
                dve.engine_nop().then_inc(sqrt_arg, 1)
                dve.wait_ge(sqrt_done, 2 + n)
                link(V.reciprocal(rb, rb))
                taken(dve, "CQ" if n == 0 else "CK", tiles - 1)
                for m in range(tiles):
                    V.scalar_tensor_tensor(out=lat[:, m, :], in0=lat[:, m, :], scalar=g[:, m:m + 1], in1=rb,
                                           op0=ALU.mult, op1=ALU.mult).then_inc(latent_ready, 1)
            latent(0, "QS", QL, QC, cqT, gq)
            dve.wait_ge(loaded["rope"], 16)
            ready(dve, "KR")
            read(V.tensor_tensor(krope[NOPE:QKD, :], bank("KR")[NOPE:QKD, :], rope[NOPE:QKD, 0, :], ALU.mult))
            dve.wait_ge(latent_ready, QC)
            latent(1, "KS", KVL, KC, ckvT, gkv)
            ready(dve, "KT")
            read(V.tensor_tensor(ktmp[NOPE:QKD, :], bank("KT")[NOPE:QKD, :],
                                 rope[NOPE:QKD, 1, :], ALU.mult))
            taken(dve, "KT")
            V.tensor_tensor(krope[NOPE:QKD, :], krope[NOPE:QKD, :], ktmp[NOPE:QKD, :], ALU.add).then_inc(kr_done, 1)
            arrived(dve, "uquk")
            for c in range(QC):
                V.tensor_scalar(wrot[:, c, :, 0:H2], wuqr[:, c, :, H2:ROPE], -1.0, None, ALU.mult)
                ins = V.tensor_copy(wrot[:, c, :, H2:ROPE], wuqr[:, c, :, 0:H2])
            ins.then_inc(rotw_ready, 1)
            for g in range(2):
                ready(dve, "QR", g)
                if g:
                    dve.wait_ge(q_rope, 4)
                read(V.tensor_tensor(rt[:, 0, :], bank("QR", g)[:, :], rope[:, 0, :], ALU.mult))
                ready(dve, "QT", g)
                read(V.tensor_tensor(rt[:, 1, :], bank("QT", g)[:, :], rope[:, 1, :], ALU.mult))
                taken(dve, "QT", g)
                for j in range(4):
                    r = slice(ROPE * j, ROPE * (j + 1))
                    V.tensor_tensor(qh[NOPE:QKD, 4 * g + j, :], rt[r, 0, :], rt[r, 1, :], ALU.add).then_inc(q_rope, 1)

            def row_max(n):
                ready(dve, "S", n)
                if n >= 4:
                    taken(dve, "S", n - 4)
                link(V.reduce_max(rowmax[:, n % 4:n % 4 + 1], bank("S", n)[:, :], X))
                V.tensor_scalar(negmax[:, n % 4:n % 4 + 1], rowmax[:, n % 4:n % 4 + 1], -SCORE_SCALE, None, ALU.mult
                                ).then_inc(max_done, 1)

            def normalise(n):
                taken(dve, "S", n)
                link(V.reciprocal(rinv[:, n % 4:n % 4 + 1], rowsum[:, n % 4:n % 4 + 1]))
                V.tensor_scalar(prob[:, n % 4, :], prob[:, n % 4, :], rinv[:, n % 4:n % 4 + 1], None, ALU.mult
                                ).then_inc(prob_done, 1)

            for n in range(NA + 1):
                if n < NA:
                    row_max(n)
                if n:
                    normalise(n - 1)
                if n < NA:
                    ada(6 + n // DC, [n % DC])
            for d in range(DC):
                if d < 2:
                    ada(10, range(4 * d, 4 * d + 4))
                elif 3 <= d < 5:
                    ada(11, range(4 * d - 12, 4 * d - 8))
                ga, gb = sg[:, 2 * d % 4, :], sg[:, (2 * d + 1) % 4, :]
                taken(dve, "GB", d)
                ready(dve, "MA", d)
                read(V.tensor_tensor(ga, bank("MA", d)[:, :], ga, ALU.mult))
                ready(dve, "MB", d)
                read(V.tensor_tensor(gb, bank("MB", d)[:, :], gb, ALU.mult))
                taken(dve, "MB", d)
                V.tensor_tensor(mixT[:, d, :], ga, gb, ALU.add).then_inc(mix_done, 1)
            taken(dve, "AB", 11)
            dve.wait_ge(loaded["ffng"], 16)
            link(V.scalar_tensor_tensor(out=bcast[:, 2 * D:3 * D], in0=bcast[:, 2 * D:3 * D], scalar=1.0, in1=g2b,
                                        op0=ALU.add, op1=ALU.mult))
            dve.wait_ge(loaded["x1"], 16)
            for t in range(TT):
                for hf in range(2):
                    ready(dve, "W", t, hf)
                    read(V.tensor_tensor(gated[:, hf, :], bank("W", t, hf)[:, :], bcast[:, hf * 512:(hf + 1) * 512], ALU.mult))
                taken(dve, "W", t, 1)
                V.tensor_tensor(x1[:, t, :], x1[:, t, :], gated[:, :, :].rearrange("p b n -> p (b n)"), ALU.add).then_inc(x1_done, 1)
                dve.wait_ge(x1_sumsq, t + 1)
                V.tensor_scalar(rstd2[:, t:t + 1], ss2[:, t:t + 1], 1.0 / D, EPS, ALU.mult, ALU.add).then_inc(sqrt_arg, 1)
                dve.wait_ge(sqrt_done, 4 + t)
                link(V.reciprocal(rstd2[:, t:t + 1], srt2[:, t:t + 1]))
                link(V.scalar_tensor_tensor(out=h2[:, t, :], in0=x1[:, t, :], scalar=rstd2[:, t:t + 1], in1=bcast[:, 2 * D:3 * D],
                                            op0=ALU.mult, op1=ALU.mult))
                V.tensor_tensor(h2[:, t, :], h2[:, t, :], bcast[:, D:2 * D], ALU.add).then_inc(h2_done, 1)

            def wide(v, n):
                return v.unsqueeze(2).broadcast_to([P, TT, n])

            def const(at_, n):
                return cst[:, at_:at_ + n].unsqueeze(1).broadcast_to([P, TT, n])

            def first_max(vals, top, scratch, index, onehot, n, iota, iota_far):
                link(V.tensor_reduce(top, vals, X, ALU.max))
                link(V.tensor_tensor(scratch, vals, wide(top, n), ALU.is_ge))
                link(V.scalar_tensor_tensor(out=scratch, in0=scratch, scalar=-100.0, in1=const(iota_far, n),
                                            op0=ALU.mult, op1=ALU.add))
                link(V.tensor_reduce(index, scratch, X, ALU.min))
                link(V.tensor_tensor(onehot, const(iota, n), wide(index, n), ALU.is_equal))

            ready(dve, "LG")
            read(V.tensor_copy(lg, bank("LG")[:, 0:144].rearrange("p (t n) -> p t n", t=TT)))
            taken(dve, "LG")
            first_max(lg[:, :, 0:NG], gmax, geq, i0, gm, NG, C_I4, C_I4B)
            V.tensor_tensor(gs, lg[:, :, 0:NG], wide(gmax, NG), ALU.subtract).then_inc(gexp, 1)
            link(V.tensor_scalar(pen, gm, BIG, -BIG, ALU.mult, ALU.add))
            for t in range(TT):
                e3 = em[:, t, :].rearrange("p (g n) -> p g n", g=NG)
                link(V.tensor_tensor(e3, lg[:, t, NG:NG + NE].rearrange("p (g n) -> p g n", g=NG),
                                     gm[:, t, :].unsqueeze(2).broadcast_to([P, NG, EPG]), ALU.mult))
                link(V.tensor_tensor(e3, e3, pen[:, t, :].unsqueeze(2).broadcast_to([P, NG, EPG]), ALU.add))
            first_max(em, m1, eq, i1, oh1, NE, C_I32, C_I32B)
            link(V.scalar_tensor_tensor(out=em, in0=oh1, scalar=-BIG, in1=em, op0=ALU.mult, op1=ALU.add))
            first_max(em, m2, eq, i2, oh2, NE, C_I32, C_I32B)
            V.tensor_tensor(ohs, oh1, oh2, ALU.add).then_inc(onehots, 1)
            V.tensor_tensor(dv, m2, m1, ALU.subtract).then_inc(wexp, 1)
            dve.wait_ge(gexp_done, 1)
            link(V.tensor_reduce(gsum, gs, X, ALU.add))
            link(V.reciprocal(psel, gsum))
            dve.wait_ge(wexp_done, 1)
            link(V.tensor_scalar(w1c, ed, 1.0, None, ALU.add))
            link(V.reciprocal(w2c, w1c))
            link(V.tensor_tensor(w1c, w2c, psel, ALU.mult))
            link(V.tensor_tensor(w2c, w1c, ed, ALU.mult))
            link(V.tensor_tensor(ohv[:, 0], oh1, wide(cst[:, C_TOK:C_TOK + TT], NE), ALU.mult))
            link(V.tensor_tensor(ohv[:, 1], oh2, wide(cst[:, C_TOK:C_TOK + TT], NE), ALU.mult))
            ready(dve, "RK")
            link(V.tensor_copy(cnt, bank("RK")[:, TT * NE:(TT + 1) * NE]))
            read(V.tensor_copy(rk, bank("RK")[:, 0:TT * NE].rearrange("p (t n) -> p t n", t=TT)))
            taken(dve, "RK")
            for oh, r in ((oh1, r1), (oh2, r2)):
                link(V.tensor_tensor(eq, oh, rk, ALU.mult))
                link(V.tensor_reduce(r, eq, X, ALU.add))

            def slot_onehots(sem_):
                for k in range(2):
                    for t in range(TT):
                        ins = V.tensor_scalar(Rm[:, k, t, :], cst[:, C_IB:C_IB + BLK], r12[:, k, t:t + 1], None, ALU.is_equal)
                ins.then_inc(sem_, 1)
            slot_onehots(slots_ready)
            link(V.tensor_reduce(over, cnt, X, ALU.max))
            link(V.tensor_scalar(over, over, float(BLK), None, ALU.is_gt))
            V.tensor_copy(overu, over).then_inc(over_ready, 1)
            ready(dve, "IX")
            read(V.tensor_copy(idxu, bank("IX")[0:BLK, 0:NE]))
            taken(dve, "IX")
            dve.engine_nop().then_inc(idx_ready, 1)
            for k, (i_, r, w) in enumerate(((i1, r1, w1c), (i2, r2, w2c))):
                link(V.tensor_scalar(rankf, r, float(BLK), None, ALU.is_lt))
                link(V.tensor_tensor(wfirst[:, k, :], w, rankf, ALU.mult))
                link(V.tensor_tensor(wmore[:, k, :], w, wfirst[:, k, :], ALU.subtract))
                link(V.tensor_scalar(rankf, r, float(BLK - 1), None, ALU.min))
                link(V.scalar_tensor_tensor(out=rowf, in0=i_, scalar=float(BLK), in1=rankf, op0=ALU.mult, op1=ALU.add))
                link(V.tensor_copy(yrow[:, k, :], rowf))
                link(V.tensor_scalar(rankf, r, float(BLK), 0.0, ALU.subtract, ALU.max))
                link(V.scalar_tensor_tensor(out=rowf, in0=i_, scalar=float(MORE), in1=rankf, op0=ALU.mult, op1=ALU.add))
                link(V.tensor_copy(morerow[:, k, :], rowf))
            dve.engine_nop().then_inc(rows_known, 1)

            def hidden(e, s):
                dve.wait_ge(silu_done, e + 1)
                if not (isinstance(e, int) and e < 2):
                    dve.wait_ge(y_done, e - 1)
                V.tensor_tensor(aT[:, s % 2, :], banks[2 + s % 2][:, 2 * BLK:4 * BLK], sgl[:, s % 2, :], ALU.mult).then_inc(a_done, 1)

            def gate_rows(b, s):
                for hf in range(2):
                    ins = V.tensor_tensor(yb[0:BLK, s % 2, hf * 512:(hf + 1) * 512], banks[4 + 2 * b + hf][0:BLK, :],
                                          bcast[0:BLK, 3 * D + hf * 512:3 * D + (hf + 1) * 512], ALU.mult)
                return ins

            def y_rows(e, s, i):
                dve.wait_ge(y_done, e + 1)
                if not (isinstance(e, int) and e < 2):
                    dve.wait_ge(y_out[s % 2], i * 32 + 16 * (s // 2))
                gate_rows(s % 2, s).then_inc(y_dve, 1)

            def four(i, first=False):
                for s in range(EXPERT_SLOTS):
                    e = i * EXPERT_SLOTS + s
                    hidden(e, s)
                    if not (first and s == 0):
                        y_rows(e - 1, (s - 1) % 4, i - 1 if s == 0 else i)
            four(0, first=True)
            with dve.Fori(1, NE // EXPERT_SLOTS - 1) as i:
                four(i)
            four(NE // EXPERT_SLOTS - 1)
            y_rows(NE - 1, 3, NE // EXPERT_SLOTS - 1)
            with dve.If(over_flag(dve) > 0):
                for s in range(2):
                    dve.wait_ge(y_out[s], 16 * (NE // 2))
                V.memset(rankf, 0.0).then_inc(o_yread, 1)
                with dve.Fori(0, NBLK - 1) as b:
                    V.tensor_scalar(r12, r12, float(BLK), None, ALU.subtract).then_inc(o_rank, 1)
                    dve.wait_ge(o_rank, b + 1)
                    slot_onehots(o_slots)
                    dve.wait_ge(o_tok, b + 1)
                    V.tensor_copy(idxu, banks[7][0:BLK, 0:NE]).then_inc(o_idxu, 1)
                    dve.wait_ge(y_out[0], 16 * (NE // 2))
                    dve.wait_ge(o_idxu, b + 1)
                    with dve.Fori(0, NE) as e:
                        n = b * NE + e
                        V.tensor_copy(idxc[:, 0:1], idxu[:, bass.ds(e, 1)]).then_inc(o_idx, 1)
                        dve.wait_ge(o_turned, n + 1)
                        V.tensor_copy(hgT[:, 0, 0:4, :], banks[0][:, 0:4 * BLK].rearrange("p (c s) -> p c s", c=4))
                        V.tensor_copy(hgT[:, 0, 4:8, :], banks[1][:, 0:4 * BLK].rearrange("p (c s) -> p c s", c=4)).then_inc(o_read, 1)
                        dve.wait_ge(o_silu, n + 1)
                        V.tensor_tensor(aT[:, 0, :], banks[2][:, 2 * BLK:4 * BLK], sgl[:, 0, :], ALU.mult).then_inc(o_hidden, 1)
                        dve.wait_ge(o_y, n + 1)
                        gate_rows(0, 0).then_inc(o_yread, 1)
                        dve.wait_ge(o_out, n * 16 + 16)
                for t in range(TT):
                    for k in range(2):
                        n = 2 * t + k
                        dve.wait_ge(o_back, 16 * n + 16)
                        V.scalar_tensor_tensor(out=x1[:, t, :], in0=yg[:, 0, :], scalar=wmore[:, k, t:t + 1], in1=x1[:, t, :],
                                               op0=ALU.mult, op1=ALU.add).then_inc(o_added, 1)
                        dve.wait_ge(o_added, n + 1)
            dve.wait_ge(loaded["fing"], 16)
            def final_norm(t):
                dve.wait_ge(x2_sumsq, t + 1)
                V.tensor_scalar(rstd3[:, t:t + 1], ss3[:, t:t + 1], 1.0 / D, EPS, ALU.mult, ALU.add).then_inc(sqrt3_arg, 1)
                dve.wait_ge(sqrt3_done, t + 1)
                link(V.reciprocal(rstd3[:, t:t + 1], srt3[:, t:t + 1]))
                if t >= 2:
                    dve.wait_ge(out_done[t % 2], 16 * (t // 2))
                V.scalar_tensor_tensor(out=outb[:, t % 2, :], in0=x1[:, t, :], scalar=rstd3[:, t:t + 1], in1=fgb,
                                       op0=ALU.mult, op1=ALU.mult).then_inc(out_ready, 1)
            for t in range(TT):
                for k in range(2):
                    b = (2 * t + k) % 4
                    dve.wait_ge(back_in[b], 16 * (t // 2 + 1))
                    ins = V.scalar_tensor_tensor(out=x1[:, t, :], in0=yg[:, b, :], scalar=wfirst[:, k, t:t + 1], in1=x1[:, t, :],
                                                 op0=ALU.mult, op1=ALU.add)
                    if k == 0:
                        link(ins)
                ins.then_inc(x2_done, 1)
                if t:
                    final_norm(t - 1)
            final_norm(TT - 1)


_INPUTS = ("x c ada_w ada_b norm_mix_g w_in hy_conv_w hy_conv_b filt_w1 filt_b1 filt_freq1 filt_w2 filt_b2 filt_freq2 "
           "filt_w3 hy_bias q_norm_g kv_norm_g w_uq w_uk w_uv w_hy_out w_mla_out w_mix_out norm_ffn_g w_group b_group "
           "w_router b_router w_gate w_up w_down final_norm_g").split()


def shape_constants():
    import numpy as np
    f32 = np.float32
    cst = np.zeros((P, C_END), f32)
    cst[:, C_ID:C_ID + P] = np.eye(P)
    cst[:, C_ONE:C_ONE + P] = 1.0
    cst[:, C_LT:C_LT + P] = np.arange(P)[:, None] < np.arange(P)[None, :]
    cst[:, C_I32:C_I32 + NE] = np.arange(NE)
    cst[:, C_I32B:C_I32B + NE] = np.arange(NE) + 100
    cst[:, C_IB:C_IB + BLK] = np.arange(BLK)
    cst[:, C_TOK:C_TOK + TT] = np.arange(P)[:, None] + P * np.arange(TT)[None, :]
    cst[:, C_I4:C_I4 + NG] = np.arange(NG)
    cst[:, C_I4B:C_I4B + NG] = np.arange(NG) + 100
    t = np.linspace(0.0, 1.0, L, dtype=f32)[:, None]
    pos = np.arange(L, dtype=f32)[:, None]
    bands = np.linspace(1e-4, 15, 16, dtype=f32)[None, :]
    ang = (f32(2.0 * math.pi) * bands * pos) / f32(L)
    z = np.concatenate([t, np.cos(ang), -np.sin(ang)], axis=1).astype(f32)
    lo, hi = math.log(1e-2) / 1.5, math.log(1e-2) / 0.3
    deltas = np.linspace(lo, hi, HY, dtype=f32)
    window = (np.exp(-t * np.abs(deltas)[None, :]) + f32(0.05)).astype(f32)
    theta = 2.0 * np.pi * (np.arange(L)[None, :] + 0.5) * np.arange(L)[:, None] / (2 * L)
    fwd = np.stack([np.cos(theta), -np.sin(theta)])
    inv = np.stack([np.cos(theta).T, -np.sin(theta).T]) / L

    def rows_to_partitions(m):
        return np.ascontiguousarray(m.reshape(2, 4, P, L).transpose(2, 0, 1, 3).reshape(P, 8 * L).astype(f32))
    rinv = f32(10000.0) ** (-np.arange(0, ROPE, 2, dtype=f32) / f32(ROPE))
    ra = np.arange(L, dtype=f32)[:, None] * rinv[None, :].astype(f32)
    rope = np.stack([np.tile(np.cos(ra).T, (8, 1)), np.tile(np.sin(ra).T, (8, 1))], axis=1).astype(f32)
    return {"cst": cst, "zT": np.ascontiguousarray(z.T), "window": window, "dftf": rows_to_partitions(fwd),
            "dfti": rows_to_partitions(inv), "rope": np.ascontiguousarray(rope)}


def kernel(**inputs):
    import numpy as np
    import concourse.bacc as bacc
    from concourse.bass_utils import run_bass_kernel_spmd

    nc = bacc.Bacc("TRN2", target_bir_lowering=False, num_devices=1)
    arrays, args = {}, {}
    given = {n: np.ascontiguousarray(inputs[n]) for n in _INPUTS}
    given.update(shape_constants())
    for n, v in given.items():
        arrays["in_" + n] = v
        args[n] = nc.dram_tensor("in_" + n, v.shape, mybir.dt.from_np(v.dtype), kind="ExternalInput").ap()
    out = nc.dram_tensor("out_0", (1, L, D), F32, kind="ExternalOutput").ap()
    h2_dram = nc.dram_tensor("h2_rows", (L, D), F32, kind="Internal").ap()
    y_dram = nc.dram_tensor("expert_rows", (NE, BLK, D), F32, kind="Internal").ap()
    y_more = nc.dram_tensor("expert_rows_more", (NE, MORE, D), F32, kind="Internal").ap()
    block_kernel(nc, args, out, h2_dram, y_dram, y_more)
    r = run_bass_kernel_spmd(nc, [arrays], core_ids=[0])
    return r.results[0]["out_0"]
```

```python
import math
from contextlib import ExitStack

import concourse.bass as bass
from concourse import mybir

F32 = mybir.dt.float32
F32R = mybir.dt.float32r
U32 = mybir.dt.uint32
I32 = mybir.dt.int32
ALU = mybir.AluOpType
ACT = mybir.ActivationFunctionType
X = mybir.AxisListType.X

P = 128
L = 512
TT = L // P
D = 1024
DC = D // P
HY = 512
HC = HY // P
NH, NOPE, ROPE, VH = 8, 64, 32, 64
QKD = NOPE + ROPE
QL, KVL = 384, 256
QC, KC = QL // P, KVL // P
OFF_Q = 3 * HY
OFF_KV = OFF_Q + QL
OFF_KR = OFF_KV + KVL
OFF_GATE = OFF_KR + ROPE
EPS = 1e-6
NG, EPG = 4, 8
NE = NG * EPG
DE = 256
BLK = 80
NBLK = -(-L // BLK)
MORE = BLK * (NBLK - 1)
EXPERT_SLOTS = 6
BIG = 3.0e38
SCORE_SCALE = float(QKD) ** -0.5
TWO_PI = 2.0 * math.pi
ROUND = 1.5 * 2.0 ** 23
PI2_HI = 6.28125
PI2_LO = TWO_PI - PI2_HI

C_ID, C_ONE, C_LT, C_I32, C_I32B, C_IB, C_TOK, C_I4, C_I4B = 0, 128, 256, 384, 416, 448, 448 + BLK, 452 + BLK, 456 + BLK
C_END = 460 + BLK

RING = 5
CHUNK = 4096


def block_kernel(nc, a, out, h2_dram, y_dram, y_more):
    ctx = ExitStack()
    with ctx:
        def sb(name, cols, dt=F32):
            return ctx.enter_context(nc.sbuf_tensor(name, [P, cols], dt))

        def sem(name):
            return ctx.enter_context(nc.semaphore(name))

        cst = sb("cst", C_END)
        K = 256
        with nc.sbuf_tensor("ring", [P, RING * CHUNK], F32) as ring, nc.sbuf_tensor("ht_mem", [P, DC * L], F32) as ht_mem, \
                nc.sbuf_tensor("arena", [P, 84 * K], F32) as arena:
            pass
        ring_r, ht_r = sb("ring_rounded", RING * CHUNK, F32R), sb("ht_rounded", DC * L, F32R)
        sb("arena_start", 36 * K)
        down_hi1, branch_hi, ymla_lo = sb("down_hi1", 4 * K, F32R), sb("branch_hi", 16 * K, F32R), sb("ymla_low", 8 * K, F32R)
        sb("arena_middle", 8 * K)
        yhy_lo = sb("yhy_low", 8 * K, F32R)
        sb("arena_end", 4 * K)
        bcast = sb("bcast", 4 * D)
        cols = sb("cols", 256)
        small = sb("small", 256)
        down_hi = [sb("down_hi0", D, F32R), down_hi1]
        a_hi, a_lo = sb("hidden_hi", 4 * BLK, F32R), sb("hidden_lo", 4 * BLK, F32R)
        smallu = sb("smallu", 256, U32)
        banks = [ctx.enter_context(nc.psum_tensor(f"bank{i}", [P, 512], F32)) for i in range(8)]

        ident, ones = cst[:, C_ID:C_ID + P], cst[:, C_ONE:C_ONE + P]
        lower = cst[:, C_LT:C_LT + P]

        def view(mem, at_, size_, **dims):
            v = mem[:, at_:at_ + size_]
            names = list(dims)
            return v.rearrange(f"p ({' '.join(names)}) -> p {' '.join(names)}", **{k: dims[k] for k in names[1:]})

        hT_hi, hT_lo = view(ht_r, 0, DC * L, c=DC, t=L), view(ring_r, 3 * CHUNK, DC * L, c=DC, t=L)
        WHI = 4 * CHUNK
        ccol, g1col = cols[:, 0:8], cols[:, 8:16]
        convw = view(cols, 16, 36, w=3, c=12)
        convb, hybias = cols[:, 52:64], cols[:, 64:68]
        gq, gkv = cols[:, 68:71], cols[:, 71:73]
        fb1, ff1, fb2, ff2 = (cols[0:64, 73 + i:74 + i] for i in range(4))
        VECS = 77
        cact, modcol, a1col = cols[:, 80:88], cols[:, 88:104], cols[:, 104:112]
        invl1 = cols[:, 112:116]
        ss, rstd, srt = cols[:, 116:120], cols[:, 120:124], cols[:, 124:128]
        ss2, rstd2, srt2 = cols[:, 128:132], cols[:, 132:136], cols[:, 136:140]
        ss3, rstd3, srt3 = cols[:, 140:144], cols[:, 144:148], cols[:, 148:152]
        rowmax, negmax, rowsum, rinv = (cols[:, 152 + 4 * i:156 + 4 * i] for i in range(4))

        filt = view(arena, 0, 16 * K, t=TT, d=2, c=HY)
        spec = view(arena, 0, 16 * K, f=4, r=2, c=HY)
        G = view(arena, 16 * K, 16 * K, f=4, r=2, c=HY)
        xin = view(arena, 32 * K, 16 * K, t=TT, d=D)
        x0T = view(arena, 32 * K, 8 * K, c=HC, t=L)
        uT = view(arena, 40 * K, 8 * K, c=HC, t=L)
        argT = arena[0:64, 48 * K:50 * K]
        rndT = arena[0:64, 50 * K:52 * K]
        fraw = view(arena, 16 * K, 16 * K, t=TT, d=2, c=HY)
        x1T = view(arena, 48 * K, 8 * K, c=HC, t=L)
        uTok = view(arena, 48 * K, 8 * K, t=TT, c=HY)
        window = view(arena, 56 * K, 8 * K, t=TT, c=HY)
        cm = view(arena, 56 * K, 8 * K, b=4, n=512)
        adasum = view(arena, 64 * K, 4 * K, b=2, n=512)
        adab = view(arena, 68 * K, 4 * K, b=2, n=512)
        zT = arena[0:33, 72 * K:74 * K]
        fw1 = arena[0:33, 74 * K:74 * K + 64]
        fw2 = arena[0:64, 74 * K + 64:74 * K + 128]
        fw3 = arena[0:64, 76 * K:80 * K]
        xsq = arena[:, 48 * K:52 * K]
        yhy = view(arena, 72 * K, 8 * K, c=HC, t=L)
        s1T = arena[0:64, 80 * K:82 * K]
        s2T = arena[0:64, 82 * K:84 * K]
        cvt = view(arena, 80 * K, 4 * K, b=2, t=512)
        dftf = view(bcast, 0, 16 * K, s=2, c=4, n=512)
        qh = view(arena, 0, 16 * K, h=NH, t=L)
        kh = view(arena, 16 * K, 16 * K, h=NH, t=L)
        cqT = view(arena, 32 * K, 6 * K, c=QC, t=L)
        ckvT = view(arena, 38 * K, 4 * K, c=KC, t=L)
        sqT = view(arena, 42 * K, 6 * K, b=3, t=L)
        rb = arena[:, 48 * K:50 * K]
        rope = view(arena, 50 * K, 4 * K, s=2, t=L)
        wrot = view(arena, 54 * K, 3 * K, c=QC, h=NH, n=ROPE)
        rt = view(arena, 58 * K, 4 * K, b=2, t=L)
        krope = arena[:, 62 * K:64 * K]
        ktmp = arena[:, 82 * K:84 * K]
        prob = view(arena, 32 * K, 8 * K, b=4, n=L)
        pT = view(arena, 42 * K, 4 * K, b=2, n=L)
        v_sb = view(arena, 48 * K, 8 * K, t=TT, n=NH * VH)
        ymla = view(arena, 56 * K, 8 * K, c=4, t=L)
        mixT = view(arena, 0, 16 * K, c=DC, t=L)
        x1 = view(arena, 16 * K, 16 * K, t=TT, d=D)
        sg = view(arena, 32 * K, 8 * K, b=4, n=512)
        x1sq = view(arena, 76 * K, 4 * K, b=2, n=512)
        gated = view(arena, 80 * K, 4 * K, b=2, n=512)
        h2T = view(arena, 0, 16 * K, c=DC, t=L)
        h2 = view(ht_mem, 0, 16 * K, t=TT, d=D)
        wr = view(arena, 32 * K, DC * (NG + NE), c=DC, n=NG + NE)
        brow = arena[0:1, 34 * K:34 * K + NG + NE]
        g2b = arena[:, 36 * K:40 * K]
        hg = view(arena, 0, 8 * K, b=2, d=D)
        hgT = view(arena, 8 * K, 2 * DC * BLK, b=2, c=DC, s=BLK)
        sgl = view(arena, 8 * K + 2 * DC * BLK, 4 * BLK, b=2, n=2 * BLK)
        aT = view(arena, 8 * K + 2 * DC * BLK + 4 * BLK, 4 * BLK, b=2, n=2 * BLK)
        assert 8 * K + 2 * DC * BLK + 8 * BLK <= 16 * K
        yb = arena[:, 32 * K:36 * K]
        def halves(m, m_r, at_):
            return [(m, m_r, at_), (m, m_r, at_ + 4 * K)]
        RG, HT, AA, BC = (ring, ring_r), (ht_mem, ht_r), (arena, None), (bcast, None)
        emem = [((ring, 32 * K), halves(*RG, 40 * K), halves(*RG, 48 * K)),
                ((arena, 48 * K), halves(*AA, 56 * K), halves(*RG, 56 * K)),
                ((arena, 64 * K), halves(*RG, 64 * K), halves(*RG, 72 * K)),
                ((ring, 0), halves(*RG, 8 * K), halves(*RG, 16 * K)),
                ((arena, 40 * K), halves(*BC, 0), halves(*RG, 24 * K)),
                ((ht_mem, 0), [(*BC, 8 * K), (*AA, 80 * K)], halves(*HT, 8 * K))]
        wg_s = [view(*m[0], 8 * K, c=DC, n=DE) for m in emem]
        wu_s = [[view(h[0], h[2], 4 * K, c=DC // 2, n=DE) for h in m[1]] for m in emem]
        wd_s = [[h[0][:, h[2]:h[2] + D] for h in m[2]] for m in emem]
        wd_lo = [[h[1][:, h[2]:h[2] + D] for h in m[2]] for m in emem]
        yg = view(ring, 24 * K, 32 * K, b=8, d=D)
        outb = view(ring, 0, 8 * K, b=2, d=D)
        osq = ring[:, 8 * K:12 * K]
        fgb = ring[:, 64 * K:68 * K]
        R0 = 72 * K
        lg = view(arena, R0, 144, t=TT, n=NG + NE)
        em = view(arena, R0 + 144, 128, t=TT, n=NE)
        eq = view(arena, R0 + 272, 128, t=TT, n=NE)
        oh1 = view(arena, R0 + 400, 128, t=TT, n=NE)
        oh2 = view(arena, R0 + 528, 128, t=TT, n=NE)
        ohs = view(arena, R0 + 656, 128, t=TT, n=NE)
        rk = view(arena, R0 + 784, 128, t=TT, n=NE)
        ohv = view(arena, R0 + 912, 256, k=2, t=TT, n=NE)
        Rm = view(arena, R0 + 1168, 8 * BLK, k=2, t=TT, s=BLK)
        (gmax, gsum, psel, i0, m1, m2, i1, i2, dv, ed, w1c, w2c, yc1, yc2, r1, r2) = (small[:, 4 * i:4 * i + 4] for i in range(16))
        r12 = view(small, 56, 8, k=2, t=TT)
        gs, gm, pen, geq = (view(small, 64 + 16 * i, 16, t=TT, n=NG) for i in range(4))
        cnt, over = small[:, 128:160], small[:, 160:161]
        idxu = smallu[0:BLK, 0:32]
        yrow = view(smallu, 32, 8, k=2, t=TT)
        morerow = view(smallu, 48, 8, k=2, t=TT)
        wfirst = view(small, 184, 8, k=2, t=TT)
        wmore = view(small, 192, 8, k=2, t=TT)
        rowf, rankf = small[:, 200:204], small[:, 204:208]
        idxc = smallu[0:BLK, 40:42]
        overu = smallu[:, 44:45]

        pe_done = sem("pe_unit_done")
        read_sem = {"act": sem("act_unit_read"), "dve": sem("dve_unit_read")}
        dve_step, act_step = sem("dve_step"), sem("act_step")
        ring_in = [sem(f"ring_in{i}") for i in range(RING)]
        bias_clear, bias_in, ada_done = sem("ada_bias_clear"), [sem(f"ada_bias_in{i}") for i in range(2)], sem("ada_sum_done")
        loaded = {n: sem("in_" + n) for n in
                  "cst vecs zT fw window dftf x rope ffng router x1 fing".split()}
        cact_done, sin_arg, sin_done, filt_ready, absum_ready = (sem(n) for n in (
            "c_act", "sin_arg", "sin_done", "filter_ready", "filter_abs_ready"))
        branch_rounded, branch_split = sem("branches_rounded"), sem("branches_split")
        ht_lo_ready, w_hi, w_lo = sem("hT_low_ready"), sem("w_high_ready"), sem("w_low_ready")
        ht_exact = view(arena, 56 * K, 8 * K, b=4, t=L)
        abs_summed = sem("filter_abs_summed")
        x_rms, zeros_ready = sem("x_rms"), sem("zeros_ready")
        x_sumsq, x_scaled, a1_ready, sqrt_arg, sqrt_done = (sem(n) for n in (
            "x_sumsq", "x_scaled", "a1_ready", "sqrt_arg", "sqrt_done"))
        conv_centre, u_ready, spec_ready, yhy_ready = (sem(n) for n in (
            "conv_centre", "u_ready", "spectrum_ready", "y_hyena"))
        sq_ready, latent_ready, rotw_ready, kr_done, kr_copied, q_rope = (sem(n) for n in (
            "latent_square", "latent_normed", "rotated_weights", "k_rope", "k_rope_copied", "q_rope"))
        max_done, prob_done = sem("row_max"), sem("probs_normed")
        mix_done, x1_done, x1_sumsq, h2_done, h2_out = (sem(n) for n in (
            "mix_done", "x1_done", "x1_sumsq", "h2_done", "h2_written"))
        onehots, gexp, gexp_done, wexp, wexp_done, slots_ready, idx_ready, over_ready = (sem(n) for n in (
            "onehots", "g_shifted", "g_exp", "w_shifted", "w_exp", "slot_onehots", "slot_tokens", "overflow_known"))
        gu_in = [sem(f"gate_up_in{i}") for i in range(EXPERT_SLOTS)]
        dn_in = [sem(f"down_in{i}") for i in range(EXPERT_SLOTS)]
        rows_in = [sem(f"rows_in{i}") for i in range(2)]
        y_out = sem("y_written")
        turned, turned_act, gu_done, silu_done, a_done, y_done, y_dve = (sem(n) for n in (
            "rows_turned", "turned_read", "gate_up_done", "silu_done", "hidden_done",
            "expert_y_done", "y_read"))
        down_rounded, down_split, a_exact, a_rounded = (sem(n) for n in (
            "down_rounded", "down_split", "hidden_exact", "hidden_rounded"))
        back_in = [sem(f"back_in{i}") for i in range(2 * TT)]
        x2_done, x2_sumsq, sqrt3_arg, sqrt3_done, out_ready = (sem(n) for n in (
            "x2_done", "x2_sumsq", "sqrt3_arg", "sqrt3_done", "out_ready"))
        out_done = [sem(f"out_written{i}") for i in range(2)]
        o_slots, o_tok, o_idx, o_rows, o_turned, o_read, o_gu, o_silu, o_hidden, o_y, o_yread, o_out, o_w = (
            sem("over_" + n) for n in ("slots", "tokens", "idx", "rows", "turned", "turned_read", "gate_up", "silu",
                                       "hidden", "y", "y_read", "y_out", "weights"))
        rows_known, o_back, o_added = sem("y_rows_known"), sem("over_back"), sem("over_added")
        o_carried = sem("over_carried")
        o_rank, o_idxu = sem("over_rank"), sem("over_slot_tokens")

        units = []

        def plan(reader, *keys):
            units.extend((k, reader) for k in keys)

        NA, LAG = NH * TT, 3
        plan("dve", ("F1",), ("F2",), *(("F3", t, d) for t in range(TT) for d in range(2)))
        SPECTRUM = [("G", 0, 0), ("G", 0, 1), ("G", 1, 0), ("AC", 0), ("G", 1, 1), ("L1",), ("G", 2, 0), ("AC", 1),
                    ("G", 2, 1), ("G", 3, 0), ("AC", 2), ("G", 3, 1), ("AC", 3)]
        for k in SPECTRUM:
            plan("dve" if k == ("L1",) else "act", k)
        plan("act", *(("XT", c) for c in range(DC)))
        H_ORDER = [*range(HC, 3 * HC), *range(HC)]
        plan("dve", *(("H", m) for m in H_ORDER))
        plan("act", *(("UT", t) for t in range(TT)))
        plan("dve", *(("UF", f, r) for f in range(4) for r in range(2)))
        plan("act", ("AB", 4), ("AB", 5))
        plan("dve", *(("YI", c) for c in range(HC)))
        plan("act", *(("CQ", m) for m in range(QC)), ("CK", 0))
        plan("dve", ("QS",))
        plan("act", ("CK", 1))
        plan("dve", ("KR",), ("KS",), ("KT",))
        plan("act", *(("QN", i) for i in range(4)))
        plan("dve", *((k, g) for g in range(2) for k in ("QR", "QT")))
        plan("act", *(("KN", i) for i in range(4)), *(("V", t) for t in range(TT)))
        AB_AT = {9: 6, 17: 7, 25: 8, 33: 9}
        AB_GATES = {3: 10, 6: 11}
        for n in range(NA + LAG + 1):
            if n < NA:
                plan("act", ("S", n))
            if n in AB_AT:
                plan("act", ("AB", AB_AT[n]))
            if n > LAG:
                plan("act", ("O", n - LAG - 1))
            if LAG <= n < NA + LAG:
                plan("act", ("T", n - LAG))
        for d in range(DC):
            plan("act", ("GA", d), ("GB", d))
            if d in AB_GATES:
                plan("act", ("AB", AB_GATES[d]))
            plan("dve", ("MA", d), ("MB", d))
        for t in range(TT):
            plan("dve", ("W", t, 0), ("W", t, 1))
            if t > 1:
                plan("dve", ("LG", t - 2))
            if t:
                plan("act", ("HT", t - 1, 0), ("HT", t - 1, 1))
        plan("dve", ("LG", TT - 2))
        plan("act", ("HT", TT - 1, 0), ("HT", TT - 1, 1))
        plan("dve", ("LG", TT - 1), ("RK",), ("IX",))
        number = {k: n for n, (k, _) in enumerate(units)}
        reader, nth, seen = dict(units), {}, {"act": 0, "dve": 0}
        for k, r in units:
            seen[r] += 1
            nth[k] = seen[r]

        def bank(*k):
            return banks[number[k] % 8]

        def claim(*k):
            n = number[k]
            if n >= 8:
                old = units[n - 8][0]
                nc.tensor.wait_ge(read_sem[reader[old]], nth[old])

        def ready(eng, *k):
            eng.wait_ge(pe_done, number[k] + 1)

        def taken(eng, *k):
            eng.wait_ge(read_sem[reader[k]], nth[k])

        w_in3 = a["w_in"][0].rearrange("(c p) n -> p c n", p=P)
        ada3 = a["ada_w"][0].rearrange("(c p) n -> p c n", p=P)
        mix3 = a["w_mix_out"][0].rearrange("(c p) n -> p c n", p=P)
        slot_of = {("ada", 0): 0, ("ada", 1): 1, ("ada", 2): 2, ("ada", 3): 3, ("hy", 1): 0, ("hy", 2): 1, ("hy", 0): 2,
                   ("ada", 4): 0, ("ada", 5): 1, ("dft",): 2, ("cq",): 0, ("ckv",): 1, ("uquk",): 2, ("uv",): 0,
                   ("ada", 6): 1, ("ada", 7): 2, ("ada", 8): 0, ("ada", 9): 1, ("m", 0): 2, ("ada", 10): 0, ("m", 1): 1,
                   ("m", 2): 2, ("ada", 11): 0, ("m", 3): 1, ("m", 4): 2, ("m", 5): 1, ("m", 6): 0, ("m", 7): 2,
                   ("mix", 0): 1, ("mix", 1): 0}
        chunks = list(slot_of)
        place = {k: n for n, k in enumerate(chunks)}
        last_use = {("hy", 0): ("H", 3), ("hy", 1): ("H", 7), ("hy", 2): ("H", 11), ("dft",): ("YI", 3),
                    ("cq",): ("CQ", QC - 1), ("ckv",): ("KT",), ("uquk",): ("KN", 3), ("uv",): ("V", 3),
                    **{("m", d): ("MB", d) for d in range(DC)}}

        def before(k):
            return [m for m in chunks[:place[k]] if slot_of[m] == slot_of[k]]

        def at(*k):
            return ring[:, slot_of[k] * CHUNK:(slot_of[k] + 1) * CHUNK]

        def arrived(eng, *k):
            loads = {"uquk": 7, "m": 4}
            eng.wait_ge(ring_in[slot_of[k]], 16 * sum(loads.get(m[0], 1) for m in before(k) + [k]))

        w8 = {k: at(*k).rearrange("p (c n) -> p c n", c=DC) for k in chunks if k[0] in ("ada", "hy", "mix")}
        wcq = at("cq")[:, 0:DC * QL].rearrange("p (c n) -> p c n", c=DC)
        wckv = at("ckv")[:, 0:DC * (KVL + ROPE)].rearrange("p (c n) -> p c n", c=DC)
        dfti = at("dft").rearrange("p (s c n) -> p s c n", s=2, c=4)
        QN_COLS = QC * NH * NOPE
        wuqn = at("uquk")[:, 0:QN_COLS].rearrange("p (c h n) -> p c h n", c=QC, h=NH)
        wuqr = at("uquk")[:, QN_COLS:QC * NH * QKD].rearrange("p (c h n) -> p c h n", c=QC, h=NH)
        wuk = at("uquk")[:, QC * NH * QKD:QC * NH * QKD + KC * NH * NOPE].rearrange("p (c n) -> p c n", c=KC)
        wuv = at("uv")[:, 0:KC * NH * VH].rearrange("p (c n) -> p c n", c=KC)
        m_gate = [[at("m", d)[:, g * D:(g + 1) * D].rearrange("p (c n) -> p c n", c=DC) for g in range(2)] for d in range(DC)]
        m_out = [[at("m", d)[:, 2 * D + g * HY:2 * D + (g + 1) * HY].rearrange("p (c n) -> p c n", c=HC) for g in range(2)]
                 for d in range(DC)]

        splits = [(("hy", m // 4), 0, 512, (m % 4) * P, P, ("H", m)) for m in H_ORDER]
        splits += [(("cq",), 0, QL, m * P, P, ("CQ", m)) for m in range(QC)]
        splits += [(("ckv",), 0, KVL + ROPE, m * P, P, ("CK", m)) for m in range(KC)]
        splits += [(("ckv",), 0, KVL + ROPE, KVL, ROPE, ("KT",))]
        splits += [(("m", d), g * D, P, 0, P, (("GA", "GB", "MB")[g], d)) for d in range(DC) for g in range(3)]
        split_of = {x[5]: u for u, x in enumerate(splits)}
        KR_SPLIT = split_of[("KT",)]

        def split_parts(u):
            chunk, start, row, col, n, _ = splits[u]
            lo_, hi_ = (slot_of[chunk] * CHUNK + start, WHI + (u % 4) * D)
            raw = ring[:, lo_:lo_ + DC * row].rearrange("p (c n) -> p c n", c=DC)[:, :, col:col + n]
            rest = ring_r[:, lo_:lo_ + DC * row].rearrange("p (c n) -> p c n", c=DC)[:, :, col:col + n]
            if u == KR_SPLIT:
                return raw, ring_r[:, hi_:hi_ + D].rearrange("p (c n) -> p c n", c=DC)[:, :, NOPE:QKD], rest
            return raw, ring_r[:, hi_:hi_ + DC * n].rearrange("p (c n) -> p c n", c=DC), rest

        kr_tile = ring_r[:, WHI + (KR_SPLIT % 4) * D:WHI + (KR_SPLIT % 4 + 1) * D].rearrange("p (c n) -> p c n", c=DC)
        kr_hi, kt_hi = kr_tile[:, :, 0:QKD], kr_tile[:, :, P - QKD:P]
        CKV_END = slot_of[("ckv",)] * CHUNK + DC * (KVL + ROPE)
        kr_lo = ring_r[:, CKV_END - DC * (KVL + ROPE):CKV_END].rearrange("p (c n) -> p c n", c=DC)[:, :, KVL - NOPE:]
        kt_lo = view(ring_r, CKV_END, DC * QKD, c=DC, n=QKD)
        assert D == DC * P and NOPE + 2 * ROPE == P

        def round_weights(eng, u):
            chunk, unit = splits[u][0], splits[u][5]
            arrived(eng, *chunk)
            if u >= 4:
                ready(eng, *splits[u - 4][5])
            raw, hi_, _ = split_parts(u)
            nc.scalar.activation(hi_, raw, ACT.Copy).then_inc(w_hi, 1)

        def rest_of_weights(eng, u):
            raw, hi_, rest = split_parts(u)
            eng.wait_ge(w_hi, u + 1)
            nc.vector.tensor_tensor(rest, raw, hi_.bitcast(F32), ALU.subtract).then_inc(w_lo, 1)

        wg_d = a["w_gate"][0].rearrange("e (p c) n -> e p (c n)", c=DC)
        wu_d = [a["w_up"][0].rearrange("e (p c) n -> e p (c n)", c=DC)[:, :, h * D:(h + 1) * D] for h in range(2)]
        wd_d = [a["w_down"][0][:, f * P:(f + 1) * P, :] for f in range(2)]
        y_flat = y_dram.rearrange("e s d -> (e s) d")
        more_flat = y_more.rearrange("e s d -> (e s) d")

        def entry(v, e):
            if isinstance(e, int):
                return v[e]
            return v[bass.ds(e, 1)].rearrange("o p n -> (o p) n")

        def over_flag(eng):
            eng.wait_ge(over_ready, 1)
            return eng.value_load(overu[0:1, 0:1], min_val=0, max_val=1)

        FULL_GROUPS = NE // EXPERT_SLOTS
        LEFT = NE % EXPERT_SLOTS
        PAIRS = 16 * EXPERT_SLOTS // 2
        assert LEFT and EXPERT_SLOTS % 2 == 0

        block = ctx.enter_context(nc.Block())

        @block.sync
        def _(sp):
            def load_expert(e, s):
                sp.dma_start(wg_s[s].rearrange("p c n -> p (c n)"), entry(wg_d, e)).then_inc(gu_in[s], 16)
                for h in range(2):
                    sp.dma_start(wu_s[s][h].rearrange("p c n -> p (c n)"), entry(wu_d[h], e)).then_inc(gu_in[s], 16)
                for f in range(2):
                    sp.dma_start(wd_s[s][f], entry(wd_d[f], e)).then_inc(dn_in[s], 16)

            source = {("dft",): (at("dft"), a["dfti"]), ("cq",): (wcq, w_in3[:, :, OFF_Q:OFF_KV]),
                      ("ckv",): (wckv, w_in3[:, :, OFF_KV:OFF_GATE]),
                      ("uv",): (wuv, a["w_uv"][0].rearrange("(c p) h n -> p c (h n)", p=P)),
                      ("uquk",): (wuk, a["w_uk"][0].rearrange("(c p) h n -> p c (h n)", p=P))}
            for k in chunks:
                if k[0] == "ada":
                    source[k] = (w8[k], ada3[:, :, k[1] * 512:(k[1] + 1) * 512])
                elif k[0] == "hy":
                    source[k] = (w8[k], w_in3[:, :, k[1] * 512:(k[1] + 1) * 512])
                elif k[0] == "m":
                    o = OFF_GATE + k[1] * P
                    source[k] = (m_gate[k[1]][0], w_in3[:, :, o:o + P])
                elif k[0] == "mix":
                    source[k] = (w8[k], mix3[:, :, k[1] * 512:(k[1] + 1) * 512])
            sp.dma_start(zT, a["zT"]).then_inc(loaded["zT"], 16)
            sp.dma_start(fw1, a["filt_w1"][0]).then_inc(loaded["zT"], 16)
            sp.dma_start(cols[:, 0:VECS], a["vecs"]).then_inc(loaded["vecs"], 16)
            sp.dma_start(fw2, a["filt_w2"][0]).then_inc(loaded["fw"], 16)
            sp.dma_start(fw3, a["filt_w3"][0]).then_inc(loaded["fw"], 16)
            sp.dma_start(window, a["window"].rearrange("(t p) c -> p t c", p=P)).then_inc(loaded["window"], 16)
            sp.dma_start(bcast[:, :], a["dftf"]).then_inc(loaded["dftf"], 16)
            for k in chunks:
                for old in before(k)[-1:]:
                    if old[0] == "ada":
                        sp.wait_ge(ada_done, old[1] + 1)
                    else:
                        ready(sp, *last_use[old])
                into = ring_in[slot_of[k]]
                sp.dma_start(*source[k]).then_inc(into, 16)
                if k[0] == "m":
                    d, o = k[1], OFF_GATE + D + k[1] * P
                    sp.dma_start(m_gate[d][1], w_in3[:, :, o:o + P]).then_inc(into, 16)
                    for g, w in enumerate(("w_hy_out", "w_mla_out")):
                        sp.dma_start(m_out[d][g], a[w][0].rearrange("(c p) n -> p c n", p=P)[:, :, d * P:(d + 1) * P]
                                     ).then_inc(into, 16)
                if k == ("uquk",):
                    wuq_d = a["w_uq"][0].rearrange("(c p) (h n) -> c p h n", p=P, h=NH)
                    for c in range(QC):
                        sp.dma_start(wuqn[:, c], wuq_d[c, :, :, 0:NOPE]).then_inc(into, 16)
                        sp.dma_start(wuqr[:, c], wuq_d[c, :, :, NOPE:QKD]).then_inc(into, 16)
                if k[0] == "ada":
                    j = k[1]
                    if j >= 2:
                        sp.wait_ge(ada_done, j - 1)
                    else:
                        sp.wait_ge(bias_clear, 1)
                    sp.dma_start(adab[0:1, j % 2, :], a["ada_b"][0:1, j * 512:(j + 1) * 512]).then_inc(bias_in[j % 2], 16)
                if k == ("ada", 0):
                    sp.dma_start(cst[:, :], a["cst"]).then_inc(loaded["cst"], 16)
                    sp.dma_start(xin, a["x"][0].rearrange("(t p) d -> p t d", p=P)).then_inc(loaded["x"], 16)
                if k == ("m", 4):
                    taken(sp, "O", NA - 1)
                    sp.dma_start(x1, a["x"][0].rearrange("(t p) d -> p t d", p=P)).then_inc(loaded["x1"], 16)
            ready(sp, "MB", DC - 1)
            for e in range(3):
                load_expert(e, e)
            ready(sp, "W", TT - 1, 1)
            load_expert(3, 3)
            sp.wait_ge(h2_done, TT)
            load_expert(4, 4)
            ready(sp, "HT", TT - 1, 1)
            sp.wait_ge(h2_out, 16 * TT)
            load_expert(5, 5)

            def write_rows(e, s):
                sp.wait_ge(y_dve, e + 1)
                sp.dma_start(entry(y_dram, e), yb[0:BLK, :]).then_inc(y_out, 16)

            with sp.Fori(0, FULL_GROUPS - 1) as i:
                for s in range(EXPERT_SLOTS):
                    e = i * EXPERT_SLOTS + s
                    write_rows(e, s)
                    load_expert(e + EXPERT_SLOTS, s)
            for e in range((FULL_GROUPS - 1) * EXPERT_SLOTS, NE):
                write_rows(e, e % EXPERT_SLOTS)
                if e + EXPERT_SLOTS < NE:
                    load_expert(e + EXPERT_SLOTS, e % EXPERT_SLOTS)
                elif e % EXPERT_SLOTS == 2:
                    sp.dma_start(fgb, a["final_norm_g"].rearrange("(o n) -> o n", o=1).broadcast_to([P, D])).then_inc(loaded["fing"], 16)

            with sp.If(over_flag(sp) > 0):
                with sp.Fori(0, NBLK - 1) as b:
                    with sp.Fori(0, NE) as e:
                        n = b * NE + e
                        sp.wait_ge(o_yread, n + 1)
                        sp.dma_start(wg_s[0].rearrange("p c n -> p (c n)"), entry(wg_d, e)).then_inc(o_w, 16)
                        for h in range(2):
                            sp.dma_start(wu_s[0][h].rearrange("p c n -> p (c n)"), entry(wu_d[h], e)).then_inc(o_w, 16)
                        for f in range(2):
                            sp.dma_start(wd_s[0][f], entry(wd_d[f], e)).then_inc(o_w, 16)
                        sp.wait_ge(o_yread, n + 2)
                        sp.dma_start(more_flat[bass.ds(e * MORE + b * BLK, BLK), :], yb[0:BLK, :]).then_inc(o_out, 16)
            for t in range(TT):
                sp.wait_ge(out_ready, t + 1)
                sp.dma_start(out[0, t * P:(t + 1) * P, :], outb[:, t % 2, :]).then_inc(out_done[t % 2], 16)
            for i in range(2):
                sp.wait_ge(out_done[i], 16 * (TT // 2))

        @block.gpsimd
        def _(pool):
            for n, (x_, y_) in enumerate(((0, 1), (2, 3), (0, 2), (0, 0))):
                pool.wait_ge(absum_ready, min(2 * n + 2, TT))
                if n:
                    pool.wait_ge(abs_summed, n)
                into, more = (fraw[:, x_, :, :], fraw[:, y_, :, :]) if n < 3 else (fraw[:, 0, 0, :], fraw[:, 0, 1, :])
                nc.gpsimd.tensor_tensor(into, into, more, ALU.add).then_inc(abs_summed, 1)
            taken(pool, "YI", 3)
            ready(pool, "YI", 3)
            pool.dma_start(rope, a["rope"]).then_inc(loaded["rope"], 16)
            pool.wait_ge(kr_done, 1)
            for h in range(NH):
                nc.gpsimd.tensor_copy(kh[NOPE:QKD, h, :], krope[NOPE:QKD, :]).then_inc(kr_copied, 1)
            pool.wait_ge(mix_done, DC)
            pool.dma_start(g2b, a["norm_ffn_g"].broadcast_to([P, D])).then_inc(loaded["ffng"], 16)
            pool.dma_start(wr[:, :, 0:NG], a["w_group"][0].rearrange("(c p) n -> p c n", p=P)).then_inc(loaded["router"], 16)
            pool.dma_start(wr[:, :, NG:NG + NE], a["w_router"][0].rearrange("(c p) n -> p c n", p=P)).then_inc(loaded["router"], 16)
            pool.dma_start(brow[:, 0:NG], a["b_group"][0:1, :]).then_inc(loaded["router"], 16)
            pool.dma_start(brow[:, NG:NG + NE], a["b_router"][0:1, :]).then_inc(loaded["router"], 16)
            pool.wait_ge(idx_ready, 1)
            pool.wait_ge(h2_out, 16 * TT)

            for e in range(NE):
                if e >= 2:
                    pool.wait_ge(turned, e - 1)
                pool.indirect_dma_start(out=hg[0:BLK, e % 2, :], out_offset=None, in_=h2_dram[:, :],
                                        in_offset=bass.IndirectOffsetOnAxis(ap=idxu[:, e:e + 1], axis=0)).then_inc(rows_in[e % 2], 16)
            with pool.If(over_flag(pool) > 0):
                with pool.Fori(0, NBLK - 1) as b:
                    with pool.Fori(0, NE) as e:
                        n = b * NE + e
                        pool.wait_ge(o_idx, n + 1)
                        nc.gpsimd.tensor_tensor(small[:, 176:177], ones[:, 0:1], ones[:, 0:1], ALU.mult).then_inc(o_carried, 1)
                        pool.indirect_dma_start(out=hg[0:BLK, 0, :], out_offset=None, in_=h2_dram[:, :],
                                                in_offset=bass.IndirectOffsetOnAxis(ap=idxc[:, 0:1], axis=0)).then_inc(o_rows, 16)
                        pool.wait_ge(o_carried, n + 1)
                pool.wait_ge(o_out, 16 * (NBLK - 1) * NE)
                for t in range(TT):
                    for k in range(2):
                        n = 2 * t + k
                        if n:
                            pool.wait_ge(o_added, n)
                        pool.indirect_dma_start(out=yg[:, 0, :], out_offset=None, in_=more_flat,
                                                in_offset=bass.IndirectOffsetOnAxis(ap=morerow[:, k, t:t + 1], axis=0)).then_inc(o_back, 16)
                pool.wait_ge(o_added, 2 * TT)
            pool.wait_ge(y_out, 16 * NE)
            pool.wait_ge(rows_known, 1)
            for t in range(TT):
                for k in range(2):
                    n = 2 * t + k
                    pool.indirect_dma_start(out=yg[:, n, :], out_offset=None, in_=y_flat,
                                            in_offset=bass.IndirectOffsetOnAxis(ap=yrow[:, k, t:t + 1], axis=0)).then_inc(back_in[n], 16)

        @block.scalar
        def _(act):
            A = nc.scalar.activation
            step = [0]

            def link(ins):
                step[0] += 1
                ins.then_inc(act_step, 1)
                act.wait_ge(act_step, step[0])

            act.wait_ge(loaded["vecs"], 16)
            A(cact, ccol, ACT.Silu).then_inc(cact_done, 1)
            for n, dst in enumerate((s1T, s2T)):
                act.wait_ge(sin_arg, n + 1)
                A(dst, argT, ACT.Sin).then_inc(sin_done, 1)
            for t in range(TT):
                act.wait_ge(filt_ready, t + 1)
                A(fraw[:, t, :, :], fraw[:, t, :, :], ACT.Abs).then_inc(absum_ready, 1)
            act.wait_ge(loaded["x"], 16)
            act.wait_ge(sin_done, 2)
            for t in range(TT):
                if t:
                    act.wait_ge(x_sumsq, t)
                A(xsq, xin[:, t, :], ACT.Square, accum_out=ss[:, t:t + 1]).then_inc(x_sumsq, 1)
            act.wait_ge(sqrt_arg, 1)
            A(srt, rstd, ACT.Sqrt).then_inc(sqrt_done, 1)
            act.wait_ge(x_rms, 1)
            for t in range(TT):
                A(xin[:, t, :], xin[:, t, :], ACT.Copy, scale=rstd[:, t:t + 1]).then_inc(x_scaled, 1)
            ready(act, "L1")
            for k in SPECTRUM:
                if k[0] == "G":
                    ready(act, *k)
                    A(G[:, k[1], k[2], :], bank(*k)[:, :], ACT.Copy).then_inc(read_sem["act"], 1)
                elif k[0] == "AC":
                    ready(act, *k)
                    A(modcol[:, 4 * k[1]:4 * k[1] + 4], bank(*k)[:, 0:4], ACT.Copy).then_inc(read_sem["act"], 1)
            act.wait_ge(a1_ready, 1)
            round_weights(act, 0), round_weights(act, 1)
            for c in range(DC):
                ready(act, "XT", c)
                if c >= 4:
                    act.wait_ge(ht_lo_ready, c - 3)
                A(ht_exact[:, c % 4, :], bank("XT", c)[:, :], ACT.Identity, bias=modcol[:, c:c + 1], scale=a1col[:, c:c + 1])
                A(hT_hi[:, c, :], bank("XT", c)[:, :], ACT.Identity, bias=modcol[:, c:c + 1],
                  scale=a1col[:, c:c + 1]).then_inc(read_sem["act"], 1)

            def ada_row(j):
                ready(act, "AB", j)
                A(bcast[:, (j - 4) * 512:(j - 3) * 512], bank("AB", j)[:, :], ACT.Copy).then_inc(read_sem["act"], 1)

            for n, m in enumerate(H_ORDER):
                if n + 2 < 3 * HC:
                    round_weights(act, n + 2)
                ready(act, "H", m)
                if m >= 10:
                    act.wait_ge(u_ready, m - 9)
                dst = x0T[:, m, :] if m < HC else x1T[:, m - HC, :] if m < 2 * HC else cvt[:, m % 2, :]
                A(dst, bank("H", m)[:, :], ACT.Identity, bias=convb[:, m:m + 1],
                  scale=convw[:, 1, m:m + 1]).then_inc(conv_centre, 1)
            for t in range(TT):
                ready(act, "UT", t)
                A(uTok[:, t, :], bank("UT", t)[:, :], ACT.Copy).then_inc(read_sem["act"], 1)
            ada_row(4), ada_row(5)
            CQ0 = split_of[("CQ", 0)]
            round_weights(act, CQ0), round_weights(act, CQ0 + 1)
            act.wait_ge(yhy_ready, HC)
            for m in range(QC + KC):
                k = ("CQ", m) if m < QC else ("CK", m - QC)
                raw = cqT[:, m, :] if m < QC else ckvT[:, m - QC, :]
                sq = sqT[:, m, :] if m < QC else rt[:, m - QC, :]
                if CQ0 + m + 2 <= KR_SPLIT:
                    round_weights(act, CQ0 + m + 2)
                ready(act, *k)
                A(sq, bank(*k)[:, :], ACT.Square).then_inc(sq_ready, 1)
                A(raw, bank(*k)[:, :], ACT.Copy).then_inc(read_sem["act"], 1)
                if k == ("CK", 0):
                    act.wait_ge(sqrt_arg, 2)
                    A(rb, rb, ACT.Sqrt).then_inc(sqrt_done, 1)
            act.wait_ge(sqrt_arg, 3)
            A(rb, rb, ACT.Sqrt).then_inc(sqrt_done, 1)

            def two_heads(k, i, dst):
                ready(act, k, i)
                link(A(dst[0:NOPE, 2 * i, :], bank(k, i)[0:64, :], ACT.Copy))
                A(dst[0:NOPE, 2 * i + 1, :], bank(k, i)[64:128, :], ACT.Copy).then_inc(read_sem["act"], 1)

            for i in range(4):
                two_heads("QN", i, qh)
            for i in range(4):
                two_heads("KN", i, kh)
            act.wait_ge(q_rope, NH)
            for t in range(TT):
                ready(act, "V", t)
                A(v_sb[:, t, :], bank("V", t)[:, :], ACT.Copy).then_inc(read_sem["act"], 1)
            act.wait_ge(kr_copied, NH)

            def exps(n):
                act.wait_ge(max_done, n + 1)
                if n >= 4:
                    ready(act, "T", n - 4)
                A(prob[:, n % 4, :], bank("S", n)[:, :], ACT.Exp, bias=negmax[:, n % 4:n % 4 + 1], scale=SCORE_SCALE,
                  accum_out=rowsum[:, n % 4:n % 4 + 1]).then_inc(read_sem["act"], 1)

            def head_rows(n):
                h, t = n // TT, n % TT
                o = VH * (h % 2)
                ready(act, "O", n)
                A(ymla[o:o + VH, h // 2, t * P:(t + 1) * P], bank("O", n)[o:o + VH, 0:P], ACT.Copy).then_inc(read_sem["act"], 1)

            def turned_probs(n):
                ready(act, "T", n)
                A(pT[:, n % 2, :], bank("T", n)[:, :], ACT.Copy).then_inc(read_sem["act"], 1)

            for n in range(NA + LAG + 1):
                if n < NA:
                    exps(n)
                if n in AB_AT:
                    ada_row(AB_AT[n])
                if n > LAG:
                    head_rows(n - LAG - 1)
                if LAG <= n < NA + LAG:
                    turned_probs(n - LAG)
                if NA - 4 <= n < NA - 2:
                    round_weights(act, KR_SPLIT + 1 + n - (NA - 4))
            ready(act, "O", NA - 1)
            taken(act, "O", NA - 1)
            A(branch_hi[:, 0:8 * K], yhy[:, :, :].rearrange("p c t -> p (c t)"), ACT.Copy).then_inc(branch_rounded, 1)
            A(branch_hi[:, 8 * K:16 * K], ymla[:, :, :].rearrange("p c t -> p (c t)"), ACT.Copy).then_inc(branch_rounded, 1)
            for d in range(DC):
                for g, k in enumerate(("GA", "GB")):
                    u = split_of[(k, d)] + 2
                    for v in range(u, min(u + 1 + g, len(splits))):
                        round_weights(act, v)
                    ready(act, k, d)
                    if d >= 2:
                        act.wait_ge(mix_done, d - 1)
                    A(sg[:, (2 * d + g) % 4, :], bank(k, d)[:, :], ACT.Sigmoid).then_inc(read_sem["act"], 1)
                if d in AB_GATES:
                    ada_row(AB_GATES[d])
            def turned_h2(t):
                for i in range(2):
                    ready(act, "HT", t, i)
                    A(h2T[:, 4 * i:4 * i + 4, t * P:(t + 1) * P], bank("HT", t, i)[:, :].rearrange("p (c s) -> p c s", c=4), ACT.Copy
                      ).then_inc(read_sem["act"], 1)

            for t in range(TT):
                act.wait_ge(x1_done, t + 1)
                if t:
                    act.wait_ge(x1_sumsq, t)
                A(x1sq[:, :, :], x1[:, t, :].rearrange("p (b n) -> p b n", b=2), ACT.Square, accum_out=ss2[:, t:t + 1]).then_inc(x1_sumsq, 1)
                act.wait_ge(sqrt_arg, 4 + t)
                A(srt2[:, t:t + 1], rstd2[:, t:t + 1], ACT.Sqrt).then_inc(sqrt_done, 1)
                if t:
                    turned_h2(t - 1)
                act.wait_ge(h2_done, t + 1)
                act.dma_start(h2_dram[t * P:(t + 1) * P, :], h2[:, t, :]).then_inc(h2_out, 16)
            turned_h2(TT - 1)
            act.wait_ge(gexp, 1)
            A(gs, gs, ACT.Exp).then_inc(gexp_done, 1)
            act.wait_ge(wexp, 1)
            A(ed, dv, ACT.Exp).then_inc(wexp_done, 1)

            def turned_rows(e, s):
                act.wait_ge(turned, e + 1)
                if not (isinstance(e, int) and e < 2):
                    act.wait_ge(gu_done, e - 1)
                for i in range(2):
                    ins = A(hgT[:, s % 2, 4 * i:4 * i + 4, :], banks[i][:, 0:4 * BLK].rearrange("p (c s) -> p c s", c=4), ACT.Copy)
                ins.then_inc(turned_act, 1)

            def silu(e, s):
                act.wait_ge(gu_done, e + 1)
                if not (isinstance(e, int) and e < 2):
                    act.wait_ge(a_done, e - 1)
                A(sgl[:, s % 2, :], banks[2 + s % 2][:, 0:2 * BLK], ACT.Silu).then_inc(silu_done, 1)

            def round_down(e, s, i):
                act.wait_ge(dn_in[s], i * 32 + 32)
                if not (isinstance(e, int) and e == 0):
                    act.wait_ge(y_done, e)
                for f in range(2):
                    ins = A(down_hi[f][:, :], wd_s[s][f], ACT.Copy)
                ins.then_inc(down_rounded, 1)

            def group(i, slots=EXPERT_SLOTS, last=False):
                for s in range(slots):
                    e = i * EXPERT_SLOTS + s
                    silu(e, s)
                    if not (last and s == slots - 1):
                        turned_rows(e + 1, s + 1)
                    if not (last and s == slots - 1):
                        round_down(e, s, i)
            turned_rows(0, 0)
            group(0)
            with act.Fori(1, FULL_GROUPS) as i:
                group(i)
            group(FULL_GROUPS, slots=LEFT, last=True)
            with act.If(over_flag(act) > 0):
                with act.Fori(0, NBLK - 1) as b:
                    with act.Fori(0, NE) as e:
                        act.wait_ge(o_gu, b * NE + e + 1)
                        A(sgl[:, 0, :], banks[2][:, 0:2 * BLK], ACT.Silu).then_inc(o_silu, 1)
            for t in range(TT):
                act.wait_ge(x2_done, t + 1)
                if t:
                    act.wait_ge(x2_sumsq, t)
                A(osq, x1[:, t, :], ACT.Square, accum_out=ss3[:, t:t + 1]).then_inc(x2_sumsq, 1)
                act.wait_ge(sqrt3_arg, t + 1)
                A(srt3[:, t:t + 1], rstd3[:, t:t + 1], ACT.Sqrt).then_inc(sqrt3_done, 1)

        @block.tensor
        def _(pe):
            def product(o, pairs):
                for i, (l, r) in enumerate(pairs):
                    mm = nc.tensor.matmul(o, l, r, start=(i == 0), stop=(i == len(pairs) - 1))
                return mm

            def tile_product(k, rows, pairs):
                claim(*k)
                product(bank(*k)[rows, :], pairs).then_inc(pe_done, 1)

            def split_product(k, rows=slice(0, P), hi=None, lo=None, arriving=False):
                if hi is None:
                    u = split_of[k]
                    pe.wait_ge(w_lo, u + 1)
                    _, hi, lo = split_parts(u)
                claim(*k)
                for c in range(DC):
                    if arriving:
                        pe.wait_ge(ht_lo_ready, c + 1)
                    nc.tensor.matmul(bank(*k)[rows, :], lo[:, c, :], hT_hi[:, c, :], start=(c == 0), stop=False)
                    nc.tensor.matmul(bank(*k)[rows, :], hi[:, c, :], hT_lo[:, c, :], start=False, stop=False)
                    mm = nc.tensor.matmul(bank(*k)[rows, :], hi[:, c, :], hT_hi[:, c, :], start=False, stop=(c == DC - 1))
                mm.then_inc(pe_done, 1)

            def full(k, pairs, width=512):
                claim(*k)
                product(bank(*k)[:, 0:width], pairs).then_inc(pe_done, 1)

            def keep_warm(n, o, v):
                for _ in range(n):
                    nc.tensor.matmul(o[:, :], v[:, 0:P], v, start=True, stop=True)
            spare = banks[(number[("IX",)] + 1) % 8]

            def turn(k, parts):
                claim(*k)
                for i, p in enumerate(parts):
                    mm = nc.tensor.transpose(bank(*k)[:, i * P:(i + 1) * P], p, ident)
                mm.then_inc(pe_done, 1)

            pe.wait_ge(zeros_ready, 1)
            keep_warm(1, banks[7], filt[:, 0, 0, :])
            pe.wait_ge(loaded["zT"], 32)
            tile_product(("F1",), slice(0, 64), [(fw1, zT)])
            keep_warm(4, banks[7], filt[:, 0, 0, :])
            pe.wait_ge(loaded["fw"], 32)
            pe.wait_ge(sin_done, 1)
            tile_product(("F2",), slice(0, 64), [(fw2, s1T)])
            keep_warm(5, banks[7], filt[:, 0, 0, :])
            pe.wait_ge(sin_done, 2)
            for t in range(TT):
                for d in range(2):
                    full(("F3", t, d), [(s2T[:, t * P:(t + 1) * P], fw3[:, d * HY:(d + 1) * HY])])
            pe.wait_ge(loaded["dftf"], 16)
            claim("G", 0, 0)
            for t in range(TT):
                pe.wait_ge(filt_ready, t + 1)
                mm = nc.tensor.matmul(bank("G", 0, 0)[:, :], dftf[:, 0, t, 0:P], filt[:, t, 0, :], start=(t == 0), stop=(t == TT - 1))
            mm.then_inc(pe_done, 1)
            pe.wait_ge(loaded["cst"], 16)
            for k in SPECTRUM[1:]:
                if k[0] == "G":
                    _, f, r = k
                    full(k, [(dftf[:, r, t, f * P:(f + 1) * P], filt[:, t, r, :]) for t in range(TT)])
                elif k == ("L1",):
                    pe.wait_ge(abs_summed, TT)
                    claim("L1")
                    for c in range(HC):
                        mm = product(bank("L1")[:, c:c + 1], [(fraw[:, 0, 0, c * P:(c + 1) * P], ones[:, 0:1])])
                    mm.then_inc(pe_done, 1)
                else:
                    j = k[1]
                    pe.wait_ge(ada_done, j + 1)
                    claim(*k)
                    for c in range(4):
                        mm = product(bank(*k)[:, c:c + 1], [(adasum[:, j % 2, c * P:(c + 1) * P], ones[:, 0:1])])
                    mm.then_inc(pe_done, 1)
            pe.wait_ge(x_scaled, TT)
            for c in range(DC):
                turn(("XT", c), [xin[:, t, c * P:(c + 1) * P] for t in range(TT)])
            for m in H_ORDER:
                split_product(("H", m), arriving=m == H_ORDER[0])
            pe.wait_ge(u_ready, HC)
            for t in range(TT):
                turn(("UT", t), [uT[:, c, t * P:(t + 1) * P] for c in range(HC)])
            taken(pe, "UT", TT - 1)
            for f in range(4):
                for r in range(2):
                    full(("UF", f, r), [(dftf[:, r, t, f * P:(f + 1) * P], uTok[:, t, :]) for t in range(TT)])

            def ada_row(j):
                pe.wait_ge(ada_done, j + 1)
                full(("AB", j), [(ones, adasum[:, j % 2, :])])
            ada_row(4), ada_row(5)
            arrived(pe, "dft")
            pe.wait_ge(spec_ready, 4)
            for c in range(HC):
                full(("YI", c), [(spec[:, f, r, c * P:(c + 1) * P], dfti[:, r, f, :]) for f in range(4) for r in range(2)])
            for m in range(QC):
                split_product(("CQ", m))
            split_product(("CK", 0))
            pe.wait_ge(sq_ready, QC)
            full(("QS",), [(ones, sqT[:, m, :]) for m in range(QC)])
            split_product(("CK", 1))
            pe.wait_ge(w_lo, KR_SPLIT + 1)
            split_product(("KR",), rows=slice(0, QKD), hi=kr_hi, lo=kr_lo)
            pe.wait_ge(sq_ready, QC + KC)
            full(("KS",), [(ones, rt[:, m, :]) for m in range(KC)])
            pe.wait_ge(rotw_ready, 1)
            split_product(("KT",), rows=slice(0, QKD), hi=kt_hi, lo=kt_lo)
            arrived(pe, "uquk")
            pe.wait_ge(latent_ready, QC)
            for i in range(4):
                full(("QN", i), [(wuqn[:, c, 2 * i:2 * i + 2, :], cqT[:, c, :]) for c in range(QC)])
            pe.wait_ge(rotw_ready, 2)
            for g in range(2):
                full(("QR", g), [(wuqr[:, c, 4 * g:4 * g + 4, :], cqT[:, c, :]) for c in range(QC)])
                full(("QT", g), [(wrot[:, c, 4 * g:4 * g + 4, :], cqT[:, c, :]) for c in range(QC)])
            pe.wait_ge(latent_ready, QC + KC)
            for i in range(4):
                full(("KN", i), [(wuk[:, c, i * P:(i + 1) * P], ckvT[:, c, :]) for c in range(KC)])
            arrived(pe, "uv")
            for t in range(TT):
                full(("V", t), [(ckvT[:, c, t * P:(t + 1) * P], wuv[:, c, :]) for c in range(KC)])
            taken(pe, "KN", 3)
            pe.wait_ge(q_rope, NH)
            pe.wait_ge(kr_copied, NH)
            taken(pe, "V", TT - 1)
            for n in range(NA + LAG + 1):
                if n < NA:
                    h, t = n // TT, n % TT
                    full(("S", n), [(qh[0:QKD, h, t * P:(t + 1) * P], kh[0:QKD, h, :])])
                if n in AB_AT:
                    ada_row(AB_AT[n])
                if n > LAG:
                    m = n - LAG - 1
                    h, o = m // TT, VH * (m // TT % 2)
                    taken(pe, "T", m)
                    claim("O", m)
                    product(bank("O", m)[o:o + VH, 0:P], [(v_sb[:, k, h * VH:(h + 1) * VH], pT[:, m % 2, k * P:(k + 1) * P])
                                                          for k in range(TT)]).then_inc(pe_done, 1)
                if LAG <= n < NA + LAG:
                    m = n - LAG
                    pe.wait_ge(prob_done, m + 1)
                    turn(("T", m), [prob[:, m % 4, k * P:(k + 1) * P] for k in range(TT)])
            for d in range(DC):
                for k in ("GA", "GB"):
                    split_product((k, d))
                if d in AB_GATES:
                    ada_row(AB_GATES[d])
                if d == 0:
                    taken(pe, "O", NA - 1)
                pe.wait_ge(w_lo, split_of[("MB", d)] + 1)
                _, hi_, lo_ = split_parts(split_of[("MB", d)])
                for g, (k, y_lo) in enumerate((("MA", yhy_lo), ("MB", ymla_lo))):
                    if d == 0:
                        pe.wait_ge(branch_split, g + 1)
                    pairs = []
                    for c in range(HC):
                        yh, yl = branch_hi[:, g * 8 * K + c * L:g * 8 * K + (c + 1) * L], y_lo[:, c * L:(c + 1) * L]
                        wh, wl = hi_[:, g * HC + c, :], lo_[:, g * HC + c, :]
                        pairs += [(wl, yh), (wh, yl), (wh, yh)]
                    full((k, d), pairs)
            pe.wait_ge(mix_done, DC - 1)
            def turn_h2(t):
                pe.wait_ge(h2_done, t + 1)
                for i in range(2):
                    turn(("HT", t, i), [h2[:, t, c * P:(c + 1) * P] for c in range(4 * i, 4 * i + 4)])

            def router(t):
                taken(pe, "HT", t, 1)
                if t == 0:
                    pe.wait_ge(loaded["router"], 64)
                full(("LG", t), [(h2T[:, c, t * P:(t + 1) * P], wr[:, c, :]) for c in range(DC)] + [(ones[0:1, :], brow)],
                     NG + NE)

            for t in range(TT):
                for hf in range(2):
                    arrived(pe, "mix", hf)
                    claim("W", t, hf)
                    for c in range(DC):
                        if (t, hf, c) == (0, 0, DC - 1):
                            pe.wait_ge(mix_done, DC)
                        mm = nc.tensor.matmul(bank("W", t, hf)[:, :], mixT[:, c, t * P:(t + 1) * P], w8[("mix", hf)][:, c, :],
                                              start=(c == 0), stop=(c == DC - 1))
                    mm.then_inc(pe_done, 1)
                if t > 1:
                    router(t - 2)
                if t:
                    turn_h2(t - 1)
            router(TT - 2)
            keep_warm(4, spare, x1[:, 0, 0:512])
            turn_h2(TT - 1)
            keep_warm(1, spare, x1[:, 0, 0:512])
            router(TT - 1)
            keep_warm(9, spare, x1[:, 0, 0:512])
            pe.wait_ge(onehots, 1)
            claim("RK")
            for t in range(TT):
                product(bank("RK")[:, t * NE:(t + 1) * NE], [(lower, ohs[:, t, :])] + [(ones, ohs[:, j, :]) for j in range(t)])
            product(bank("RK")[:, TT * NE:(TT + 1) * NE], [(ones, ohs[:, j, :]) for j in range(TT)]).then_inc(pe_done, 1)
            keep_warm(3, spare, x1[:, 0, 0:512])
            pe.wait_ge(slots_ready, 1)
            claim("IX")
            product(bank("IX")[0:BLK, 0:NE], [(Rm[:, k, t, :], ohv[:, k, t, :]) for k in range(2) for t in range(TT)]
                    ).then_inc(pe_done, 1)

            def turn_rows(s, sem_):
                v = hg[0:BLK, s % 2, :].rearrange("s (p c) -> s c p", c=DC)
                for c in range(DC):
                    mm = nc.tensor.transpose(banks[c // 4][:, (c % 4) * BLK:(c % 4 + 1) * BLK], v[:, c, :], ident[0:BLK, 0:BLK])
                mm.then_inc(sem_, 1)

            def gate_up(w, s, b, sem_):
                for g in range(4):
                    rows = [wg_s[w][:, c] if g < 2 else wu_s[w][c // 4][:, c % 4] for c in range(DC)]
                    mm = product(banks[2 + b][:, g * BLK:(g + 1) * BLK],
                                 [(rows[c][:, (g % 2) * P:(g % 2 + 1) * P], hgT[:, s % 2, c, :]) for c in range(DC)])
                mm.then_inc(sem_, 1)

            def down(w, s, b, sem_):
                for hf in range(2):
                    mm = product(banks[4 + 2 * b + hf][0:BLK, :],
                                 [(aT[:, s % 2, f * BLK:(f + 1) * BLK], wd_s[w][f][:, hf * 512:(hf + 1) * 512]) for f in range(2)])
                mm.then_inc(sem_, 1)

            def turn_expert(e, s, i):
                pe.wait_ge(rows_in[s % 2], i * PAIRS + 16 * (s // 2) + 16)
                if not (isinstance(e, int) and e == 0):
                    pe.wait_ge(turned_act, e)
                turn_rows(s, turned)

            def gate_up_expert(e, s, i):
                pe.wait_ge(turned_act, e + 1)
                pe.wait_ge(gu_in[s], i * 48 + 48)
                if not (isinstance(e, int) and e < 2):
                    pe.wait_ge(a_done, e - 1)
                gate_up(s, s, s % 2, gu_done)

            def down_expert(e, s, i):
                pe.wait_ge(a_done, e + 1)
                pe.wait_ge(down_split, e + 1)
                if not (isinstance(e, int) and e < 2):
                    pe.wait_ge(y_dve, e - 1)
                for hf in range(2):
                    h = slice(hf * 512, (hf + 1) * 512)
                    pairs = []
                    for f in range(2):
                        r = slice((s % 2) * 2 * BLK + f * BLK, (s % 2) * 2 * BLK + (f + 1) * BLK)
                        w_hi_, w_lo_ = down_hi[f][:, h], wd_lo[s][f][:, h]
                        pairs += [(a_lo[:, r], w_hi_), (a_hi[:, r], w_lo_), (a_hi[:, r], w_hi_)]
                    mm = product(banks[4 + 2 * (s % 2) + hf][0:BLK, :], pairs)
                mm.then_inc(y_done, 1)

            def group(i, first=False, slots=EXPERT_SLOTS, last=False):
                for s in range(slots):
                    e = i * EXPERT_SLOTS + s
                    gate_up_expert(e, s, i)
                    if not (last and s == slots - 1):
                        wrap = s == EXPERT_SLOTS - 1
                        turn_expert(e + 1, (s + 1) % EXPERT_SLOTS, i + 1 if wrap else i)
                    if not (first and s == 0):
                        down_expert(e - 1, (s - 1) % EXPERT_SLOTS, i - 1 if s == 0 else i)
                    else:
                        keep_warm(3, banks[7], x1[:, 0, 0:512])
            keep_warm(4, spare, x1[:, 0, 0:512])
            taken(pe, "IX")
            turn_expert(0, 0, 0)
            keep_warm(2, banks[7], x1[:, 0, 0:512])
            group(0, first=True)
            with pe.Fori(1, FULL_GROUPS) as i:
                group(i)
            group(FULL_GROUPS, slots=LEFT, last=True)
            pe.wait_ge(a_done, NE)
            pe.wait_ge(dn_in[LEFT - 1], FULL_GROUPS * 32 + 32)
            pe.wait_ge(y_dve, NE - 2)
            down(LEFT - 1, LEFT - 1, (LEFT - 1) % 2, y_done)
            with pe.If(over_flag(pe) > 0):
                with pe.Fori(0, NBLK - 1) as b:
                    pe.wait_ge(o_slots, b + 1)
                    product(banks[7][0:BLK, 0:NE], [(Rm[:, k, t, :], ohv[:, k, t, :]) for k in range(2) for t in range(TT)]
                            ).then_inc(o_tok, 1)
                    with pe.Fori(0, NE) as e:
                        n = b * NE + e
                        pe.wait_ge(o_rows, n * 16 + 16)
                        turn_rows(0, o_turned)
                        pe.wait_ge(o_read, n + 1)
                        pe.wait_ge(o_w, n * 80 + 80)
                        gate_up(0, 0, 0, o_gu)
                        pe.wait_ge(o_hidden, n + 1)
                        down(0, 0, 0, o_y)

        @block.vector
        def _(dve):
            V = nc.vector
            step = [0]

            def link(ins):
                step[0] += 1
                ins.then_inc(dve_step, 1)
                dve.wait_ge(dve_step, step[0])

            def read(ins):
                ins.then_inc(read_sem["dve"], 1)

            def ada(j, rows=range(DC)):
                if j == 0:
                    dve.wait_ge(cact_done, 1)
                if rows[0] == 0:
                    arrived(dve, "ada", j)
                    dve.wait_ge(bias_in[j % 2], 16 * (j // 2 + 1))
                    if j >= 2:
                        ready(dve, "AC" if j < 6 else "AB", j - 2)
                for c in rows:
                    ins = V.scalar_tensor_tensor(out=adasum[:, j % 2, :], in0=w8[("ada", j)][:, c, :], scalar=cact[:, c:c + 1],
                                                 in1=adab[:, j % 2, :] if c == 0 else adasum[:, j % 2, :], op0=ALU.mult, op1=ALU.add)
                    if c < DC - 1:
                        link(ins)
                    else:
                        ins.then_inc(ada_done, 1)

            V.memset(filt[:, 0, 0, :], 0.0).then_inc(zeros_ready, 1)
            link(V.memset(adab[:, :, :], 0.0))
            V.memset(over, 0.0).then_inc(bias_clear, 1)
            dve.wait_ge(loaded["vecs"], 16)
            for n, (b, f) in enumerate(((fb1, ff1), (fb2, ff2))):
                k = (f"F{n + 1}",)
                ready(dve, *k)
                if n:
                    dve.wait_ge(sin_done, n)
                ins = V.tensor_scalar(argT, bank(*k)[0:64, :], b, f, ALU.add, ALU.mult)
                read(ins)
                taken(dve, *k)
                link(V.tensor_scalar(rndT, argT, 1.0 / TWO_PI, ROUND, ALU.mult, ALU.add))
                link(V.tensor_scalar(rndT, rndT, ROUND, None, ALU.subtract))
                link(V.scalar_tensor_tensor(out=argT, in0=rndT, scalar=-PI2_HI, in1=argT, op0=ALU.mult, op1=ALU.add))
                link(V.scalar_tensor_tensor(out=argT, in0=rndT, scalar=-PI2_LO, in1=argT, op0=ALU.mult, op1=ALU.add))
                V.tensor_scalar(argT, argT, -3.1415925, 3.1415925, ALU.max, ALU.min).then_inc(sin_arg, 1)

            dve.wait_ge(loaded["window"], 16)
            dve.wait_ge(sin_done, 2)
            for t in range(TT):
                for d in range(2):
                    ready(dve, "F3", t, d)
                    read(V.tensor_tensor(fraw[:, t, d, :], bank("F3", t, d)[:, :], window[:, t, :], ALU.mult))
                taken(dve, "F3", t, 1)
                if t == 0:
                    link(V.memset(fraw[0:1, 0, 1, :], 0.0))
                V.tensor_tensor(filt[:, t, 0, :], fraw[:, t, 0, :], fraw[:, t, 1, :], ALU.add)
                V.tensor_tensor(filt[:, t, 1, :], fraw[:, t, 0, :], fraw[:, t, 1, :], ALU.subtract).then_inc(filt_ready, 1)
            ada(0)
            dve.wait_ge(x_sumsq, TT)
            V.tensor_scalar(rstd, ss, 1.0 / D, EPS, ALU.mult, ALU.add).then_inc(sqrt_arg, 1)
            dve.wait_ge(sqrt_done, 1)
            V.reciprocal(rstd, srt).then_inc(x_rms, 1)
            ada(1)
            ready(dve, "L1")
            read(V.reciprocal(invl1, bank("L1")[:, 0:HC]))
            ada(2)
            ada(3)
            taken(dve, "AC", 3)
            V.scalar_tensor_tensor(out=a1col, in0=modcol[:, 8:16], scalar=1.0, in1=g1col, op0=ALU.add, op1=ALU.mult
                                   ).then_inc(a1_ready, 1)
            rest_of_weights(dve, 0), rest_of_weights(dve, 1)
            for c in range(DC):
                taken(dve, "XT", c)
                V.tensor_tensor(hT_lo[:, c, :], ht_exact[:, c % 4, :], hT_hi[:, c, :].bitcast(F32), ALU.subtract).then_inc(ht_lo_ready, 1)
            for n, m in enumerate(H_ORDER):
                if n + 2 < 3 * HC:
                    rest_of_weights(dve, n + 2)
                dve.wait_ge(conv_centre, n + 1)
                dst = x0T[:, m, :] if m < HC else x1T[:, m - HC, :] if m < 2 * HC else cvt[:, m % 2, :]
                b = bank("H", m)
                link(V.scalar_tensor_tensor(out=dst[:, 1:L], in0=b[:, 0:L - 1], scalar=convw[:, 0, m:m + 1],
                                            in1=dst[:, 1:L], op0=ALU.mult, op1=ALU.add))
                read(V.scalar_tensor_tensor(out=dst[:, 0:L - 1], in0=b[:, 1:L], scalar=convw[:, 2, m:m + 1],
                                            in1=dst[:, 0:L - 1], op0=ALU.mult, op1=ALU.add))
                if m >= 2 * HC:
                    taken(dve, "H", m)
                    V.tensor_tensor(uT[:, m - 2 * HC, :], dst, x1T[:, m - 2 * HC, :], ALU.mult).then_inc(u_ready, 1)
            ada(4)
            ada(5)
            taken(dve, "G", 3, 1)
            for f in range(4):
                ready(dve, "UF", f, 1)
                if f:
                    dve.wait_ge(spec_ready, f)
                ur, ui, gr, gi = bank("UF", f, 0)[:, :], bank("UF", f, 1)[:, :], G[:, f, 0, :], G[:, f, 1, :]
                V.tensor_tensor(cm[:, 0, :], ur, gr, ALU.mult)
                V.tensor_tensor(cm[:, 1, :], ui, gi, ALU.mult)
                read(V.tensor_tensor(cm[:, 2, :], ur, gi, ALU.mult))
                read(V.tensor_tensor(cm[:, 3, :], ui, gr, ALU.mult))
                taken(dve, "UF", f, 1)
                V.tensor_tensor(spec[:, f, 0, :], cm[:, 0, :], cm[:, 1, :], ALU.subtract)
                V.tensor_tensor(spec[:, f, 1, :], cm[:, 2, :], cm[:, 3, :], ALU.add).then_inc(spec_ready, 1)
            CQ0 = split_of[("CQ", 0)]
            rest_of_weights(dve, CQ0), rest_of_weights(dve, CQ0 + 1)
            for c in range(HC):
                ready(dve, "YI", c)
                read(V.tensor_scalar(cm[:, c, :], bank("YI", c)[:, :], invl1[:, c:c + 1], None, ALU.mult))
                taken(dve, "YI", c)
                link(V.scalar_tensor_tensor(out=cm[:, c, :], in0=uT[:, c, :], scalar=hybias[:, c:c + 1], in1=cm[:, c, :],
                                            op0=ALU.mult, op1=ALU.add))
                V.tensor_tensor(yhy[:, c, :], cm[:, c, :], x0T[:, c, :], ALU.mult).then_inc(yhy_ready, 1)
            H2 = ROPE // 2
            for u in range(CQ0 + 2, KR_SPLIT + 1):
                rest_of_weights(dve, u)
            _, hi_, lo_ = split_parts(KR_SPLIT)
            dve.wait_ge(w_lo, KR_SPLIT + 1)
            V.tensor_copy(kt_lo[:, :, 0:NOPE], kr_lo[:, :, 0:NOPE].bitcast(F32))
            for dst, src in ((kt_hi[:, :, NOPE:], hi_), (kt_lo[:, :, NOPE:], lo_)):
                src = src.bitcast(F32)
                V.tensor_scalar(dst[:, :, 0:H2], src[:, :, H2:ROPE], -1.0, None, ALU.mult)
                ins = V.tensor_copy(dst[:, :, H2:ROPE], src[:, :, 0:H2])
            ins.then_inc(rotw_ready, 1)

            def latent(n, k, width, tiles, lat, g):
                ready(dve, k)
                read(V.tensor_scalar(rb, bank(k)[:, :], 1.0 / width, EPS, ALU.mult, ALU.add))
                taken(dve, k)
                dve.engine_nop().then_inc(sqrt_arg, 1)
                dve.wait_ge(sqrt_done, 2 + n)
                link(V.reciprocal(rb, rb))
                taken(dve, "CQ" if n == 0 else "CK", tiles - 1)
                for m in range(tiles):
                    V.scalar_tensor_tensor(out=lat[:, m, :], in0=lat[:, m, :], scalar=g[:, m:m + 1], in1=rb,
                                           op0=ALU.mult, op1=ALU.mult).then_inc(latent_ready, 1)
            latent(0, "QS", QL, QC, cqT, gq)
            dve.wait_ge(loaded["rope"], 16)
            ready(dve, "KR")
            read(V.tensor_tensor(krope[NOPE:QKD, :], bank("KR")[NOPE:QKD, :], rope[NOPE:QKD, 0, :], ALU.mult))
            dve.wait_ge(latent_ready, QC)
            latent(1, "KS", KVL, KC, ckvT, gkv)
            ready(dve, "KT")
            read(V.tensor_tensor(ktmp[NOPE:QKD, :], bank("KT")[NOPE:QKD, :],
                                 rope[NOPE:QKD, 1, :], ALU.mult))
            taken(dve, "KT")
            V.tensor_tensor(krope[NOPE:QKD, :], krope[NOPE:QKD, :], ktmp[NOPE:QKD, :], ALU.add).then_inc(kr_done, 1)
            arrived(dve, "uquk")
            for c in range(QC):
                V.tensor_scalar(wrot[:, c, :, 0:H2], wuqr[:, c, :, H2:ROPE], -1.0, None, ALU.mult)
                ins = V.tensor_copy(wrot[:, c, :, H2:ROPE], wuqr[:, c, :, 0:H2])
            ins.then_inc(rotw_ready, 1)
            for g in range(2):
                ready(dve, "QR", g)
                if g:
                    dve.wait_ge(q_rope, 4)
                read(V.tensor_tensor(rt[:, 0, :], bank("QR", g)[:, :], rope[:, 0, :], ALU.mult))
                ready(dve, "QT", g)
                read(V.tensor_tensor(rt[:, 1, :], bank("QT", g)[:, :], rope[:, 1, :], ALU.mult))
                taken(dve, "QT", g)
                for j in range(4):
                    r = slice(ROPE * j, ROPE * (j + 1))
                    V.tensor_tensor(qh[NOPE:QKD, 4 * g + j, :], rt[r, 0, :], rt[r, 1, :], ALU.add).then_inc(q_rope, 1)

            def row_max(n):
                ready(dve, "S", n)
                if n >= 4:
                    taken(dve, "S", n - 4)
                link(V.reduce_max(rowmax[:, n % 4:n % 4 + 1], bank("S", n)[:, :], X))
                V.tensor_scalar(negmax[:, n % 4:n % 4 + 1], rowmax[:, n % 4:n % 4 + 1], -SCORE_SCALE, None, ALU.mult
                                ).then_inc(max_done, 1)

            def normalise(n):
                taken(dve, "S", n)
                link(V.reciprocal(rinv[:, n % 4:n % 4 + 1], rowsum[:, n % 4:n % 4 + 1]))
                V.tensor_scalar(prob[:, n % 4, :], prob[:, n % 4, :], rinv[:, n % 4:n % 4 + 1], None, ALU.mult
                                ).then_inc(prob_done, 1)

            for n in range(NA + 1):
                if n < NA:
                    row_max(n)
                if n:
                    normalise(n - 1)
                if n < NA:
                    ada(6 + n // DC, [n % DC])
                if NA - 3 <= n < NA - 1:
                    rest_of_weights(dve, KR_SPLIT + 1 + n - (NA - 3))
            for g, (y, lo_) in enumerate(((yhy, yhy_lo), (ymla, ymla_lo))):
                dve.wait_ge(branch_rounded, g + 1)
                V.tensor_tensor(lo_[:, :], y[:, :, :].rearrange("p c t -> p (c t)"), branch_hi[:, g * 8 * K:(g + 1) * 8 * K].bitcast(F32),
                                ALU.subtract).then_inc(branch_split, 1)
            for d in range(DC):
                for u in range(KR_SPLIT + 3 + 3 * d, min(KR_SPLIT + 6 + 3 * d, len(splits))):
                    rest_of_weights(dve, u)
                if d < 2:
                    ada(10, range(4 * d, 4 * d + 4))
                elif 3 <= d < 5:
                    ada(11, range(4 * d - 12, 4 * d - 8))
                ga, gb = sg[:, 2 * d % 4, :], sg[:, (2 * d + 1) % 4, :]
                taken(dve, "GB", d)
                ready(dve, "MA", d)
                read(V.tensor_tensor(ga, bank("MA", d)[:, :], ga, ALU.mult))
                ready(dve, "MB", d)
                read(V.tensor_tensor(gb, bank("MB", d)[:, :], gb, ALU.mult))
                taken(dve, "MB", d)
                V.tensor_tensor(mixT[:, d, :], ga, gb, ALU.add).then_inc(mix_done, 1)
            taken(dve, "AB", 11)
            dve.wait_ge(loaded["ffng"], 16)
            link(V.scalar_tensor_tensor(out=bcast[:, 2 * D:3 * D], in0=bcast[:, 2 * D:3 * D], scalar=1.0, in1=g2b,
                                        op0=ALU.add, op1=ALU.mult))
            dve.wait_ge(loaded["x1"], 16)

            def logits(t):
                ready(dve, "LG", t)
                read(V.tensor_copy(lg[:, t, :], bank("LG", t)[:, 0:NG + NE]))

            for t in range(TT):
                for hf in range(2):
                    ready(dve, "W", t, hf)
                    read(V.tensor_tensor(gated[:, hf, :], bank("W", t, hf)[:, :], bcast[:, hf * 512:(hf + 1) * 512], ALU.mult))
                taken(dve, "W", t, 1)
                V.tensor_tensor(x1[:, t, :], x1[:, t, :], gated[:, :, :].rearrange("p b n -> p (b n)"), ALU.add).then_inc(x1_done, 1)
                dve.wait_ge(x1_done, t + 1)
                V.tensor_tensor(h2[:, t, :], x1[:, t, :], bcast[:, 2 * D:3 * D], ALU.mult)
                dve.wait_ge(x1_sumsq, t + 1)
                V.tensor_scalar(rstd2[:, t:t + 1], ss2[:, t:t + 1], 1.0 / D, EPS, ALU.mult, ALU.add).then_inc(sqrt_arg, 1)
                dve.wait_ge(sqrt_done, 4 + t)
                link(V.reciprocal(rstd2[:, t:t + 1], srt2[:, t:t + 1]))
                V.scalar_tensor_tensor(out=h2[:, t, :], in0=h2[:, t, :], scalar=rstd2[:, t:t + 1], in1=bcast[:, D:2 * D],
                                       op0=ALU.mult, op1=ALU.add).then_inc(h2_done, 1)
                if t > 1:
                    logits(t - 2)
            logits(TT - 2)

            def wide(v, n):
                return v.unsqueeze(2).broadcast_to([P, TT, n])

            def const(at_, n):
                return cst[:, at_:at_ + n].unsqueeze(1).broadcast_to([P, TT, n])

            def first_max(vals, top, scratch, index, onehot, n, iota, iota_far):
                link(V.tensor_reduce(top, vals, X, ALU.max))
                link(V.tensor_tensor(scratch, vals, wide(top, n), ALU.is_ge))
                link(V.scalar_tensor_tensor(out=scratch, in0=scratch, scalar=-100.0, in1=const(iota_far, n),
                                            op0=ALU.mult, op1=ALU.add))
                link(V.tensor_reduce(index, scratch, X, ALU.min))
                link(V.tensor_tensor(onehot, const(iota, n), wide(index, n), ALU.is_equal))

            logits(TT - 1)
            taken(dve, "LG", TT - 1)
            first_max(lg[:, :, 0:NG], gmax, geq, i0, gm, NG, C_I4, C_I4B)
            V.tensor_tensor(gs, lg[:, :, 0:NG], wide(gmax, NG), ALU.subtract).then_inc(gexp, 1)
            link(V.tensor_scalar(pen, gm, BIG, -BIG, ALU.mult, ALU.add))
            e4 = em.rearrange("p t (g n) -> p t g n", g=NG)
            grouped = [P, TT, NG, EPG]
            link(V.tensor_tensor(e4, lg[:, :, NG:NG + NE].rearrange("p t (g n) -> p t g n", g=NG),
                                 gm.unsqueeze(3).broadcast_to(grouped), ALU.mult))
            link(V.tensor_tensor(e4, e4, pen.unsqueeze(3).broadcast_to(grouped), ALU.add))
            first_max(em, m1, eq, i1, oh1, NE, C_I32, C_I32B)
            link(V.scalar_tensor_tensor(out=em, in0=oh1, scalar=-BIG, in1=em, op0=ALU.mult, op1=ALU.add))
            first_max(em, m2, eq, i2, oh2, NE, C_I32, C_I32B)
            V.tensor_tensor(ohs, oh1, oh2, ALU.add).then_inc(onehots, 1)
            V.tensor_tensor(dv, m2, m1, ALU.subtract).then_inc(wexp, 1)
            dve.wait_ge(gexp_done, 1)
            link(V.tensor_reduce(gsum, gs, X, ALU.add))
            link(V.reciprocal(psel, gsum))
            dve.wait_ge(wexp_done, 1)
            link(V.tensor_scalar(w1c, ed, 1.0, None, ALU.add))
            link(V.reciprocal(w2c, w1c))
            link(V.tensor_tensor(w1c, w2c, psel, ALU.mult))
            link(V.tensor_tensor(w2c, w1c, ed, ALU.mult))
            link(V.tensor_tensor(ohv[:, 0], oh1, wide(cst[:, C_TOK:C_TOK + TT], NE), ALU.mult))
            link(V.tensor_tensor(ohv[:, 1], oh2, wide(cst[:, C_TOK:C_TOK + TT], NE), ALU.mult))
            ready(dve, "RK")
            link(V.tensor_copy(cnt, bank("RK")[:, TT * NE:(TT + 1) * NE]))
            read(V.tensor_copy(rk, bank("RK")[:, 0:TT * NE].rearrange("p (t n) -> p t n", t=TT)))
            taken(dve, "RK")
            for oh, r in ((oh1, r1), (oh2, r2)):
                link(V.tensor_tensor(eq, oh, rk, ALU.mult))
                link(V.tensor_reduce(r, eq, X, ALU.add))

            def slot_onehots(sem_):
                for k in range(2):
                    for t in range(TT):
                        ins = V.tensor_scalar(Rm[:, k, t, :], cst[:, C_IB:C_IB + BLK], r12[:, k, t:t + 1], None, ALU.is_equal)
                ins.then_inc(sem_, 1)
            slot_onehots(slots_ready)
            link(V.tensor_reduce(over, cnt, X, ALU.max))
            link(V.tensor_scalar(over, over, float(BLK), None, ALU.is_gt))
            V.tensor_copy(overu, over).then_inc(over_ready, 1)
            ready(dve, "IX")
            read(V.tensor_copy(idxu, bank("IX")[0:BLK, 0:NE]))
            taken(dve, "IX")
            dve.engine_nop().then_inc(idx_ready, 1)
            for k, (i_, r, w) in enumerate(((i1, r1, w1c), (i2, r2, w2c))):
                link(V.tensor_scalar(rankf, r, float(BLK), None, ALU.is_lt))
                link(V.tensor_tensor(wfirst[:, k, :], w, rankf, ALU.mult))
                link(V.tensor_tensor(wmore[:, k, :], w, wfirst[:, k, :], ALU.subtract))
                link(V.tensor_scalar(rankf, r, float(BLK - 1), None, ALU.min))
                link(V.scalar_tensor_tensor(out=rowf, in0=i_, scalar=float(BLK), in1=rankf, op0=ALU.mult, op1=ALU.add))
                link(V.tensor_copy(yrow[:, k, :], rowf))
                link(V.tensor_scalar(rankf, r, float(BLK), 0.0, ALU.subtract, ALU.max))
                link(V.scalar_tensor_tensor(out=rowf, in0=i_, scalar=float(MORE), in1=rankf, op0=ALU.mult, op1=ALU.add))
                link(V.tensor_copy(morerow[:, k, :], rowf))
            dve.engine_nop().then_inc(rows_known, 1)

            def hidden(e, s):
                dve.wait_ge(silu_done, e + 1)
                if not (isinstance(e, int) and e < 2):
                    dve.wait_ge(y_done, e - 1)
                V.tensor_tensor(aT[:, s % 2, :], banks[2 + s % 2][:, 2 * BLK:4 * BLK], sgl[:, s % 2, :], ALU.mult).then_inc(a_exact, 1)
                r = slice((s % 2) * 2 * BLK, (s % 2 + 1) * 2 * BLK)
                dve.wait_ge(a_exact, e + 1)
                V.tensor_copy(a_hi[:, r], aT[:, s % 2, :]).then_inc(a_rounded, 1)
                dve.wait_ge(a_rounded, e + 1)
                V.tensor_tensor(a_lo[:, r], aT[:, s % 2, :], a_hi[:, r].bitcast(F32), ALU.subtract).then_inc(a_done, 1)

            def rest_of_down(e, s):
                dve.wait_ge(down_rounded, e + 1)
                for f in range(2):
                    ins = V.tensor_tensor(wd_lo[s][f], wd_s[s][f], down_hi[f][:, :].bitcast(F32), ALU.subtract)
                ins.then_inc(down_split, 1)

            def gate_rows(b):
                for hf in range(2):
                    ins = V.tensor_tensor(yb[0:BLK, hf * 512:(hf + 1) * 512], banks[4 + 2 * b + hf][0:BLK, :],
                                          bcast[0:BLK, 3 * D + hf * 512:3 * D + (hf + 1) * 512], ALU.mult)
                return ins

            def y_rows(e, s, i):
                dve.wait_ge(y_done, e + 1)
                if not (isinstance(e, int) and e == 0):
                    dve.wait_ge(y_out, i * 16 * EXPERT_SLOTS + 16 * s)
                gate_rows(s % 2).then_inc(y_dve, 1)

            def group(i, first=False, slots=EXPERT_SLOTS, last=False):
                for s in range(slots):
                    e = i * EXPERT_SLOTS + s
                    hidden(e, s)
                    if not (last and s == slots - 1):
                        rest_of_down(e, s)
                    if not (first and s == 0):
                        y_rows(e - 1, (s - 1) % EXPERT_SLOTS, i - 1 if s == 0 else i)
            group(0, first=True)
            with dve.Fori(1, FULL_GROUPS) as i:
                group(i)
            group(FULL_GROUPS, slots=LEFT, last=True)
            y_rows(NE - 1, LEFT - 1, FULL_GROUPS)
            with dve.If(over_flag(dve) > 0):
                dve.wait_ge(y_out, 16 * NE)
                V.memset(rankf, 0.0).then_inc(o_yread, 1)
                with dve.Fori(0, NBLK - 1) as b:
                    V.tensor_scalar(r12, r12, float(BLK), None, ALU.subtract).then_inc(o_rank, 1)
                    dve.wait_ge(o_rank, b + 1)
                    slot_onehots(o_slots)
                    dve.wait_ge(o_tok, b + 1)
                    V.tensor_copy(idxu, banks[7][0:BLK, 0:NE]).then_inc(o_idxu, 1)
                    dve.wait_ge(y_out, 16 * NE)
                    dve.wait_ge(o_idxu, b + 1)
                    with dve.Fori(0, NE) as e:
                        n = b * NE + e
                        V.tensor_copy(idxc[:, 0:1], idxu[:, bass.ds(e, 1)]).then_inc(o_idx, 1)
                        dve.wait_ge(o_turned, n + 1)
                        V.tensor_copy(hgT[:, 0, 0:4, :], banks[0][:, 0:4 * BLK].rearrange("p (c s) -> p c s", c=4))
                        V.tensor_copy(hgT[:, 0, 4:8, :], banks[1][:, 0:4 * BLK].rearrange("p (c s) -> p c s", c=4)).then_inc(o_read, 1)
                        dve.wait_ge(o_silu, n + 1)
                        V.tensor_tensor(aT[:, 0, :], banks[2][:, 2 * BLK:4 * BLK], sgl[:, 0, :], ALU.mult).then_inc(o_hidden, 1)
                        dve.wait_ge(o_y, n + 1)
                        gate_rows(0).then_inc(o_yread, 1)
                        dve.wait_ge(o_out, n * 16 + 16)
                for t in range(TT):
                    for k in range(2):
                        n = 2 * t + k
                        dve.wait_ge(o_back, 16 * n + 16)
                        V.scalar_tensor_tensor(out=x1[:, t, :], in0=yg[:, 0, :], scalar=wmore[:, k, t:t + 1], in1=x1[:, t, :],
                                               op0=ALU.mult, op1=ALU.add).then_inc(o_added, 1)
                        dve.wait_ge(o_added, n + 1)
            dve.wait_ge(loaded["fing"], 16)
            def mean_square(t):
                dve.wait_ge(x2_sumsq, t + 1)
                V.tensor_scalar(rstd3[:, t:t + 1], ss3[:, t:t + 1], 1.0 / D, EPS, ALU.mult, ALU.add).then_inc(sqrt3_arg, 1)

            def final_norm(t):
                dve.wait_ge(sqrt3_done, t + 1)
                link(V.reciprocal(rstd3[:, t:t + 1], srt3[:, t:t + 1]))
                if t >= 2:
                    dve.wait_ge(out_done[t % 2], 16 * (t // 2))
                V.scalar_tensor_tensor(out=outb[:, t % 2, :], in0=x1[:, t, :], scalar=rstd3[:, t:t + 1], in1=fgb,
                                       op0=ALU.mult, op1=ALU.mult).then_inc(out_ready, 1)

            def add_rows(t, k):
                dve.wait_ge(back_in[2 * t + k], 16)
                return V.scalar_tensor_tensor(out=x1[:, t, :], in0=yg[:, 2 * t + k, :], scalar=wfirst[:, k, t:t + 1], in1=x1[:, t, :],
                                              op0=ALU.mult, op1=ALU.add)

            for t in range(TT):
                link(add_rows(t, 0))
                if t:
                    mean_square(t - 1)
                add_rows(t, 1).then_inc(x2_done, 1)
                if t:
                    final_norm(t - 1)
            mean_square(TT - 1)
            final_norm(TT - 1)


_INPUTS = ("x c ada_w ada_b norm_mix_g w_in hy_conv_w hy_conv_b filt_w1 filt_b1 filt_freq1 filt_w2 filt_b2 filt_freq2 "
           "filt_w3 hy_bias q_norm_g kv_norm_g w_uq w_uk w_uv w_hy_out w_mla_out w_mix_out norm_ffn_g w_group b_group "
           "w_router b_router w_gate w_up w_down final_norm_g").split()


def shape_constants():
    import numpy as np
    f32 = np.float32
    cst = np.zeros((P, C_END), f32)
    cst[:, C_ID:C_ID + P] = np.eye(P)
    cst[:, C_ONE:C_ONE + P] = 1.0
    cst[:, C_LT:C_LT + P] = np.arange(P)[:, None] < np.arange(P)[None, :]
    cst[:, C_I32:C_I32 + NE] = np.arange(NE)
    cst[:, C_I32B:C_I32B + NE] = np.arange(NE) + 100
    cst[:, C_IB:C_IB + BLK] = np.arange(BLK)
    cst[:, C_TOK:C_TOK + TT] = np.arange(P)[:, None] + P * np.arange(TT)[None, :]
    cst[:, C_I4:C_I4 + NG] = np.arange(NG)
    cst[:, C_I4B:C_I4B + NG] = np.arange(NG) + 100
    t = np.linspace(0.0, 1.0, L, dtype=f32)[:, None]
    pos = np.arange(L, dtype=f32)[:, None]
    bands = np.linspace(1e-4, 15, 16, dtype=f32)[None, :]
    ang = (f32(2.0 * math.pi) * bands * pos) / f32(L)
    z = np.concatenate([t, np.cos(ang), -np.sin(ang)], axis=1).astype(f32)
    lo, hi = math.log(1e-2) / 1.5, math.log(1e-2) / 0.3
    deltas = np.linspace(lo, hi, HY, dtype=f32)
    window = (np.exp(-t * np.abs(deltas)[None, :]) + f32(0.05)).astype(f32)
    theta = 2.0 * np.pi * (np.arange(L)[None, :] + 0.5) * np.arange(L)[:, None] / (2 * L)
    fwd = np.stack([np.cos(theta), -np.sin(theta)])
    inv = np.stack([np.cos(theta).T, -np.sin(theta).T]) / L

    def rows_to_partitions(m):
        return np.ascontiguousarray(m.reshape(2, 4, P, L).transpose(2, 0, 1, 3).reshape(P, 8 * L).astype(f32))
    rinv = f32(10000.0) ** (-np.arange(0, ROPE, 2, dtype=f32) / f32(ROPE))
    ra = np.arange(L, dtype=f32)[:, None] * rinv[None, :].astype(f32)
    rope = np.stack([np.tile(np.cos(ra).T, (8, 1)), np.tile(np.sin(ra).T, (8, 1))], axis=1).astype(f32)
    return {"cst": cst, "zT": np.ascontiguousarray(z.T), "window": window, "dftf": rows_to_partitions(fwd),
            "dfti": rows_to_partitions(inv), "rope": np.ascontiguousarray(rope)}


def packed_vectors(given):
    import numpy as np

    def columns(v):
        return v.reshape(-1, P).T
    small_ = np.zeros((P, 4), np.float32)
    for i, n in enumerate(("filt_b1", "filt_freq1", "filt_b2", "filt_freq2")):
        small_[0:64, i] = given[n][0]
    parts = [columns(given[n][0]) for n in ("c", "norm_mix_g", "hy_conv_w", "hy_conv_b", "hy_bias", "q_norm_g", "kv_norm_g")]
    return np.ascontiguousarray(np.concatenate(parts + [small_], axis=1))


def kernel(**inputs):
    import numpy as np
    import concourse.bacc as bacc
    from concourse.bass_utils import run_bass_kernel_spmd

    nc = bacc.Bacc("TRN2", target_bir_lowering=False, num_devices=1)
    arrays, args = {}, {}
    given = {n: np.ascontiguousarray(inputs[n]) for n in _INPUTS}
    given["vecs"] = packed_vectors(given)
    given.update(shape_constants())
    for n, v in given.items():
        arrays["in_" + n] = v
        args[n] = nc.dram_tensor("in_" + n, v.shape, mybir.dt.from_np(v.dtype), kind="ExternalInput").ap()
    out = nc.dram_tensor("out_0", (1, L, D), F32, kind="ExternalOutput").ap()
    h2_dram = nc.dram_tensor("h2_rows", (L, D), F32, kind="Internal").ap()
    y_dram = nc.dram_tensor("expert_rows", (NE, BLK, D), F32, kind="Internal").ap()
    y_more = nc.dram_tensor("expert_rows_more", (NE, MORE, D), F32, kind="Internal").ap()
    block_kernel(nc, args, out, h2_dram, y_dram, y_more)
    r = run_bass_kernel_spmd(nc, [arrays], core_ids=[0])
    return r.results[0]["out_0"]
```
